# Optimizing a Trainium2 kernel written in Bass

```python
import math
import jax, jax.numpy as jnp
from jax import lax
import numpy as np
import jax
import jax.numpy as jnp

D_MODEL = 1024
BATCH = 1
SEQ = 1024
DEPTH = 1

GRID_W = 64
D_MIX = D_MODEL
GDN_WIDTH = D_MIX // 2
NA_WIDTH = D_MIX - GDN_WIDTH
GDN_HEAD_DIM = 128
GDN_HEADS = GDN_WIDTH // GDN_HEAD_DIM
NA_HEAD_DIM = 64
NA_HEADS = NA_WIDTH // NA_HEAD_DIM
CONV_WIDTH = 5
GDN_CHUNK = 64
GDN_CONV_CH = 3 * GDN_WIDTH
NA_WIN_R = 8
NA_WIN_C = 16
NA_QBLK_C = 16
NA_KSPAN_C = NA_QBLK_C + NA_WIN_C
D_FF = 4 * D_MODEL
DEEPNORM_ALPHA = (2 * DEPTH) ** 0.25
DEEPNORM_BETA = (8 * DEPTH) ** -0.25
LN_EPS = 1e-5
RMS_EPS = 1e-6
SPLIT_POINTS = (3 * GDN_WIDTH, 4 * GDN_WIDTH, 4 * GDN_WIDTH + 2 * GDN_HEADS, 4 * GDN_WIDTH + 4 * GDN_HEADS)
D_IN = 4 * GDN_WIDTH + 4 * GDN_HEADS + 3 * NA_WIDTH


def layer_norm(x, g, b):
    xf = x.astype(jnp.float32)
    mu = jnp.mean(xf, axis=-1, keepdims=True)
    var = jnp.mean(jnp.square(xf - mu), axis=-1, keepdims=True)
    y = (xf - mu) * lax.rsqrt(var + LN_EPS)
    return (y * g + b).astype(x.dtype)

def rms_norm(x, g):
    xf = x.astype(jnp.float32)
    y = xf * lax.rsqrt(jnp.mean(jnp.square(xf), axis=-1, keepdims=True) + RMS_EPS)
    return y * g

def l2_normalize(x):
    xf = x.astype(jnp.float32)
    return xf * lax.rsqrt(jnp.sum(jnp.square(xf), axis=-1, keepdims=True) + RMS_EPS)

def short_conv(x, w):
    pad = CONV_WIDTH // 2
    T = x.shape[1]
    xp = jnp.pad(x, ((0, 0), (pad, pad), (0, 0)))
    return sum(xp[:, i:i + T] * w[i] for i in range(CONV_WIDTH))

def gated_delta_chunked(q, k, v, g, beta):
    out_dtype = v.dtype
    B, T, H, dk = q.shape
    dv = v.shape[-1]
    C = GDN_CHUNK
    N = T // C
    f32 = jnp.float32

    def chunk(t):
        t = t.astype(f32).reshape((B, N, C, H) + t.shape[3:])
        return jnp.moveaxis(t, 3, 1)

    q = chunk(q) * (dk ** -0.5)
    k = chunk(k)
    v = chunk(v)
    g = chunk(g)
    beta = chunk(beta)
    gc = jnp.cumsum(g, axis=-1)
    lower = jnp.tril(jnp.ones((C, C), dtype=bool))
    strict = jnp.tril(jnp.ones((C, C), dtype=bool), -1)
    gamma = jnp.exp(jnp.where(lower, gc[..., :, None] - gc[..., None, :], -jnp.inf))
    kb = k * beta[..., None]
    a_mat = jnp.where(strict, jnp.einsum('bhncd,bhnsd->bhncs', kb, k) * gamma, 0.0)
    t_mat = a_mat + jnp.eye(C, dtype=f32)
    u = lax.linalg.triangular_solve(t_mat, v * beta[..., None], left_side=True, lower=True, unit_diagonal=True)
    w = lax.linalg.triangular_solve(t_mat, kb * jnp.exp(gc)[..., None], left_side=True, lower=True, unit_diagonal=True)
    qk = jnp.einsum('bhncd,bhnsd->bhncs', q, k) * gamma
    q_dec = q * jnp.exp(gc)[..., None]
    k_dec = k * jnp.exp(gc[..., -1:] - gc)[..., None]
    g_last = jnp.exp(gc[..., -1])
    xs = tuple(jnp.moveaxis(t, 2, 0) for t in (q_dec, k_dec, u, w, qk, g_last))

    def step(S, inp):
        qd, kd, u_n, w_n, qk_n, gl = inp
        v_new = u_n - jnp.einsum('bhck,bhkv->bhcv', w_n, S)
        o = jnp.einsum('bhck,bhkv->bhcv', qd, S) + jnp.einsum('bhcs,bhsv->bhcv', qk_n, v_new)
        S = S * gl[..., None, None] + jnp.einsum('bhck,bhcv->bhkv', kd, v_new)
        return S, o

    S0 = jnp.zeros((B, H, dk, dv), f32)
    _, o = lax.scan(step, S0, xs)
    o = jnp.transpose(o, (1, 0, 3, 2, 4)).reshape(B, T, H, dv)
    return o.astype(out_dtype)

def gdn_mixer(h_qkv, h_z, h_a, h_b, conv_w, a_log, dt_bias, norm_g):
    B, T, _ = h_qkv.shape
    qkv = jax.nn.silu(short_conv(h_qkv, conv_w))
    q, k, v = jnp.split(qkv, 3, axis=-1)
    q = l2_normalize(q.reshape(B, T, GDN_HEADS, GDN_HEAD_DIM))
    k = l2_normalize(k.reshape(B, T, GDN_HEADS, GDN_HEAD_DIM))
    v = v.reshape(B, T, GDN_HEADS, GDN_HEAD_DIM)
    a = h_a.astype(jnp.float32).reshape(B, T, 2, GDN_HEADS)
    b = h_b.astype(jnp.float32).reshape(B, T, 2, GDN_HEADS)
    g = -jnp.exp(a_log.astype(jnp.float32)) * jax.nn.softplus(a + dt_bias.astype(jnp.float32))
    beta = jax.nn.sigmoid(b)
    q2 = jnp.concatenate([q, q[:, ::-1]], axis=0)
    k2 = jnp.concatenate([k, k[:, ::-1]], axis=0)
    v2 = jnp.concatenate([v, v[:, ::-1]], axis=0)
    g2 = jnp.concatenate([g[:, :, 0], g[:, ::-1, 1]], axis=0)
    beta2 = jnp.concatenate([beta[:, :, 0], beta[:, ::-1, 1]], axis=0)
    o2 = gated_delta_chunked(q2, k2, v2, g2, beta2)
    o = o2[:B].astype(jnp.float32) + o2[B:, ::-1].astype(jnp.float32)
    z = h_z.reshape(B, T, GDN_HEADS, GDN_HEAD_DIM).astype(jnp.float32)
    o = rms_norm(o, norm_g) * jax.nn.silu(z)
    return o.reshape(B, T, GDN_WIDTH).astype(h_qkv.dtype)

def _na_column_tables():
    n_blk = GRID_W // NA_QBLK_C
    j = np.arange(n_blk)
    span_start = np.clip(j * NA_QBLK_C - NA_WIN_C // 2, 0, GRID_W - NA_KSPAN_C)
    key_cols = span_start[:, None] + np.arange(NA_KSPAN_C)[None, :]
    q_cols = j[:, None] * NA_QBLK_C + np.arange(NA_QBLK_C)[None, :]
    win_start = np.clip(q_cols - NA_WIN_C // 2, 0, GRID_W - NA_WIN_C)
    kc = key_cols[:, None, :]
    in_win = (kc >= win_start[:, :, None]) & (kc < win_start[:, :, None] + NA_WIN_C)
    rel_idx = np.clip(kc - q_cols[:, :, None] + NA_WIN_C - 1, 0, 2 * NA_WIN_C - 2)
    return key_cols, in_win, rel_idx

def neighborhood_attention(q, k, v, rpb):
    B, T, H, d = q.shape
    rows = T // GRID_W
    kr = min(NA_WIN_R, rows)
    n_blk = GRID_W // NA_QBLK_C
    key_cols, in_win, rel_idx = _na_column_tables()
    qg = q.reshape(B, rows, n_blk, NA_QBLK_C, H, d)
    kg = k.reshape(B, rows, GRID_W, H, d)
    vg = v.reshape(B, rows, GRID_W, H, d)
    scale = d ** -0.5
    mask = jnp.asarray(in_win)[None, None, :, :, None, :]
    rpb_cols = rpb.astype(jnp.float32)[:, :, rel_idx]

    def one_row(r):
        r0 = jnp.clip(r - kr // 2, 0, rows - kr)
        k_band = lax.dynamic_slice_in_dim(kg, r0, kr, axis=1)[:, :, key_cols]
        v_band = lax.dynamic_slice_in_dim(vg, r0, kr, axis=1)[:, :, key_cols]
        q_row = lax.dynamic_index_in_dim(qg, r, axis=1, keepdims=False)
        s = jnp.einsum('bjqhd,brjkhd->bhjqrk', q_row, k_band).astype(jnp.float32) * scale
        dr = r0 + jnp.arange(kr) - r + NA_WIN_R - 1
        bias = jnp.take(rpb_cols, dr, axis=1)
        s = s + jnp.transpose(bias, (0, 2, 3, 1, 4))[None]
        s = jnp.where(mask, s, -jnp.inf)
        p = jax.nn.softmax(s.reshape(s.shape[:4] + (kr * NA_KSPAN_C,)), axis=-1).reshape(s.shape)
        o = jnp.einsum('bhjqrk,brjkhd->bjqhd', p.astype(v.dtype), v_band)
        return o.reshape(B, GRID_W, H, d)

    out = lax.map(one_row, jnp.arange(rows))
    return jnp.transpose(out, (1, 0, 2, 3, 4)).reshape(B, T, H, d)

def first_inputs(seed: int = 0) -> dict:
    key = jax.random.key(seed)
    ks = jax.random.split(key, 20)
    f32 = jnp.float32

    def nrm(k, shape, scale):
        return jax.random.normal(k, shape, f32) * scale

    x = nrm(ks[0], (BATCH, SEQ, D_MODEL), 1.0)
    ln_in_g = 1.0 + nrm(ks[1], (D_MODEL,), 0.02)
    ln_in_b = nrm(ks[2], (D_MODEL,), 0.02)
    w_in = nrm(ks[3], (DEPTH, D_MODEL, D_IN), D_MODEL ** -0.5)
    conv_w = nrm(ks[4], (DEPTH, CONV_WIDTH, GDN_CONV_CH), CONV_WIDTH ** -0.5)
    a_log = jnp.log(jax.random.uniform(ks[5], (DEPTH, 2, GDN_HEADS), f32, 1.0, 16.0))
    dt = jnp.exp(jax.random.uniform(ks[6], (DEPTH, 2, GDN_HEADS), f32, math.log(1e-3), math.log(1e-1)))
    dt_bias = dt + jnp.log(-jnp.expm1(-dt))
    gdn_norm_g = 1.0 + nrm(ks[7], (DEPTH, GDN_HEAD_DIM), 0.02)
    rpb = nrm(ks[8], (DEPTH, NA_HEADS, 2 * NA_WIN_R - 1, 2 * NA_WIN_C - 1), 0.1)
    na_norm_g = 1.0 + nrm(ks[9], (DEPTH, NA_HEAD_DIM), 0.02)
    w_out = nrm(ks[10], (DEPTH, D_MIX, D_MODEL), D_MIX ** -0.5 * DEEPNORM_BETA)
    ln1_g = 1.0 + nrm(ks[11], (DEPTH, D_MODEL), 0.02)
    ln1_b = nrm(ks[12], (DEPTH, D_MODEL), 0.02)
    w1 = nrm(ks[13], (DEPTH, D_MODEL, D_FF), D_MODEL ** -0.5)
    b1 = nrm(ks[14], (DEPTH, D_FF), 0.01)
    w2 = nrm(ks[15], (DEPTH, D_FF, D_MODEL), D_FF ** -0.5 * DEEPNORM_BETA)
    b2 = nrm(ks[16], (DEPTH, D_MODEL), 0.01)
    ln2_g = 1.0 + nrm(ks[17], (DEPTH, D_MODEL), 0.02)
    ln2_b = nrm(ks[18], (DEPTH, D_MODEL), 0.02)
    return {"x": x, "ln_in_g": ln_in_g, "ln_in_b": ln_in_b, "w_in": w_in, "conv_w": conv_w,
            "a_log": a_log, "dt_bias": dt_bias, "gdn_norm_g": gdn_norm_g, "rpb": rpb,
            "na_norm_g": na_norm_g, "w_out": w_out, "ln1_g": ln1_g, "ln1_b": ln1_b,
            "w1": w1, "b1": b1, "w2": w2, "b2": b2, "ln2_g": ln2_g, "ln2_b": ln2_b}

def first_block(x, ln_in_g, ln_in_b, w_in, conv_w, a_log, dt_bias, gdn_norm_g, rpb,
              na_norm_g, w_out, ln1_g, ln1_b, w1, b1, w2, b2, ln2_g, ln2_b):
    B, T, _ = x.shape
    x = layer_norm(x, ln_in_g, ln_in_b)
    for l in range(DEPTH):
        h = jnp.einsum('btd,de->bte', x, w_in[l])
        h_qkv, h_z, h_a, h_b, h_na = jnp.split(h, SPLIT_POINTS, axis=-1)
        o_gdn = gdn_mixer(h_qkv, h_z, h_a, h_b, conv_w[l], a_log[l], dt_bias[l], gdn_norm_g[l])
        q_na, k_na, v_na = (t.reshape(B, T, NA_HEADS, NA_HEAD_DIM) for t in jnp.split(h_na, 3, axis=-1))
        o_na = neighborhood_attention(q_na, k_na, v_na, rpb[l])
        o_na = rms_norm(o_na, na_norm_g[l]).reshape(B, T, NA_WIDTH).astype(x.dtype)
        mix = jnp.einsum('bte,ed->btd', jnp.concatenate([o_gdn, o_na], axis=-1), w_out[l])
        x = layer_norm(DEEPNORM_ALPHA * x + mix, ln1_g[l], ln1_b[l])
        ff = jnp.square(jax.nn.relu(jnp.einsum('btd,df->btf', x, w1[l]) + b1[l]))
        ff = jnp.einsum('btf,fd->btd', ff, w2[l]) + b2[l]
        x = layer_norm(DEEPNORM_ALPHA * x + ff, ln2_g[l], ln2_b[l])
    return x


_first_inputs = first_inputs


def first_inputs(seed=0):
    import zlib

    import numpy as np

    out = dict(_first_inputs(seed))
    spreads = {}
    factors = {'gdn_norm_g': 38.333,
     'na_norm_g': 21.652,
     'ln1_g': 2.708,
     'ln1_b': 2.761,
     'b1': 8.0,
     'b2': 35.337,
     'ln2_g': 8.18,
     'ln2_b': 8.325}
    for name, (base, spread) in spreads.items():
        noise = np.random.default_rng([zlib.crc32(name.encode()), seed]).standard_normal(out[name].shape)
        drawn = base * np.exp(spread * noise) if base else spread * noise
        out[name] = __import__('jax').numpy.asarray(drawn.astype(out[name].dtype))
    for name, factor in factors.items():
        out[name] = (out[name] * factor).astype(out[name].dtype)
    return out


_narrow_inputs = first_inputs


def first_inputs(seed=0):

    out = dict(_narrow_inputs(seed))
    wider = {'gdn_norm_g': 3.81, 'na_norm_g': 3.75, 'ln2_g': 3.21, 'ln2_b': 3.21}
    for name, times in wider.items():
        mean = out[name].mean()
        out[name] = (mean + times * (out[name] - mean)).astype(out[name].dtype)
    return out


HEAD_DIM = 64
N_HEADS = 8
N_KV_HEADS = 2
GQA_GROUP = N_HEADS // N_KV_HEADS
ATTN_WIDTH = N_HEADS * HEAD_DIM
KV_WIDTH = N_KV_HEADS * HEAD_DIM
CONV_WIDTH_2 = D_MODEL - ATTN_WIDTH
MIX_WIDTH = ATTN_WIDTH + CONV_WIDTH_2
IN_WIDTH = ATTN_WIDTH + 2 * KV_WIDTH + 2 * CONV_WIDTH_2
WINDOW = 128
BLOCK = 128
CONV_KERNEL = 31
NUM_BUCKETS = 32
MAX_DISTANCE = 128
D_FF_2 = 4 * D_MODEL
EPS = 1e-6
NEG = -1e30


def rms_norm_2(x, g):
    xf = x.astype(jnp.float32)
    y = xf * lax.rsqrt(jnp.mean(xf * xf, axis=-1, keepdims=True) + EPS)
    return (y * g.astype(jnp.float32)).astype(x.dtype)

def layer_norm_2(x, g, b):
    xf = x.astype(jnp.float32)
    mu = jnp.mean(xf, axis=-1, keepdims=True)
    var = jnp.mean(jnp.square(xf - mu), axis=-1, keepdims=True)
    y = (xf - mu) * lax.rsqrt(var + EPS)
    return (y * g.astype(jnp.float32) + b.astype(jnp.float32)).astype(x.dtype)

def t5_causal_bucket(n):
    n = np.asarray(n)
    max_exact = NUM_BUCKETS // 2
    large = max_exact + (np.log(np.maximum(n, 1) / max_exact)
                         / np.log(MAX_DISTANCE / max_exact)
                         * (NUM_BUCKETS - max_exact)).astype(np.int32)
    large = np.minimum(large, NUM_BUCKETS - 1)
    return np.where(n < max_exact, n, large).astype(np.int32)

def band_structure(seq_len):
    n_blocks = seq_len // BLOCK
    qi = np.arange(BLOCK)[:, None]
    kj = np.arange(2 * BLOCK)[None, :]
    dist = qi + BLOCK - kj
    in_window = (dist >= 0) & (dist < WINDOW)
    bucket = t5_causal_bucket(np.clip(dist, 0, None))
    k_abs = (np.arange(n_blocks)[:, None] - 1) * BLOCK + np.arange(2 * BLOCK)[None, :]
    valid = in_window[None, :, :] & (k_abs >= 0)[:, None, :]
    return bucket, valid

def sliding_window_gqa(q, k, v, sinks, rel_bias):
    B, T = q.shape[0], q.shape[1]
    nb = T // BLOCK
    bucket, valid = band_structure(T)
    bias = jnp.transpose(rel_bias[bucket].astype(jnp.float32), (2, 0, 1))
    bias = bias.reshape(N_KV_HEADS, GQA_GROUP, BLOCK, 2 * BLOCK)

    qb = q.reshape(B, nb, BLOCK, N_KV_HEADS, GQA_GROUP, HEAD_DIM)

    def band(t):
        tp = jnp.pad(t, ((0, 0), (BLOCK, 0), (0, 0), (0, 0)))
        prev = tp[:, :T].reshape(B, nb, BLOCK, N_KV_HEADS, HEAD_DIM)
        cur = t.reshape(B, nb, BLOCK, N_KV_HEADS, HEAD_DIM)
        return jnp.concatenate([prev, cur], axis=2)

    kb, vb = band(k), band(v)
    scale = 1.0 / math.sqrt(HEAD_DIM)
    s = jnp.einsum('bnqkgd,bnskd->bnkgqs', qb, kb).astype(jnp.float32) * scale
    s = s + bias[None, None]
    s = jnp.where(jnp.asarray(valid)[None, :, None, None, :, :], s, NEG)
    sink = sinks.astype(jnp.float32).reshape(N_KV_HEADS, GQA_GROUP)[None, None, :, :, None, None]
    m = jnp.maximum(jnp.max(s, axis=-1, keepdims=True), sink)
    p = jnp.exp(s - m)
    p = p / (jnp.sum(p, axis=-1, keepdims=True) + jnp.exp(sink - m))
    o = jnp.einsum('bnkgqs,bnskd->bnqkgd', p.astype(v.dtype), vb)
    return o.reshape(B, T, ATTN_WIDTH)

def conformer_conv(u, gate, conv_w, conv_b, ln_g, ln_b):
    h = u * jax.nn.sigmoid(gate)
    hp = jnp.pad(h, ((0, 0), (CONV_KERNEL - 1, 0), (0, 0)))
    y = lax.conv_general_dilated(
        hp, conv_w[:, None, :].astype(h.dtype), window_strides=(1,), padding='VALID',
        dimension_numbers=('NWC', 'WIO', 'NWC'), feature_group_count=CONV_WIDTH_2)
    y = y + conv_b
    y = layer_norm_2(y, ln_g, ln_b)
    return jax.nn.silu(y)

def second_inputs(seed: int = 0) -> dict:
    key = jax.random.key(seed)
    ks = jax.random.split(key, 20)
    f32 = jnp.float32
    nrm = lambda k, shape, s: (jax.random.normal(k, shape, f32) * s).astype(f32)
    return {
        "x": nrm(ks[0], (BATCH, SEQ, D_MODEL), 1.0),
        "rel_bias": nrm(ks[1], (NUM_BUCKETS, N_HEADS), 0.5),
        "norm_mix_g": 1.0 + nrm(ks[2], (DEPTH, D_MODEL), 0.02),
        "w_in": nrm(ks[3], (DEPTH, D_MODEL, IN_WIDTH), D_MODEL ** -0.5),
        "q_norm_g": 1.0 + nrm(ks[4], (DEPTH, HEAD_DIM), 0.02),
        "k_norm_g": 1.0 + nrm(ks[5], (DEPTH, HEAD_DIM), 0.02),
        "sinks": nrm(ks[6], (DEPTH, N_HEADS), 0.5),
        "conv_w": nrm(ks[7], (DEPTH, CONV_KERNEL, CONV_WIDTH_2), CONV_KERNEL ** -0.5),
        "conv_b": nrm(ks[8], (DEPTH, CONV_WIDTH_2), 0.02),
        "conv_ln_g": 1.0 + nrm(ks[9], (DEPTH, CONV_WIDTH_2), 0.02),
        "conv_ln_b": nrm(ks[10], (DEPTH, CONV_WIDTH_2), 0.02),
        "attn_out_g": 1.0 + nrm(ks[11], (DEPTH, ATTN_WIDTH), 0.02),
        "conv_out_g": 1.0 + nrm(ks[12], (DEPTH, CONV_WIDTH_2), 0.02),
        "w_out": nrm(ks[13], (DEPTH, MIX_WIDTH, D_MODEL), (MIX_WIDTH * 2 * DEPTH) ** -0.5),
        "norm_mlp_g": 1.0 + nrm(ks[14], (DEPTH, D_MODEL), 0.02),
        "w_mlp_up": nrm(ks[15], (DEPTH, D_MODEL, D_FF_2), D_MODEL ** -0.5),
        "w_mlp_down": nrm(ks[16], (DEPTH, D_FF_2, D_MODEL), (D_FF_2 * 2 * DEPTH) ** -0.5),
    }

def second_block(x, rel_bias, norm_mix_g, w_in, q_norm_g, k_norm_g, sinks, conv_w, conv_b,
              conv_ln_g, conv_ln_b, attn_out_g, conv_out_g, w_out, norm_mlp_g,
              w_mlp_up, w_mlp_down):
    B, T, _ = x.shape
    splits = [ATTN_WIDTH, ATTN_WIDTH + KV_WIDTH, ATTN_WIDTH + 2 * KV_WIDTH,
              ATTN_WIDTH + 2 * KV_WIDTH + CONV_WIDTH_2]
    for l in range(DEPTH):
        h = rms_norm_2(x, norm_mix_g[l])
        z = h @ w_in[l]
        q, k, v, u, gate = jnp.split(z, splits, axis=-1)
        q = rms_norm_2(q.reshape(B, T, N_HEADS, HEAD_DIM), q_norm_g[l])
        k = rms_norm_2(k.reshape(B, T, N_KV_HEADS, HEAD_DIM), k_norm_g[l])
        v = v.reshape(B, T, N_KV_HEADS, HEAD_DIM)
        a = sliding_window_gqa(q, k, v, sinks[l], rel_bias)
        c = conformer_conv(u, gate, conv_w[l], conv_b[l], conv_ln_g[l], conv_ln_b[l])
        mix = jnp.concatenate([rms_norm_2(a, attn_out_g[l]), rms_norm_2(c, conv_out_g[l])], axis=-1)
        x = x + mix @ w_out[l]
        h = rms_norm_2(x, norm_mlp_g[l])
        x = x + jnp.square(jax.nn.relu(h @ w_mlp_up[l])) @ w_mlp_down[l]
    return x


_first_inputs_2 = second_inputs


def second_inputs(seed=0):
    import zlib

    import numpy as np

    out = dict(_first_inputs_2(seed))
    spreads = {}
    factors = {'norm_mix_g': 3.208,
     'q_norm_g': 7.287,
     'k_norm_g': 6.321,
     'sinks': 61.133,
     'conv_b': 3.516,
     'conv_ln_g': 73.411,
     'conv_ln_b': 69.044,
     'attn_out_g': 83.328,
     'conv_out_g': 85.668,
     'norm_mlp_g': 15.323}
    for name, (base, spread) in spreads.items():
        noise = np.random.default_rng([zlib.crc32(name.encode()), seed]).standard_normal(out[name].shape)
        drawn = base * np.exp(spread * noise) if base else spread * noise
        out[name] = __import__('jax').numpy.asarray(drawn.astype(out[name].dtype))
    for name, factor in factors.items():
        out[name] = (out[name] * factor).astype(out[name].dtype)
    return out


_narrow_inputs_2 = second_inputs


def second_inputs(seed=0):

    out = dict(_narrow_inputs_2(seed))
    wider = {'conv_ln_g': 3.96, 'conv_ln_b': 3.98, 'attn_out_g': 3.89, 'conv_out_g': 3.92}
    for name, times in wider.items():
        mean = out[name].mean()
        out[name] = (mean + times * (out[name] - mean)).astype(out[name].dtype)
    return out


N_META = 16
GLA_WIDTH = D_MODEL // 2
GLA_HEADS = 4
GLA_DV = GLA_WIDTH // GLA_HEADS
GLA_DK = GLA_DV // 2
GLA_QK = GLA_HEADS * GLA_DK
GATE_RANK = 16
GATE_NORM = 16.0
CHUNK = 64
SUB = 16
CONV_CH = D_MODEL - GLA_WIDTH
CONV_K = 3
D_FF_3 = 4 * D_MODEL
PROJ_SIZES = (GLA_QK, GLA_QK, GLA_WIDTH, GLA_WIDTH, GATE_RANK, CONV_CH, CONV_CH, CONV_CH)
PROJ_WIDTH = 2 * GLA_QK + 2 * GLA_WIDTH + GATE_RANK + 3 * CONV_CH


def rms_norm_3(x, w):
    xf = x.astype(jnp.float32)
    y = xf * lax.rsqrt(jnp.mean(xf * xf, axis=-1, keepdims=True) + EPS)
    return (y * w.astype(jnp.float32)).astype(x.dtype)

def split_cols(p):
    outs = []
    start = 0
    for s in PROJ_SIZES:
        outs.append(p[..., start:start + s])
        start += s
    return outs

def gla_chunked(q, k, v, gk):
    Bsz, Lp, H, dk = q.shape
    dv = v.shape[-1]
    N = Lp // CHUNK
    S = CHUNK // SUB

    def blk(t):
        return t.reshape(Bsz, N, S, SUB, H, t.shape[-1]).transpose(0, 4, 1, 2, 3, 5)

    q, k, v, gk = blk(q), blk(k), blk(v), blk(gk)
    b = jnp.cumsum(gk.reshape(Bsz, H, N, CHUNK, dk), axis=3).reshape(Bsz, H, N, S, SUB, dk)

    b_end = b[..., -1, :]
    r = jnp.concatenate([jnp.zeros_like(b_end[:, :, :, :1]), b_end[:, :, :, :-1]], axis=3)
    q_r = q * jnp.exp(b - r[..., None, :])
    lower = jnp.arange(S)[:, None] > jnp.arange(S)[None, :]
    expo = r[:, :, :, :, None, None, :] - b[:, :, :, None, :, :, :]
    expo = jnp.where(lower[:, :, None, None], expo, -jnp.inf)
    k_rel = k[:, :, :, None] * jnp.exp(expo)
    a_off = jnp.einsum('bhnsid,bhnstjd->bhnsitj', q_r, k_rel)

    causal = jnp.tril(jnp.ones((SUB, SUB), dtype=bool))
    pair = b[..., :, None, :] - b[..., None, :, :]
    pair = jnp.where(causal[:, :, None], pair, -jnp.inf)
    a_diag = jnp.einsum('bhnsid,bhnsjd,bhnsijd->bhnsij', q, k, jnp.exp(pair))
    eye = jnp.eye(S, dtype=a_off.dtype)
    a = a_off + a_diag[..., None, :] * eye[:, None, :, None]
    a = a.reshape(Bsz, H, N, CHUNK, CHUNK)

    qc = q.reshape(Bsz, H, N, CHUNK, dk)
    kc = k.reshape(Bsz, H, N, CHUNK, dk)
    vc = v.reshape(Bsz, H, N, CHUNK, dv)
    bc = b.reshape(Bsz, H, N, CHUNK, dk)
    o_intra = jnp.einsum('bhnij,bhnjv->bhniv', a, vc)

    b_last = bc[..., -1, :]
    kv = jnp.einsum('bhncd,bhncv->bhndv', kc * jnp.exp(b_last[..., None, :] - bc), vc)

    def step(h, inp):
        decay, kv_n = inp
        return h * decay[..., None] + kv_n, h

    h0 = jnp.zeros((Bsz, H, dk, dv), dtype=q.dtype)
    _, h_prev = lax.scan(step, h0, (jnp.moveaxis(jnp.exp(b_last), 2, 0), jnp.moveaxis(kv, 2, 0)))
    h_prev = jnp.moveaxis(h_prev, 0, 2)
    o_inter = jnp.einsum('bhncd,bhndv->bhncv', qc * jnp.exp(bc), h_prev)

    o = o_intra + o_inter
    return o.transpose(0, 2, 3, 1, 4).reshape(Bsz, Lp, H, dv)

def gla_branch(q, k, v, g, gr, w_gate_up, b_gate, norm_w):
    Bsz, L, _ = q.shape
    f32 = jnp.float32
    qh = q.astype(f32).reshape(Bsz, L, GLA_HEADS, GLA_DK) * (GLA_DK ** -0.5)
    kh = k.astype(f32).reshape(Bsz, L, GLA_HEADS, GLA_DK)
    vh = v.astype(f32).reshape(Bsz, L, GLA_HEADS, GLA_DV)
    gk = jax.nn.log_sigmoid(gr.astype(f32) @ w_gate_up.astype(f32) + b_gate.astype(f32)) / GATE_NORM
    gk = gk.reshape(Bsz, L, GLA_HEADS, GLA_DK)
    front = (-N_META) % CHUNK
    back = (-(front + L)) % CHUNK

    def padf(t):
        return jnp.pad(t, ((0, 0), (front, back), (0, 0), (0, 0)))

    o = gla_chunked(padf(qh), padf(kh), padf(vh), padf(gk))[:, front:front + L]
    o = rms_norm_3(o, norm_w)
    o = o.reshape(Bsz, L, GLA_WIDTH) * jax.nn.silu(g.astype(f32))
    return o.astype(q.dtype)

def short_conv_branch(cb, cc, cx, conv_w):
    u = cc * cx
    y = lax.conv_general_dilated(
        u, conv_w[:, None, :].astype(u.dtype), window_strides=(1,),
        padding=[(CONV_K - 1, 0)], dimension_numbers=('NWC', 'WIO', 'NWC'),
        feature_group_count=CONV_CH)
    return cb * y

def third_inputs(seed: int = 0) -> dict:
    key = jax.random.key(seed)
    ks = jax.random.split(key, 14)
    n = jax.random.normal
    return {
        'x': n(ks[0], (BATCH, SEQ, D_MODEL), jnp.float32),
        'meta_tokens': n(ks[1], (N_META, D_MODEL), jnp.float32),
        'norm_mix_w': 1.0 + 0.01 * n(ks[2], (DEPTH, D_MODEL), jnp.float32),
        'w_in': n(ks[3], (DEPTH, D_MODEL, PROJ_WIDTH), jnp.float32) * D_MODEL ** -0.5,
        'w_gate_up': n(ks[4], (DEPTH, GATE_RANK, GLA_QK), jnp.float32) * GATE_RANK ** -0.5,
        'b_gate': 0.1 * n(ks[5], (DEPTH, GLA_QK), jnp.float32),
        'gla_norm_w': 1.0 + 0.01 * n(ks[6], (DEPTH, GLA_DV), jnp.float32),
        'conv_w': n(ks[7], (DEPTH, CONV_K, CONV_CH), jnp.float32) * CONV_K ** -0.5,
        'w_out': n(ks[8], (DEPTH, D_MODEL, D_MODEL), jnp.float32) * D_MODEL ** -0.5,
        'norm_mlp_w': 1.0 + 0.01 * n(ks[9], (DEPTH, D_MODEL), jnp.float32),
        'w_up': n(ks[10], (DEPTH, D_MODEL, D_FF_3), jnp.float32) * D_MODEL ** -0.5,
        'w_down': n(ks[11], (DEPTH, D_FF_3, D_MODEL), jnp.float32) * D_FF_3 ** -0.5,
        'norm_final_w': 1.0 + 0.01 * n(ks[12], (D_MODEL,), jnp.float32),
    }

def third_block(x, meta_tokens, norm_mix_w, w_in, w_gate_up, b_gate, gla_norm_w, conv_w,
              w_out, norm_mlp_w, w_up, w_down, norm_final_w):
    Bsz = x.shape[0]
    meta = jnp.broadcast_to(meta_tokens.astype(x.dtype)[None], (Bsz, N_META, D_MODEL))
    h = jnp.concatenate([meta, x], axis=1)
    for layer in range(DEPTH):
        hn = rms_norm_3(h, norm_mix_w[layer])
        proj = hn @ w_in[layer]
        q, k, v, g, gr, cb, cc, cx = split_cols(proj)
        y_gla = gla_branch(q, k, v, g, gr, w_gate_up[layer], b_gate[layer], gla_norm_w[layer])
        y_conv = short_conv_branch(cb, cc, cx, conv_w[layer]).astype(h.dtype)
        mixed = jnp.concatenate([y_gla.astype(h.dtype), y_conv], axis=-1) @ w_out[layer]
        h = h + mixed
        hn = rms_norm_3(h, norm_mlp_w[layer])
        h = h + jnp.square(jax.nn.relu(hn @ w_up[layer])) @ w_down[layer]
    out = rms_norm_3(h, norm_final_w)
    return out[:, N_META:]


_first_inputs_3 = third_inputs


def third_inputs(seed=0):
    import zlib

    import numpy as np

    out = dict(_first_inputs_3(seed))
    spreads = {}
    factors = {'norm_mix_w': 4.48,
     'b_gate': 3.429,
     'gla_norm_w': 8.0,
     'norm_mlp_w': 7.164,
     'norm_final_w': 5.758}
    for name, (base, spread) in spreads.items():
        noise = np.random.default_rng([zlib.crc32(name.encode()), seed]).standard_normal(out[name].shape)
        drawn = base * np.exp(spread * noise) if base else spread * noise
        out[name] = jnp.asarray(drawn.astype(out[name].dtype))
    for name, factor in factors.items():
        out[name] = (out[name] * factor).astype(out[name].dtype)
    return out


_narrow_inputs_3 = third_inputs


def third_inputs(seed=0):

    out = dict(_narrow_inputs_3(seed))
    wider = {'norm_mix_w': 3.26, 'gla_norm_w': 12.0, 'norm_mlp_w': 7.97, 'norm_final_w': 6.48}
    for name, times in wider.items():
        mean = out[name].mean()
        out[name] = (mean + times * (out[name] - mean)).astype(out[name].dtype)
    return out


def setup_inputs(seed=0):
    out = dict(first_inputs(seed))
    for name, value in second_inputs(seed + 1).items():
        if name != "x":
            out[name + "_2"] = value
    for name, value in third_inputs(seed + 2).items():
        if name != "x":
            out[name + "_3"] = value
    return out


def reference(
    x, ln_in_g, ln_in_b, w_in, conv_w, a_log, dt_bias, gdn_norm_g, rpb, na_norm_g, w_out, ln1_g,
    ln1_b, w1, b1, w2, b2, ln2_g, ln2_b, rel_bias_2, norm_mix_g_2, w_in_2, q_norm_g_2,
    k_norm_g_2, sinks_2, conv_w_2, conv_b_2, conv_ln_g_2, conv_ln_b_2, attn_out_g_2,
    conv_out_g_2, w_out_2, norm_mlp_g_2, w_mlp_up_2, w_mlp_down_2, meta_tokens_3, norm_mix_w_3,
    w_in_3, w_gate_up_3, b_gate_3, gla_norm_w_3, conv_w_3, w_out_3, norm_mlp_w_3, w_up_3,
    w_down_3, norm_final_w_3,
):
    x = first_block(
        x, ln_in_g, ln_in_b, w_in, conv_w, a_log, dt_bias, gdn_norm_g, rpb, na_norm_g, w_out,
        ln1_g, ln1_b, w1, b1, w2, b2, ln2_g, ln2_b,
    )
    x = second_block(
        x, rel_bias_2, norm_mix_g_2, w_in_2, q_norm_g_2, k_norm_g_2, sinks_2, conv_w_2,
        conv_b_2, conv_ln_g_2, conv_ln_b_2, attn_out_g_2, conv_out_g_2, w_out_2, norm_mlp_g_2,
        w_mlp_up_2, w_mlp_down_2,
    )
    return third_block(
        x, meta_tokens_3, norm_mix_w_3, w_in_3, w_gate_up_3, b_gate_3, gla_norm_w_3, conv_w_3,
        w_out_3, norm_mlp_w_3, w_up_3, w_down_3, norm_final_w_3,
    )


_drawn_inputs = setup_inputs


def setup_inputs(seed=0):
    import zlib

    import numpy as np

    out = dict(_drawn_inputs(seed))
    spreads = {}
    factors = {'meta_tokens_3': 5.038,
     'norm_mix_w_3': 3.19,
     'b_gate_3': 5.749,
     'gla_norm_w_3': 17.429,
     'norm_mlp_w_3': 8.0}
    for name, (base, spread) in spreads.items():
        noise = np.random.default_rng([zlib.crc32(name.encode()), seed]).standard_normal(out[name].shape)
        drawn = base * np.exp(spread * noise) if base else spread * noise
        out[name] = jnp.asarray(drawn.astype(out[name].dtype))
    for name, factor in factors.items():
        out[name] = (out[name] * factor).astype(out[name].dtype)
    return out
```

```python
from contextlib import ExitStack

import numpy as np

import concourse.bass as bass
from concourse import mybir

F32 = mybir.dt.float32
F32R = mybir.dt.float32r
I32 = mybir.dt.int32
ALU = mybir.AluOpType
ACT = mybir.ActivationFunctionType
AX = mybir.AxisListType

P = 128
D = 1024
DC = D // P
T = 1024
HALF = 512
TC = T // P
FF = 4 * D
FG = 512
NG = FF // FG
META = 16
TM = META + T
ALPHA = 2.0 ** 0.25
UNIT = 1024

GH = 4
NH1 = 8
GRID = 64
ROWS = T // GRID
KR, KC = 8, 16
COLS1, COLS2, COLS3 = 3600, 1792, 3088


def padded(cols):
    return -(-cols // 256) * 256


PARAMS = {}
_n = 0
for _name, _w in [
    ("ln_in_g", 8), ("ln_in_b", 8), ("ln1_g", 8), ("ln1_b", 8), ("ln2_g", 8), ("ln2_b", 8), ("b1", 32), ("b2", 8),
    ("gdn_g", 1), ("na_g", 1), ("conv_w", 60), ("a_log", 8), ("dt_bias", 8),
    ("mix_g_2", 8), ("q_g", 1), ("k_g", 1), ("conv_w_2", 124), ("conv_b_2", 4), ("cln_g", 4), ("cln_b", 4),
    ("attn_g", 4), ("cout_g", 4), ("mlp_g_2", 8), ("sinks", 8),
    ("mix_g_3", 8), ("b_gate", 2), ("gla_g", 1), ("conv_w_3", 12), ("mlp_g_3", 8), ("final_g", 8),
    ("eps5", 1), ("eps6", 1), ("zero", 1), ("one", 1),
]:
    PARAMS[_name] = (_n, _w)
    _n += _w
NPARAM = _n

CONSTS = {}
_n = 0
for _name, _w in [("ident", 128), ("ones", 128), ("ones_half", 128), ("fold", 64)]:
    CONSTS[_name] = (_n, _w)
    _n += _w
NCONST = _n
GDN_LEVELS = 7


def lay_consts():
    i = np.arange(P)
    c = np.zeros((P, NCONST), np.float32)
    c[:, 0:128] = np.eye(P)
    c[:, 128:256] = 1.0
    c[:, 256:384] = (i[:, None] // 64) == (i[None, :] // 64)
    c[:, 384:448] = (i[:, None] % 64) == np.arange(64)[None, :]
    return c


def lay_gdn_consts():
    r, s = np.arange(P)[:, None], np.arange(P)[None, :]
    out = np.zeros((P, 20, P), np.float32)
    for d in range(2):
        below = (r > s) if d == 0 else (r < s)
        out[:, 10 * d] = (r <= s) if d == 0 else (r >= s)
        out[:, 10 * d + 1] = np.where((r <= s) if d == 0 else (r >= s), 0.0, -1e30)
        out[:, 10 * d + 2] = np.where(below, 0.0, -1e30)
        for l in range(GDN_LEVELS):
            b = 1 << l
            out[:, 10 * d + 3 + l] = below & (r // (2 * b) == s // (2 * b)) & (r // b != s // b)
    return out


def lay_na_mask():
    q, k = np.arange(GRID)[:, None], np.arange(GRID)[None, :]
    start = np.clip(q - KC // 2, 0, GRID - KC)
    m = np.where((k >= start) & (k < start + KC), 0.0, -1e30).astype(np.float32)
    return np.concatenate([m, m], 0)


def build_program(nc, g):
    ctx = ExitStack()
    with ctx:
        base = -(-nc.sbuf_base // 64) * 64
        end = nc.sbuf_usable_end // 64 * 64

        class Region:

            def __init__(self, start, stop):
                self.at, self.stop = start, stop

            def take(self, name, shape, dt=F32):
                size = -(-4 * int(np.prod(shape[1:])) // 32) * 32
                assert self.at + size <= self.stop, (name, self.at + size - self.stop)
                t = nc.alloc_sbuf_tensor_at(name, shape, dt, offset=self.at)
                self.at += size
                return t

        def sem(name):
            return ctx.enter_context(nc.semaphore(name))

        def param(name, j=0, n=1):
            return params[:, bass.ds(j + PARAMS[name][0], n)]

        def const(name):
            return consts[:, CONSTS[name][0]:CONSTS[name][0] + CONSTS[name][1]]

        keep = Region(base, end)
        xT = keep.take("xT", [P, DC, T])
        w_raw = [keep.take(f"w_raw{s}", [P, UNIT]) for s in range(2)]
        w_hi = [keep.take(f"w_hi{s}", [P, UNIT], F32R) for s in range(2)]
        w_lo = [keep.take(f"w_lo{s}", [P, UNIT], F32R) for s in range(2)]
        params = keep.take("params", [P, NPARAM])
        consts = keep.take("consts", [P, NCONST])
        tick = keep.take("tick", [P, 16])
        arena = keep.at
        ops_end = arena + 2 * DC * TM * 4
        lin = Region(arena, ops_end)
        a_hi = lin.take("a_hi", [P, DC, TM], F32R)
        a_lo = lin.take("a_lo", [P, DC, TM], F32R)
        mix_end = ops_end + DC * T * 4
        hid = Region(ops_end, mix_end)
        h_hi = hid.take("h_hi", [P, FG // P, T], F32R)
        h_lo = hid.take("h_lo", [P, FG // P, T], F32R)
        mixT = Region(ops_end, mix_end).take("mixT", [P, DC, T])
        tmp = Region(mix_end, end)
        metaT = tmp.take("metaT", [P, DC, META])
        n_sq = [tmp.take(f"n_sq{s}", [P, T]) for s in range(2)]
        n_rs = tmp.take("n_rs", [P, T])
        n_y = [tmp.take(f"n_y{s}", [P, T]) for s in range(2)]
        u_act = [tmp.take(f"u_act{s}", [P, T]) for s in range(2)]
        u_sq = [tmp.take(f"u_sq{s}", [P, T]) for s in range(2)]
        stage_tiles = Region(ops_end, mix_end)
        staged = [stage_tiles.take(f"staged{s}", [P, TM]) for s in range(2)]

        ps = ctx.enter_context(nc.psum_tensor("ps", [P, 8, HALF], F32))

        def banks(b, n=2):
            return ps[:, b:b + n, :].rearrange("p b n -> p (b n)")

        w_landed = [sem(f"w_landed{s}") for s in range(2)]
        w_hi_done = [sem(f"w_hi_done{s}") for s in range(2)]
        w_split = [sem(f"w_split{s}") for s in range(2)]
        mm_done = [sem(f"mm_done{s}") for s in range(2)]
        ps_free = [sem(f"ps_free{s}") for s in range(2)]
        stored = [sem(f"stored{s}") for s in range(2)]
        loaded = sem("loaded")
        hid_sq = sem("hid_sq")
        hid_hi = sem("hid_hi")
        hid_ready = sem("hid_ready")
        mix_hi = sem("mix_hi")
        mix_ready = sem("mix_ready")

        class Stage:
            pass

        counts = {"pairs": 0, "stores": [0, 0], "mlps": 0}

        def linear(kind, weights, pairs, h=None, tail=False, n=T, bias=False):
            st = Stage()
            st.kind, st.w, st.pairs, st.next = kind, weights, pairs, None
            st.h, st.tail, st.n, st.bias = h, tail, n, bias
            st.k0, st.m0 = counts["pairs"], counts["mlps"]
            st.q0 = list(counts["stores"])
            counts["pairs"] += pairs
            if kind == "proj":
                counts["stores"] = [st.q0[0] + pairs, st.q0[1] + pairs - tail]
            counts["mlps"] += kind == "mlp"
            return st

        proj1 = linear("proj", g["w_in1"], padded(COLS1) // 256, h=g["h1"], tail=True)
        out1 = linear("out", g["w_out1"], 4)
        mlp1 = linear("mlp", g["w_mlp1"], 4 * NG, bias=True)
        proj2 = linear("proj", g["w_in2"], padded(COLS2) // 256, h=g["h2"])
        out2 = linear("out", g["w_out2"], 4)
        mlp2 = linear("mlp", g["w_mlp2"], 4 * NG, bias=False)
        proj3 = linear("proj", g["w_in3"], padded(COLS3) // 256, h=g["h3"], tail=True, n=TM)
        out3 = linear("out", g["w_out3"], 4)
        mlp3 = linear("mlp", g["w_mlp3"], 4 * NG, bias=False)
        linears = [proj1, out1, mlp1, proj2, out2, mlp2, proj3, out3, mlp3]
        for a, b in zip(linears, linears[1:]):
            a.next = b

        def layer_read(eng, st):
            for s in range(2):
                eng.wait_ge(ps_free[s], st.k0 + st.pairs + 1)

        def first_pair_sp(sp, st):
            for s in range(2):
                sp.wait_ge(w_split[s], st.k0 + 1)
                sp.dma_start(w_raw[s][:, :], st.w[s]).then_inc(w_landed[s], 16)

        def linear_sp(sp, st):
            first = TM - st.n

            def store(s, row, k):
                sp.wait_ge(ps_free[s], k + 2)
                sp.dma_start(st.h[bass.ds(row, P), :], staged[s][:, first:TM]).then_inc(stored[s], 16)

            with sp.Fori(1, st.pairs) as p:
                units = [sp.snap(2 * p + s) for s in range(2)]
                rows = [sp.snap(2 * P * p + (s - 2) * P) for s in range(2)]
                for s in range(2):
                    sp.wait_ge(w_split[s], p + (st.k0 + 1))
                    sp.dma_start(w_raw[s][:, :], st.w[bass.ds(units[s], 1)].rearrange("o p n -> (o p) n"))\
                        .then_inc(w_landed[s], 16)
                if st.kind == "proj":
                    for s in range(2):
                        store(s, rows[s], p + (st.k0 - 1))
            if st.next is not None:
                first_pair_sp(sp, st.next)
            if st.kind == "proj":
                store(0, 2 * P * (st.pairs - 1), st.k0 + st.pairs - 1)
                if not st.tail:
                    store(1, 2 * P * (st.pairs - 1) + P, st.k0 + st.pairs - 1)

        def split_hi(act, s, k):
            act.wait_ge(w_landed[s], 16 * k + 16)
            act.wait_ge(mm_done[s], k + 1)
            nc.scalar.activation(w_hi[s][:, :], w_raw[s][:, :], ACT.Copy).then_inc(w_hi_done[s], 1)

        def split_lo(dve, s, k):
            dve.wait_ge(w_hi_done[s], k + 1)
            nc.vector.tensor_tensor(w_lo[s][:, :], w_raw[s][:, :], w_hi[s][:, :].bitcast(F32),
                                    ALU.subtract).then_inc(w_split[s], 1)

        def three(s, hi, lo):
            return (w_hi[s], hi), (w_hi[s], lo), (w_lo[s], hi)

        def unit_mm(s, n):
            spans = [(META, META + HALF), (META + HALF, TM), (0, META)][:3 if n == TM else 2]
            for k in range(DC):
                for j, (w, a) in enumerate(three(s, a_hi, a_lo)):
                    for b, (t0, t1) in enumerate(spans):
                        last = nc.tensor.matmul(ps[:, 4 * s + b, 0:t1 - t0], w[:, k * P:(k + 1) * P], a[:, k, t0:t1],
                                                start=(k == 0 and j == 0), stop=(k == DC - 1 and j == 2))
            return last

        def unit_wait(pe, s, k):
            pe.wait_ge(w_split[s], k + 2)
            pe.wait_ge(ps_free[s], k + 1)

        def proj_pe(pe, st):
            with pe.Fori(0, st.pairs - st.tail) as p:
                for s in range(2):
                    unit_wait(pe, s, p + st.k0)
                    unit_mm(s, st.n).then_inc(mm_done[s], 1)
            if st.tail:
                k = st.k0 + st.pairs - 1
                unit_wait(pe, 0, k)
                unit_mm(0, st.n).then_inc(mm_done[0], 1)
                unit_wait(pe, 1, k)
                nc.tensor.matmul(ps[:, 4, 0:P], w_hi[1][:, 0:P], a_hi[:, 0, META:META + P], start=True, stop=True)\
                    .then_inc(mm_done[1], 1)

        def proj_act(act, st):
            def unit(s, k, q, whole=True):
                split_hi(act, s, k + 1)
                act.wait_ge(mm_done[s], k + 2)
                if not whole:
                    nc.scalar.activation(tick[:, 7:8], param("zero"), ACT.Copy).then_inc(ps_free[s], 1)
                    return
                act.wait_ge(stored[s], 16 * q + 16)
                if st.n == TM:
                    nc.scalar.activation(staged[s][:, 0:META], ps[:, 4 * s + 2, 0:META], ACT.Copy)
                nc.scalar.activation(staged[s][:, META:TM], banks(4 * s), ACT.Copy)\
                    .then_inc(ps_free[s], 1)

            with act.Fori(0, st.pairs - st.tail) as p:
                for s in range(2):
                    unit(s, p + st.k0, p + st.q0[s])
            if st.tail:
                for s in range(2):
                    unit(s, st.k0 + st.pairs - 1, st.q0[s] + st.pairs - 1, whole=(s == 0))

        def proj_dve(dve, st):
            with dve.Fori(0, st.pairs) as p:
                for s in range(2):
                    split_lo(dve, s, p + (st.k0 + 1))

        def proj_stored(eng, st):
            for s in range(2):
                eng.wait_ge(stored[s], 16 * (st.q0[s] + st.pairs - (st.tail and s == 1)) + 16)

        def mix_split_act(act, i):
            for c in range(DC):
                nc.scalar.activation(a_hi[:, c, META:TM], mixT[:, c, :], ACT.Copy).then_inc(mix_hi, 1)

        def mix_split_dve(dve, i):
            for c in range(DC):
                dve.wait_ge(mix_hi, DC * i + c + 1)
                nc.vector.tensor_tensor(a_lo[:, c, META:TM], mixT[:, c, :], a_hi[:, c, META:TM].bitcast(F32),
                                        ALU.subtract).then_inc(mix_ready, 1)

        def out_pe(pe, st, i):
            pe.wait_ge(mix_ready, DC * i + DC)
            with pe.Fori(0, st.pairs) as p:
                for s in range(2):
                    unit_wait(pe, s, p + st.k0)
                    unit_mm(s, T).then_inc(mm_done[s], 1)

        def out_act(act, st):
            with act.Fori(0, st.pairs) as p:
                for s in range(2):
                    split_hi(act, s, p + (st.k0 + 1))

        def out_dve(dve, st):
            with dve.Fori(0, st.pairs) as p:
                for s in range(2):
                    chunk = xT[:, bass.ds(2 * p + s, 1), :].rearrange("p o t -> p (o t)")
                    split_lo(dve, s, p + (st.k0 + 1))
                    dve.wait_ge(mm_done[s], p + (st.k0 + 2))
                    nc.vector.tensor_tensor(chunk, chunk, banks(4 * s), ALU.add).then_inc(ps_free[s], 1)

        def mlp_pe(pe, st):
            with pe.Fori(0, NG) as gr:
                for j in range(4):
                    unit_wait(pe, j % 2, 4 * gr + (st.k0 + j // 2))
                    unit_mm(j % 2, T).then_inc(mm_done[j % 2], 1)
                for j in range(4):
                    s = j % 2
                    unit_wait(pe, s, 4 * gr + (st.k0 + 2 + j // 2))
                    for k in range(FG // P):
                        if j == 0:
                            pe.wait_ge(hid_ready, 4 * gr + (4 * NG * st.m0 + k + 1))
                        for c in range(2):
                            for i, (w, a) in enumerate(three(s, h_hi, h_lo)):
                                for b in range(2):
                                    last = nc.tensor.matmul(
                                        ps[:, 4 * s + 2 * c + b, :], w[:, k * 256 + c * P:k * 256 + (c + 1) * P],
                                        a[:, k, b * HALF:(b + 1) * HALF], start=(k == 0 and i == 0),
                                        stop=(k == FG // P - 1 and i == 2))
                    last.then_inc(mm_done[s], 1)

        def mlp_act(act, st):
            def group(gr, final=False):
                for j in range(4):
                    s = j % 2
                    k, q = 4 * gr + (st.k0 + j // 2), 4 * gr + (4 * NG * st.m0 + j)
                    split_hi(act, s, k + 1)
                    act.wait_ge(mm_done[s], k + 2)
                    act.wait_ge(hid_sq, q + 1)
                    bias = param("b1", 4 * gr + j) if st.bias else 0.0
                    nc.scalar.activation(u_act[s][:, :], banks(4 * s), ACT.Relu, bias=bias).then_inc(ps_free[s], 1)
                    act.wait_ge(ps_free[s], k + 2)
                    nc.scalar.activation(h_hi[:, j, :], u_act[s][:, :], ACT.Square).then_inc(hid_hi, 1)
                for j in range(4):
                    if not (final and j >= 2):
                        split_hi(act, j % 2, 4 * gr + (st.k0 + 2 + j // 2 + 1))

            with act.Fori(0, NG - (st.next is None)) as gr:
                group(gr)
            if st.next is None:
                group(NG - 1, final=True)

        def mlp_dve(dve, st):
            def group(gr, final=False):
                for j in range(4):
                    s = j % 2
                    k, q = 4 * gr + (st.k0 + j // 2), 4 * gr + (4 * NG * st.m0 + j)
                    split_lo(dve, s, k + 1)
                    dve.wait_ge(ps_free[s], k + 2)
                    nc.vector.tensor_tensor(u_sq[s][:, :], u_act[s][:, :], u_act[s][:, :], ALU.mult).then_inc(hid_sq, 1)
                    dve.wait_ge(hid_sq, q + 3)
                    dve.wait_ge(hid_hi, q + 1)
                    nc.vector.tensor_tensor(h_lo[:, j, :], u_sq[s][:, :], h_hi[:, j, :].bitcast(F32),
                                            ALU.subtract).then_inc(hid_ready, 1)
                for j in range(4):
                    s = j % 2
                    k = 4 * gr + (st.k0 + 2 + j // 2)
                    if not (final and j >= 2):
                        split_lo(dve, s, k + 1)
                    dve.wait_ge(mm_done[s], k + 2)
                    two = xT[:, 2 * j:2 * j + 2, :].rearrange("p c t -> p (c t)")
                    nc.vector.tensor_tensor(two, two, banks(4 * s, 4), ALU.add).then_inc(ps_free[s], 1)

            with dve.Fori(0, NG - (st.next is None)) as gr:
                group(gr)
            if st.next is None:
                group(NG - 1, final=True)

        n_sum = sem("n_sum")
        n_centred = sem("n_centred")
        n_squared = sem("n_squared")
        n_summed = sem("n_summed")
        n_ln = sem("n_ln")
        n_rstd = sem("n_rstd")
        n_scaled = sem("n_scaled")
        n_hi = sem("n_hi")
        n_done = sem("n_done")
        norms = {"all": 0, "centred": 0, "hi": 0, "split": 0}

        class Norm:

            def __init__(self, x, n, at, gamma, beta=None, eps="eps6", scale=None, plus=None, split=True):
                self.x, self.n, self.at, self.gamma, self.beta, self.eps = x, n, at, gamma, beta, eps
                self.scale, self.plus, self.split = scale, plus, split
                self.shift = beta is not None
                self.i, self.ic, self.ih, self.io = (norms[key] for key in ("all", "centred", "hi", "split"))
                norms["all"] += 1
                norms["centred"] += self.shift
                norms["hi"] += self.shift or split
                norms["split"] += split
                self.spans = [(0, HALF), (HALF, T)] if n == T else [(0, n)]

        def norm_pe(pe, m):
            if m.beta:
                for c in range(DC):
                    for b, (t0, t1) in enumerate(m.spans):
                        last = nc.tensor.matmul(ps[:, b, 0:t1 - t0], const("ones"), m.x[:, c, t0:t1],
                                                start=(c == 0), stop=(c == DC - 1))
                last.then_inc(n_sum, 1)
            for c in range(DC):
                pe.wait_ge(n_squared, DC * m.i + c + 1)
                for b, (t0, t1) in enumerate(m.spans):
                    last = nc.tensor.matmul(ps[:, 2 + b, 0:t1 - t0], const("ones"), n_sq[c % 2][:, t0:t1],
                                            start=(c == 0), stop=(c == DC - 1))
                last.then_inc(n_summed, 1)

        def norm_act(act, m):
            for c in range(DC):
                if m.beta:
                    act.wait_ge(n_centred, DC * m.ic + c + 1)
                if c >= 2:
                    act.wait_ge(n_summed, DC * m.i + c - 1)
                nc.scalar.activation(n_sq[c % 2][:, 0:m.n], m.x[:, c, :], ACT.Square).then_inc(n_squared, 1)
            act.wait_ge(n_summed, DC * m.i + DC)
            nc.scalar.activation(n_rs[:, 0:m.n], banks(2)[:, 0:m.n], ACT.Ln, bias=param(m.eps), scale=1.0 / D).then_inc(n_ln, 1)
            act.wait_ge(n_ln, m.i + 1)
            nc.scalar.activation(n_rs[:, 0:m.n], n_rs[:, 0:m.n], ACT.Exp, scale=-0.5).then_inc(n_rstd, 1)
            if not (m.split or m.beta):
                return
            for c in range(DC):
                act.wait_ge(n_scaled, DC * m.i + c + 1)
                hi = a_hi[:, c, m.at:m.at + m.n]
                if m.beta:
                    if m.split:
                        nc.scalar.activation(hi, m.x[:, c, :], ACT.Identity, bias=param(m.beta, c))
                    nc.scalar.activation(m.x[:, c, :], m.x[:, c, :], ACT.Identity, bias=param(m.beta, c)).then_inc(n_hi, 1)
                else:
                    nc.scalar.activation(hi, n_y[c % 2][:, 0:m.n], ACT.Copy).then_inc(n_hi, 1)

        def norm_dve(dve, m):
            if m.beta:
                dve.wait_ge(n_sum, m.ic + 1)
                for c in range(DC):
                    nc.vector.scalar_tensor_tensor(m.x[:, c, :], banks(0)[:, 0:m.n], -1.0 / D, m.x[:, c, :],
                                                   op0=ALU.mult, op1=ALU.add).then_inc(n_centred, 1)
            dve.wait_ge(n_rstd, m.i + 1)

            def scale(c):
                out = m.x[:, c, :] if m.beta or not m.split else n_y[c % 2][:, 0:m.n]
                if m.beta:
                    dve.wait_ge(n_centred, DC * m.ic + c + 1)
                elif m.split:
                    dve.wait_ge(n_done, DC * m.io + max(c - 1, 0))
                nc.vector.scalar_tensor_tensor(out, m.x[:, c, :], param(m.gamma, c), n_rs[:, 0:m.n],
                                               op0=ALU.mult, op1=ALU.mult).then_inc(n_scaled, 1)

            def low(c):
                dve.wait_ge(n_hi, DC * m.ih + c + 1)
                val = m.x[:, c, :] if m.beta else n_y[c % 2][:, 0:m.n]
                nc.vector.tensor_tensor(a_lo[:, c, m.at:m.at + m.n], val, a_hi[:, c, m.at:m.at + m.n].bitcast(F32),
                                        ALU.subtract).then_inc(n_done, 1)
                if m.scale:
                    plus = param(m.plus, c) if m.plus else param("zero")
                    nc.vector.tensor_scalar(val, val, m.scale, plus, ALU.mult, ALU.add).then_inc(res_scaled, 1)

            if not m.split:
                for c in range(DC):
                    scale(c)
                return
            scale(0)
            for c in range(1, DC):
                scale(c)
                low(c - 1)
            low(DC - 1)

        res_scaled = sem("res_scaled")

        def norm_split(eng, m):
            eng.wait_ge(n_done, DC * m.io + DC)

        def norm_shifted(eng, m):
            eng.wait_ge(n_hi, DC * m.ih + DC)

        ln_in = Norm(xT, T, META, "ln_in_g", "ln_in_b", "eps5", scale=ALPHA)
        ln1 = Norm(xT, T, META, "ln1_g", "ln1_b", "eps5", scale=ALPHA, plus="b2")
        ln2 = Norm(xT, T, META, "ln2_g", "ln2_b", "eps5", split=False)
        rms_mix2 = Norm(xT, T, META, "mix_g_2")
        rms_mlp2 = Norm(xT, T, META, "mlp_g_2")
        rms_meta = Norm(metaT, META, 0, "mix_g_3")
        rms_mix3 = Norm(xT, T, META, "mix_g_3")
        rms_mlp3 = Norm(xT, T, META, "mlp_g_3")
        rms_final = Norm(xT, T, META, "final_g", split=False)
        gop = Region(arena, ops_end)
        g_qT = gop.take("g_qT", [P, GH, T])
        g_kT = gop.take("g_kT", [P, GH, T])
        g_kt = gop.take("g_kt", [P, TC, GH, P])
        g_vt = gop.take("g_vt", [P, TC, GH, P])
        gwork = [Region(mix_end, end - 64), Region(ops_end + 4 * T * 4, mix_end)]
        g_const = gwork[0].take("g_const", [P, 20, P])
        g_gates = gwork[0].take("g_gates", [P, 8, 2, TC, GH])
        G_LOG, G_CUM, G_TOT, G_BETA, G_NEGDEC, G_KDEC, G_LAST, G_TMP = range(8)

        def gate(i):
            return g_gates[:, i].rearrange("p d c h -> p (d c h)")

        prep = Region(gwork[0].at, end - 64)
        g_in = [prep.take(f"g_in{j}", [P, T + 4]) for j in range(3)]
        g_act = [prep.take(f"g_act{j}", [P, T]) for j in range(3)]
        g_kn = prep.take("g_kn", [P, T])
        prep2 = Region(ops_end + 4 * T * 4, mix_end)
        g_sq = [prep2.take(f"g_sq{j}", [P, T]) for j in range(2)]
        g_rs = [prep2.take(f"g_rs{j}", [P, T]) for j in range(2)]
        g_ab = Region(gwork[0].at, end).take("g_ab", [16, T])
        g_alog = Region(gwork[0].at + 4 * T, end).take("g_alog", [P, 8])

        def work(d, name, shape):
            r = gwork[d]
            if r.at + 4 * int(np.prod(shape[1:])) > r.stop:
                r = gwork[0]
            return r.take(f"{name}{d}", shape)

        g_S = [work(d, "g_S", [P, GH, P]) for d in range(2)]
        g_gu = [work(d, "g_gu", [P, GH, P]) for d in range(2)]
        g_qd = [work(d, "g_qd", [P, GH, P]) for d in range(2)]
        g_D = [work(d, "g_D", [P, GH, P]) for d in range(2)]
        g_Dt = [work(d, "g_Dt", [P, GH, P]) for d in range(2)]
        g_A = [work(d, "g_A", [P, GH, P]) for d in range(2)]
        g_kd = [work(d, "g_kd", [P, GH, P]) for d in range(2)]
        g_vn = [work(d, "g_vn", [P, GH, P]) for d in range(2)]
        g_kc = [work(d, "g_kc", [P, GH, P]) for d in range(2)]
        g_gam = [work(d, "g_gam", [P, 2, GH, P]) for d in range(2)]
        g_off = [work(d, "g_off", [P, 2, GH, P]) for d in range(2)]

        gp_in = [sem(f"gp_in{j}") for j in range(3)]
        gp_free = [sem(f"gp_free{j}") for j in range(3)]
        gp_tap = sem("gp_tap")
        gp_silu = sem("gp_silu")
        gp_sq = sem("gp_sq")
        gp_sum = sem("gp_sum")
        gp_ln = sem("gp_ln")
        gp_rs = sem("gp_rs")
        gp_norm = sem("gp_norm")
        gp_tr = sem("gp_tr")
        gp_end = sem("gp_end")
        gg_in = sem("gg_in")
        gg = sem("gg")
        gg_tr = sem("gg_tr")
        gg_trc = sem("gg_trc")
        gg_act = sem("gg_act")
        gg_sum = sem("gg_sum")
        gg_ready = sem("gg_ready")
        NT = 5

        def gdn_sp(sp):
            proj_stored(sp, proj1)
            layer_read(sp, proj1)
            sp.dma_start(g_const[:, :, :], g["gdn_consts"]).then_inc(gg_in, 16)
            sp.dma_start(g_ab[:, :], g["h1"][4 * GH * P:4 * GH * P + 16, :]).then_inc(gg_in, 16)
            with sp.Fori(0, GH) as h:
                rows = [sp.snap(h * P + j * GH * P) for j in range(3)]
                for j in range(3):
                    if j == 0:
                        sp.wait_ge(gg_ready, 1)
                    sp.wait_ge(gp_free[j], h + 1)
                    sp.dma_start(g_in[j][:, 2:T + 2], g["h1"][bass.ds(rows[j], P), :]).then_inc(gp_in[j], 16)

        def gdn_gates_pe(pe):
            pe.wait_ge(gg_in, 32)
            for c in range(TC):
                last = nc.tensor.transpose(ps[:, 0, c * 16:(c + 1) * 16], g_ab[:, c * P:(c + 1) * P], const("ident")[0:16, 0:16])
            last.then_inc(gg_tr, 1)
            pe.wait_ge(gg, 8)
            for d in range(2):
                nc.tensor.matmul(ps[:, 1, 32 * d:32 * d + 32], g_const[:, 10 * d, :], gate(G_LOG)[:, 32 * d:32 * d + 32],
                                 start=True, stop=True)
            nc.tensor.matmul(ps[:, 2, 0:64], const("ones"), gate(G_LOG), start=True, stop=True).then_inc(gg_sum, 1)

        def gdn_gates_dve(dve):
            steps = [0]

            def step(ins):
                steps[0] += 1
                ins.then_inc(gg, 1)
                dve.wait_ge(gg, steps[0])

            dve.wait_ge(gg_tr, 1)
            a_part = ps[:, 0, 0:P].rearrange("p (c x) -> p c x", x=16)[:, :, 0:8].rearrange("p c (d h) -> p d c h", d=2)
            b_part = ps[:, 0, 0:P].rearrange("p (c x) -> p c x", x=16)[:, :, 8:16].rearrange("p c (d h) -> p d c h", d=2)
            bias = param("dt_bias", 0, 8).rearrange("p (d h) -> p d h", d=2)
            for d in range(2):
                step(nc.vector.tensor_tensor(g_gates[:, G_LOG, d], a_part[:, d],
                                             bias[:, d].unsqueeze(1).to_broadcast([P, TC, GH]), ALU.add))
            step(nc.vector.tensor_scalar(gate(G_TMP), gate(G_LOG), -1.0, None, ALU.mult))
            step(nc.vector.tensor_tensor(gate(G_TMP), gate(G_TMP), gate(G_LOG), ALU.min))
            for d in range(2):
                step(nc.vector.tensor_scalar(g_gates[:, G_BETA, d], b_part[:, d], -1.0, 85.0, ALU.mult, ALU.min))
            dve.wait_ge(gg_act, 3)
            step(nc.vector.scalar_tensor_tensor(gate(G_TMP), gate(G_LOG), 0.0, gate(G_TMP), op0=ALU.max, op1=ALU.add))
            nexp = g_alog[:, :].rearrange("p (d h) -> p d h", d=2)
            for d in range(2):
                ins = nc.vector.scalar_tensor_tensor(g_gates[:, G_LOG, d], g_gates[:, G_TMP, d], -1.0,
                                                     nexp[:, d].unsqueeze(1).to_broadcast([P, TC, GH]),
                                                     op0=ALU.mult, op1=ALU.mult)
                if d == 1:
                    step(ins)
            step(nc.vector.tensor_scalar(gate(G_BETA), gate(G_BETA), 1.0, None, ALU.add))
            step(nc.vector.reciprocal(gate(G_BETA), gate(G_BETA)))
            dve.wait_ge(gg_sum, 1)
            step(nc.vector.tensor_copy(gate(G_CUM), ps[:, 1, 0:64]))
            step(nc.vector.tensor_copy(gate(G_TOT), ps[:, 2, 0:64]))
            step(nc.vector.tensor_tensor(gate(G_KDEC), gate(G_TOT), gate(G_CUM), ALU.subtract))
            dve.wait_ge(gg_act, 6)
            step(nc.vector.tensor_scalar(gate(G_NEGDEC), gate(G_NEGDEC), -1.0, None, ALU.mult))
            nc.vector.memset(mixT[:, 0:GH, :], 0.0).then_inc(gg_ready, 1)

        def gdn_gates_act(act):
            act.wait_ge(gg, 6)
            nc.scalar.activation(gate(G_TMP), gate(G_TMP), ACT.Exp).then_inc(gg_trc, 1)
            nc.scalar.activation(gate(G_BETA), gate(G_BETA), ACT.Exp).then_inc(gg_act, 1)
            nc.scalar.activation(g_alog[:, :], param("a_log", 0, 8), ACT.Exp).then_inc(gg_act, 1)
            act.wait_ge(gg_trc, 1)
            nc.scalar.activation(gate(G_TMP), gate(G_TMP), ACT.Ln, bias=param("one")).then_inc(gg_act, 1)
            act.wait_ge(gg, 13)
            nc.scalar.activation(gate(G_NEGDEC), gate(G_CUM), ACT.Exp).then_inc(gg_act, 1)
            nc.scalar.activation(gate(G_KDEC), gate(G_KDEC), ACT.Exp).then_inc(gg_act, 1)
            nc.scalar.activation(gate(G_LAST), gate(G_TOT), ACT.Exp).then_inc(gg_act, 1)

        def gdn_prep_dve(dve):
            for j in range(3):
                ends = g_in[j][:, 0:T + 4]
                nc.vector.memset(ends[:, 0:2], 0.0)
                nc.vector.memset(ends[:, T + 2:T + 4], 0.0).then_inc(gp_free[j], 1)
            with dve.Fori(0, GH) as h:
                for j in range(3):
                    dve.wait_ge(gp_in[j], 16 * h + 16)
                    dve.wait_ge(gp_end, h + 1)
                    for tap in range(NT):
                        w = param("conv_w", h * NT + (j * GH * NT + tap))
                        src = g_in[j][:, tap:tap + T]
                        if tap == 0:
                            ins = nc.vector.tensor_scalar(g_act[j][:, :], src, w, None, ALU.mult)
                        else:
                            dve.wait_ge(gp_tap, 3 * (NT - 1) * h + (j * (NT - 1) + tap))
                            ins = nc.vector.scalar_tensor_tensor(g_act[j][:, :], src, w, g_act[j][:, :],
                                                                 op0=ALU.mult, op1=ALU.add)
                        ins.then_inc(gp_tap if tap < NT - 1 else gp_free[j], 1)
                for j in range(2):
                    dve.wait_ge(gp_rs, 2 * h + (j + 1))
                    out = g_qT[:, bass.ds(h, 1), :].rearrange("p o t -> p (o t)") if j == 0 else g_kn[:, :]
                    nc.vector.scalar_tensor_tensor(out, g_act[j][:, :], float(P) ** -0.5 if j == 0 else 1.0, g_rs[j][:, :],
                                                   op0=ALU.mult, op1=ALU.mult).then_inc(gp_norm, 1)

        def gdn_prep_act(act):
            nc.scalar.activation(g_rs[0][:, 0:1], param("zero"), ACT.Copy).then_inc(gp_end, 1)
            with act.Fori(0, GH) as h:
                for j in range(3):
                    act.wait_ge(gp_free[j], h + 2)
                    nc.scalar.activation(g_act[j][:, :], g_act[j][:, :], ACT.Silu).then_inc(gp_silu, 1)
                for j in range(2):
                    act.wait_ge(gp_silu, 3 * h + (j + 1))
                    nc.scalar.activation(g_sq[j][:, :], g_act[j][:, :], ACT.Square).then_inc(gp_sq, 1)
                for j in range(2):
                    act.wait_ge(gp_sum, 2 * h + (j + 1))
                    nc.scalar.activation(g_rs[j][:, :], banks(2 * j), ACT.Ln, bias=param("eps6")).then_inc(gp_ln, 1)
                for j in range(2):
                    act.wait_ge(gp_ln, 2 * h + (j + 1))
                    nc.scalar.activation(g_rs[j][:, :], g_rs[j][:, :], ACT.Exp, scale=-0.5).then_inc(gp_rs, 1)
                head = bass.ds(h, 1)
                act.wait_ge(gp_tr, 2 * h + 1)
                nc.scalar.activation(g_vt[:, :, head, :].rearrange("p c o t -> p c (o t)"),
                                     banks(6).rearrange("p (c t) -> p c t", t=P), ACT.Copy)
                act.wait_ge(gp_norm, 2 * h + 2)
                nc.scalar.activation(g_kT[:, head, :].rearrange("p o t -> p (o t)"), g_kn[:, :], ACT.Copy)
                act.wait_ge(gp_tr, 2 * h + 2)
                nc.scalar.activation(g_kt[:, :, head, :].rearrange("p c o t -> p c (o t)"),
                                     banks(4).rearrange("p (c t) -> p c t", t=P), ACT.Copy).then_inc(gp_end, 1)

        def gdn_prep_pe(pe):
            with pe.Fori(0, GH) as h:
                for j in range(2):
                    pe.wait_ge(gp_end, h + 1)
                    pe.wait_ge(gp_sq, 2 * h + (j + 1))
                    for b in range(2):
                        last = nc.tensor.matmul(ps[:, 2 * j + b, :], const("ones"), g_sq[j][:, b * HALF:(b + 1) * HALF],
                                                start=True, stop=True)
                    last.then_inc(gp_sum, 1)
                pe.wait_ge(gp_silu, 3 * h + 3)
                for c in range(TC):
                    last = nc.tensor.transpose(banks(6)[:, c * P:(c + 1) * P], g_act[2][:, c * P:(c + 1) * P], const("ident"))
                last.then_inc(gp_tr, 1)
                pe.wait_ge(gp_norm, 2 * h + 2)
                for c in range(TC):
                    last = nc.tensor.transpose(banks(4)[:, c * P:(c + 1) * P], g_kn[:, c * P:(c + 1) * P], const("ident"))
                last.then_inc(gp_tr, 1)

        gs_names = ["gu", "kc", "row", "diff", "dec", "gam", "eg", "kk", "kq", "A", "qk", "qd", "kd", "off", "D", "Dt", "Q", "Qs",
                    "X1", "X2", "kS", "r1", "R", "V", "vn", "o", "su", "end"]
        gs = {name: sem(f"gs_{name}") for name in gs_names}
        NL = GDN_LEVELS

        def chunk_of(n, d):
            return n if d == 0 else n * -1 + (TC - 1)

        def gate_of(n, d):
            return 4 * n if d == 0 else n * -4 + (32 + 4 * (TC - 1))

        def once(n, d):
            return 2 * n + (d + 1)

        def level(n, d, l):
            return 2 * NL * n + (2 * l + d + 1)

        def four(t):
            return t.rearrange("p h x -> p (h x)")

        def pbank(b):
            return ps[:, b, :].rearrange("p (h x) -> p h x", h=GH)

        def gmask(d, j):
            return g_const[:, 10 * d + j, :].unsqueeze(1).to_broadcast([P, GH, P])

        def gcols(i, n, d):
            return gate(i)[:, bass.ds(gate_of(n, d), GH)].unsqueeze(2).to_broadcast([P, GH, P])

        def gcol(i, n, d, h):
            return gate(i)[:, bass.ds(gate_of(n, d) + h, 1)]

        ident4 = const("ident").unsqueeze(1).to_broadcast([P, GH, P])

        def gdn_loop_pe(pe):
            def heads(b, lhsT, rhs, start=True, stop=True):
                for h in range(GH):
                    last = nc.tensor.matmul(pbank(b)[:, h, :], lhsT[:, h, :], rhs[:, h, :], start=start, stop=stop)
                return last

            with pe.Fori(0, TC) as n:
                toks = [bass.ds(P * chunk_of(n, d), P) for d in range(2)]
                for d in range(2):
                    pe.wait_ge(gs["gu"], once(n, d))
                    nc.tensor.matmul(ps[:, 4 * d, :], const("ones"), four(g_gu[d][:, :, :]), start=True, stop=True)\
                        .then_inc(gs["row"], 1)
                    pe.wait_ge(gs["kc"], once(n, d))
                    heads(4 * d + 1, g_kc[d], g_kc[d]).then_inc(gs["kk"], 1)
                    heads(4 * d + 2, g_kc[d], g_qT[:, :, toks[d]]).then_inc(gs["kq"], 1)
                for l in range(NL):
                    for d in range(2):
                        pe.wait_ge(gs["off"], level(n, d, l))
                        if l:
                            pe.wait_ge(gs["Dt"], level(n, d, l - 1))
                        for h in range(GH):
                            rhs = g_Dt[d][:, h, :] if l else const("ident")
                            last = nc.tensor.matmul(pbank(4 * d + 1)[:, h, :], g_off[d][:, l % 2, h, :], rhs, start=True, stop=True)
                        last.then_inc(gs["Q"], 1)
                    if l == 0:
                        continue
                    for d in range(2):
                        pe.wait_ge(gs["Qs"], 2 * (NL - 1) * n + (2 * (l - 1) + d + 1))
                        pe.wait_ge(gs["D"], 2 * (NL - 1) * n + (2 * (l - 1) + d + 1))
                        if l == 1:
                            pe.wait_ge(gs["qk"], once(n, d))
                        heads(4 * d + 2, g_D[d], g_gu[d]).then_inc(gs["X1"], 1)
                        if l < NL - 1:
                            heads(4 * d + 3, g_gu[d], g_D[d]).then_inc(gs["X2"], 1)
                for d in range(2):
                    pe.wait_ge(gs["qd"], once(n, d))
                    heads(4 * d, g_kc[d], g_S[d]).then_inc(gs["kS"], 1)
                for d in range(2):
                    pe.wait_ge(gs["R"], once(n, d))
                    pe.wait_ge(gs["Dt"], level(n, d, NL - 1))
                    heads(4 * d + 1, g_Dt[d], g_A[d]).then_inc(gs["V"], 1)
                for d in range(2):
                    pe.wait_ge(gs["vn"], once(n, d))
                    pe.wait_ge(gs["kd"], once(n, d))
                    for h in range(GH):
                        o = pbank(4 * d + 2)[:, h, :]
                        nc.tensor.matmul(o, g_S[d][:, h, :], g_qd[d][:, h, :], start=True, stop=False)
                        last = nc.tensor.matmul(o, g_vn[d][:, h, :], g_gam[d][:, 0, h, :], start=False, stop=True)
                    last.then_inc(gs["o"], 1)
                    heads(4 * d + 3, g_kd[d], g_vn[d]).then_inc(gs["su"], 1)

        def gdn_loop_act(act):
            with act.Fori(0, TC) as n:
                for d in range(2):
                    act.wait_ge(gs["end"], once(n, d))
                    nc.scalar.activation(g_kc[d][:, :, :], g_kT[:, :, bass.ds(P * chunk_of(n, d), P)], ACT.Copy)\
                        .then_inc(gs["kc"], 1)
                for d in range(2):
                    act.wait_ge(gs["row"], once(n, d))
                    nc.scalar.activation(four(g_qd[d][:, :, :]), ps[:, 4 * d, :], ACT.Exp).then_inc(gs["eg"], 1)
                for d in range(2):
                    act.wait_ge(gs["dec"], once(n, d))
                    nc.scalar.activation(g_gam[d][:, :, :, :].rearrange("p a h x -> p (a h x)"),
                                         g_gam[d][:, :, :, :].rearrange("p a h x -> p (a h x)"), ACT.Exp).then_inc(gs["gam"], 1)
                for l in range(1, NL):
                    for d in range(2):
                        act.wait_ge(gs["Q"], level(n, d, l))
                        nc.scalar.activation(four(g_gu[d][:, :, :]), ps[:, 4 * d + 1, :], ACT.Copy).then_inc(gs["Qs"], 1)
                for d in range(2):
                    act.wait_ge(gs["V"], once(n, d))
                    nc.scalar.activation(four(g_vn[d][:, :, :]), ps[:, 4 * d + 1, :], ACT.Copy).then_inc(gs["vn"], 1)

        def gdn_loop_pool(pool):
            with pool.Fori(0, TC) as n:
                for l in range(NL):
                    for d in range(2):
                        if l == 0:
                            pool.wait_ge(gs["A"], once(n, d))
                        if l >= 2:
                            pool.wait_ge(gs["Q"], level(n, d, l - 2))
                        if l == 2:
                            pool.wait_ge(gs["D"], 2 * (NL - 1) * n + (d + 1))
                        nc.gpsimd.tensor_tensor(g_off[d][:, l % 2], g_A[d][:, :, :], gmask(d, 3 + l), ALU.mult)\
                            .then_inc(gs["off"], 1)

        def gdn_loop_dve(dve):
            dve.wait_ge(gp_end, GH + 1)
            for d in range(2):
                nc.vector.memset(g_S[d][:, :, :], 0.0).then_inc(gs["end"], 1)
            with dve.Fori(0, TC) as n:
                toks = [bass.ds(P * chunk_of(n, d), P) for d in range(2)]
                for d in range(2):
                    dve.wait_ge(gs["end"], once(n, d))
                    nc.vector.tensor_tensor(g_gu[d][:, :, :], gmask(d, 0), gcols(G_LOG, n, d), ALU.mult).then_inc(gs["gu"], 1)
                for d in range(2):
                    nc.vector.tensor_tensor(g_kd[d][:, :, :], g_kt[:, bass.ds(chunk_of(n, d), 1)].rearrange("p o h x -> p (o h) x"),
                                            gcols(G_KDEC, n, d), ALU.mult).then_inc(gs["kd"], 1)
                for d in range(2):
                    dve.wait_ge(gs["eg"], once(n, d))
                    nc.vector.tensor_tensor(g_gam[d][:, 0], pbank(4 * d), gcols(G_CUM, n, d), ALU.subtract).then_inc(gs["diff"], 1)
                    dve.wait_ge(gs["diff"], 2 * once(n, d) - 1)
                    nc.vector.tensor_tensor(g_gam[d][:, 1], gmask(d, 2), g_gam[d][:, 0], ALU.subtract).then_inc(gs["diff"], 1)
                    dve.wait_ge(gs["diff"], 2 * once(n, d))
                    nc.vector.tensor_tensor(g_gam[d][:, 0], g_gam[d][:, 0], gmask(d, 1), ALU.add).then_inc(gs["dec"], 1)
                for d in range(2):
                    dve.wait_ge(gs["gam"], once(n, d))
                    dve.wait_ge(gs["kk"], once(n, d))
                    for h in range(GH):
                        ins = nc.vector.scalar_tensor_tensor(g_A[d][:, h, :], pbank(4 * d + 1)[:, h, :], gcol(G_BETA, n, d, h),
                                                             g_gam[d][:, 1, h, :], op0=ALU.mult, op1=ALU.mult)
                    ins.then_inc(gs["A"], 1)
                for d in range(2):
                    dve.wait_ge(gs["kq"], once(n, d))
                    nc.vector.tensor_tensor(g_gam[d][:, 0], pbank(4 * d + 2), g_gam[d][:, 0], ALU.mult).then_inc(gs["qk"], 1)
                    nc.vector.tensor_tensor(g_qd[d][:, :, :], g_qd[d][:, :, :], g_qT[:, :, toks[d]], ALU.mult).then_inc(gs["qd"], 1)
                for d in range(2):
                    dve.wait_ge(gs["off"], level(n, d, 0))
                    nc.vector.tensor_tensor(g_D[d][:, :, :], ident4, g_off[d][:, 0], ALU.subtract).then_inc(gs["D"], 1)
                for d in range(2):
                    dve.wait_ge(gs["Q"], level(n, d, 0))
                    nc.vector.tensor_tensor(g_Dt[d][:, :, :], ident4, pbank(4 * d + 1), ALU.subtract).then_inc(gs["Dt"], 1)
                for l in range(1, NL):
                    for d in range(2):
                        dve.wait_ge(gs["X1"], 2 * (NL - 1) * n + (2 * (l - 1) + d + 1))
                        nc.vector.tensor_tensor(g_Dt[d][:, :, :], g_Dt[d][:, :, :], pbank(4 * d + 2), ALU.subtract)\
                            .then_inc(gs["Dt"], 1)
                        if l < NL - 1:
                            dve.wait_ge(gs["X2"], 2 * (NL - 2) * n + (2 * (l - 1) + d + 1))
                            nc.vector.tensor_tensor(g_D[d][:, :, :], g_D[d][:, :, :], pbank(4 * d + 3), ALU.subtract)\
                                .then_inc(gs["D"], 1)
                for d in range(2):
                    dve.wait_ge(gs["kS"], once(n, d))
                    dve.wait_ge(gs["off"], level(n, d, NL - 1))
                    v = g_vt[:, bass.ds(chunk_of(n, d), 1)].rearrange("p o h x -> p (o h) x")
                    for h in range(GH):
                        ins = nc.vector.scalar_tensor_tensor(g_A[d][:, h, :], pbank(4 * d)[:, h, :], gcol(G_NEGDEC, n, d, h),
                                                             v[:, h, :], op0=ALU.mult, op1=ALU.add)
                    ins.then_inc(gs["r1"], 1)
                    dve.wait_ge(gs["r1"], once(n, d))
                    nc.vector.tensor_tensor(g_A[d][:, :, :], g_A[d][:, :, :], gcols(G_BETA, n, d), ALU.mult).then_inc(gs["R"], 1)
                for d in range(2):
                    dve.wait_ge(gs["o"], once(n, d))
                    out = mixT[:, 0:GH, toks[d]]
                    nc.vector.tensor_tensor(out, out, pbank(4 * d + 2), ALU.add)
                    dve.wait_ge(gs["su"], once(n, d))
                    for h in range(GH):
                        ins = nc.vector.scalar_tensor_tensor(g_S[d][:, h, :], g_S[d][:, h, :], gcol(G_LAST, n, d, h),
                                                             pbank(4 * d + 3)[:, h, :], op0=ALU.mult, op1=ALU.add)
                    ins.then_inc(gs["end"], 1)

        go_z = sem("go_z")
        go_silu = sem("go_silu")
        go_sq = sem("go_sq")
        go_sum = sem("go_sum")
        go_ln = sem("go_ln")
        go_rs = sem("go_rs")
        go_norm = sem("go_norm")
        go_end = sem("go_end")
        gout = Region(arena, ops_end)
        g_z = gout.take("g_z", [P, GH, T])
        g_osq = [gout.take(f"g_osq{j}", [P, T]) for j in range(2)]
        g_ors = [gout.take(f"g_ors{j}", [P, T]) for j in range(2)]

        def gdn_out_sp(sp):
            sp.wait_ge(gs["end"], 2 * TC + 2)
            sp.dma_start(g_z[:, :, :], g["h1"][3 * GH * P:4 * GH * P, :].rearrange("(h p) t -> p h t", p=P)).then_inc(go_z, 16)

        def gdn_out_pe(pe):
            for h in range(GH):
                pe.wait_ge(go_sq, h + 1)
                if h >= 2:
                    pe.wait_ge(go_ln, h - 1)
                for b in range(2):
                    last = nc.tensor.matmul(ps[:, 2 * (h % 2) + b, :], const("ones"), g_osq[h % 2][:, b * HALF:(b + 1) * HALF],
                                            start=True, stop=True)
                last.then_inc(go_sum, 1)

        def gdn_out_act(act):
            act.wait_ge(go_z, 16)
            for h in range(GH):
                nc.scalar.activation(g_z[:, h, :], g_z[:, h, :], ACT.Silu).then_inc(go_silu, 1)
            act.wait_ge(gs["end"], 2 * TC + 2)
            for h in range(GH):
                if h >= 2:
                    act.wait_ge(go_sum, h - 1)
                nc.scalar.activation(g_osq[h % 2][:, :], mixT[:, h, :], ACT.Square).then_inc(go_sq, 1)
                act.wait_ge(go_sum, h + 1)
                if h >= 2:
                    act.wait_ge(go_norm, h - 1)
                nc.scalar.activation(g_ors[h % 2][:, :], banks(2 * (h % 2)), ACT.Ln, bias=param("eps6"), scale=1.0 / P)\
                    .then_inc(go_ln, 1)
                act.wait_ge(go_ln, h + 1)
                nc.scalar.activation(g_ors[h % 2][:, :], g_ors[h % 2][:, :], ACT.Exp, scale=-0.5).then_inc(go_rs, 1)

        def gdn_out_dve(dve):
            for h in range(GH):
                dve.wait_ge(go_rs, h + 1)
                nc.vector.scalar_tensor_tensor(mixT[:, h, :], mixT[:, h, :], param("gdn_g"), g_ors[h % 2][:, :],
                                               op0=ALU.mult, op1=ALU.mult).then_inc(go_norm, 1)
                dve.wait_ge(go_norm, h + 1)
                dve.wait_ge(go_silu, h + 1)
                nc.vector.tensor_tensor(mixT[:, h, :], mixT[:, h, :], g_z[:, h, :], ALU.mult).then_inc(go_end, 1)

        at_names = ["load", "prep", "prepc", "zq", "s", "sc", "max", "neg", "p", "pt", "ptc", "av", "rs", "z", "sq", "ss", "ln", "r",
                    "zs", "o", "end", "bias"]
        at = {name: sem(f"at_{name}") for name in at_names}

        NP = NH1 // 2
        BAND = KR * GRID
        NA0 = 4 * GH * P + 16
        nop = Region(arena, ops_end)
        n_q = nop.take("n_q", [P, NP, T])
        n_k = nop.take("n_k", [P, NP, T])
        n_v = nop.take("n_v", [P, ROWS - 1, NP * P])
        nwk = Region(mix_end, end)
        n_bias = nwk.take("n_bias", [P, NP, 2 * KR - 1, GRID])
        n_mask = nwk.take("n_mask", [P, GRID])
        n_zq = nwk.take("n_zq", [P, NP, P])
        n_z = nwk.take("n_z", [P, NP, P])
        n_zsq = nwk.take("n_zsq", [P, NP, GRID])
        n_pt = [nwk.take(f"n_pt{j}", [P, KR // 2, P]) for j in range(2)]
        n_small = nwk.take("n_small", [P, 8, NP])
        N_MAX, N_NEG, N_SUM, N_INV, N_SS, N_LN, N_R = range(7)
        n_s = Region(nwk.at, end).take("n_s", [P, NP, BAND])
        n_vT = Region(nwk.at, end).take("n_vT", [P, NP, T])
        NA_END = {}

        RPB_W = 2 * KC - 1 + 2 * 48
        RPB = (2 * KR - 1) * RPB_W

        def na_bias_sp(sp):
            sp.dma_start(g["rpb_rows"], g["rpb"].unsqueeze(1).to_broadcast([NH1, GRID, RPB])).then_inc(at["bias"], 16)

        def na_sp(sp):
            def rows(first):
                return g["h1"][first:first + NP * P, :].rearrange("(c p) t -> p c t", p=P)

            sp.wait_ge(go_end, GH)
            sp.dma_start(n_vT[:, :, :], rows(NA0 + 2 * NP * P)).then_inc(at["load"], 16)
            sp.dma_start(n_q[:, :, :], rows(NA0)).then_inc(at["load"], 16)
            sp.dma_start(n_k[:, :, :], rows(NA0 + NP * P)).then_inc(at["load"], 16)
            sp.dma_start(n_mask[:, :], g["na_mask"]).then_inc(at["bias"], 16)
            sp.wait_ge(at["bias"], 32)
            for h in range(NH1):
                src = bass.AP(g["rpb_rows"].tensor, g["rpb_rows"].offset + h * GRID * RPB + GRID - 1,
                              [[RPB - 1, GRID], [RPB_W, 2 * KR - 1], [1, GRID]])
                sp.dma_start(n_bias[GRID * (h % 2):GRID * (h % 2) + GRID, h // 2], src).then_inc(at["bias"], 16)

        def na_pe(pe):
            pe.wait_ge(at["load"], 48)
            for i in range(ROWS - 1):
                if i >= 2:
                    pe.wait_ge(at["prepc"], i - 1)
                for c in range(NP):
                    last = nc.tensor.transpose(ps[:, i % 2, c * P:(c + 1) * P], n_vT[:, c, GRID * i:GRID * i + P], const("ident"))
                last.then_inc(at["prep"], 1)
            pe.wait_ge(at["prepc"], ROWS - 1)

            def row(r, r0, dr0):
                pe.wait_ge(at["zq"], r + 1)
                for c in range(NP):
                    nc.tensor.matmul(ps[:, c, :], n_zq[:, c, :], n_k[:, c, bass.ds(r0 * GRID, BAND)], start=True, stop=True)\
                        .then_inc(at["s"], 1)

                def turn(c):
                    pe.wait_ge(at["p"], NP * r + (c + 1))
                    if c >= 2:
                        pe.wait_ge(at["ptc"], NP * r + (c - 1))
                    for t in range(KR // 2):
                        last = nc.tensor.transpose(ps[:, 4 + c % 2, t * P:(t + 1) * P], n_s[:, c, t * P:(t + 1) * P], const("ident"))
                    last.then_inc(at["pt"], 1)

                def weigh(c):
                    pe.wait_ge(at["ptc"], NP * r + (c + 1))
                    for t in range(KR // 2):
                        v = n_v[:, bass.ds(r0 + 2 * t, 1), c * P:(c + 1) * P].rearrange("p o x -> p (o x)")
                        last = nc.tensor.matmul(ps[:, 6, c * P:(c + 1) * P], n_pt[c % 2][:, t, :], v,
                                                start=(t == 0), stop=(t == KR // 2 - 1))
                    last.then_inc(at["av"], 1)

                turn(0)
                turn(1)
                for c in range(NP):
                    weigh(c)
                    if c + 2 < NP:
                        turn(c + 2)
                pe.wait_ge(at["zs"], r + 1)
                for c in range(NP):
                    last = nc.tensor.matmul(ps[:, 7, c * GRID:(c + 1) * GRID], n_z[:, c, :], const("fold"), start=True, stop=True)
                last.then_inc(at["o"], 1)

            na_rows(pe, row)

        def na_rows(eng, row):
            with eng.Fori(0, KR // 2) as r:
                row(r, r * 0, r * -1 + (KR - 1))
            with eng.Fori(KR // 2, ROWS - KR // 2 + 1) as r:
                row(r, r + -(KR // 2), r * 0 + (KR // 2 - 1))
            with eng.Fori(ROWS - KR // 2 + 1, ROWS) as r:
                row(r, r * 0 + (ROWS - KR), r * -1 + (ROWS - 1))

        def diagonals(t, width):
            return [(slice(GRID * j, GRID * j + GRID), t[GRID * j:GRID * j + GRID, :, width * j:width * (j + 1)]) for j in range(2)]

        def na_act(act):
            for i in range(ROWS - 1):
                act.wait_ge(at["prep"], i + 1)
                nc.scalar.activation(n_v[:, i, :], ps[:, i % 2, :], ACT.Copy).then_inc(at["prepc"], 1)
            act.wait_ge(at["end"], 1)

            def row(r, r0, dr0):
                for j, (rows, block) in enumerate(diagonals(n_zq, GRID)):
                    ins = nc.scalar.activation(block, n_q[rows, :, bass.ds(r * GRID, GRID)], ACT.Copy)
                ins.then_inc(at["zq"], 1)
                act.wait_ge(at["neg"], r + 1)
                for c in range(NP):
                    nc.scalar.activation(n_s[:, c, :], n_s[:, c, :], ACT.Exp, bias=n_small[:, N_NEG, c:c + 1],
                                         accum_out=n_small[:, N_SUM, c:c + 1]).then_inc(at["p"], 1)
                for c in range(NP):
                    act.wait_ge(at["pt"], NP * r + (c + 1))
                    if c >= 2:
                        act.wait_ge(at["av"], NP * r + (c - 1))
                    nc.scalar.activation(n_pt[c % 2][:, :, :].rearrange("p t x -> p (t x)"), ps[:, 4 + c % 2, :], ACT.Copy)\
                        .then_inc(at["ptc"], 1)
                act.wait_ge(at["ss"], r + 1)
                nc.scalar.activation(n_small[:, N_LN, :], n_small[:, N_SS, :], ACT.Ln, bias=param("eps6"), scale=1.0 / GRID)\
                    .then_inc(at["ln"], 1)
                act.wait_ge(at["ln"], r + 1)
                nc.scalar.activation(n_small[:, N_R, :], n_small[:, N_LN, :], ACT.Exp, scale=-0.5).then_inc(at["r"], 1)
                act.wait_ge(at["o"], r + 1)
                nc.scalar.activation(mixT[:, GH:DC, bass.ds(r * GRID, GRID)], ps[:, 7, 0:NP * GRID].rearrange("p (c x) -> p c x", c=NP),
                                     ACT.Copy, scale=param("na_g")).then_inc(at["end"], 1)

            na_rows(act, row)

        def na_dve(dve):
            dve.wait_ge(go_end, GH)
            nc.vector.memset(n_zq[:, :, :], 0.0)
            nc.vector.memset(n_z[:, :, :], 0.0).then_inc(at["end"], 1)
            dve.wait_ge(at["bias"], 16 * (NH1 + 2))
            flat = n_bias[:, :, :, :].rearrange("p c r x -> p (c r) x")
            nc.vector.tensor_tensor(flat, flat, n_mask[:, :].unsqueeze(1).to_broadcast([P, NP * (2 * KR - 1), GRID]), ALU.add)\
                .then_inc(at["bias"], 1)
            dve.wait_ge(at["bias"], 16 * (NH1 + 2) + 1)
            dve.wait_ge(at["prepc"], ROWS - 1)

            def row(r, r0, dr0):
                for c in range(NP):
                    dve.wait_ge(at["s"], NP * r + (c + 1))
                    nc.vector.scalar_tensor_tensor(
                        n_s[:, c, :], ps[:, c, :], float(GRID) ** -0.5,
                        n_bias[:, c, bass.ds(dr0, KR), :].rearrange("p r x -> p (r x)"), op0=ALU.mult, op1=ALU.add)\
                        .then_inc(at["sc"], 1)
                dve.wait_ge(at["sc"], NP * r + NP)
                nc.vector.tensor_reduce(n_small[:, N_MAX, :], n_s[:, :, :], AX.X, ALU.max).then_inc(at["max"], 1)
                dve.wait_ge(at["max"], r + 1)
                nc.vector.tensor_scalar(n_small[:, N_NEG, :], n_small[:, N_MAX, :], -1.0, None, ALU.mult).then_inc(at["neg"], 1)
                dve.wait_ge(at["p"], NP * r + NP)
                nc.vector.reciprocal(n_small[:, N_INV, :], n_small[:, N_SUM, :]).then_inc(at["rs"], 1)
                dve.wait_ge(at["rs"], r + 1)
                dve.wait_ge(at["av"], NP * r + NP)
                dve.wait_ge(at["end"], r + 1)
                out = ps[:, 6, :].rearrange("p (c x) -> p c x", c=NP)
                for j, (rows, block) in enumerate(diagonals(n_z, GRID)):
                    inv = n_small[rows, N_INV, :].unsqueeze(2).to_broadcast([GRID, NP, GRID])
                    ins = nc.vector.tensor_tensor(block, out[rows, :, GRID * j:GRID * j + GRID], inv, ALU.mult)
                ins.then_inc(at["z"], 1)
                dve.wait_ge(at["z"], r + 1)
                for rows, block in diagonals(n_z, GRID):
                    ins = nc.vector.tensor_tensor(n_zsq[rows, :, :], block, block, ALU.mult)
                ins.then_inc(at["sq"], 1)
                dve.wait_ge(at["sq"], r + 1)
                nc.vector.tensor_reduce(n_small[:, N_SS, :], n_zsq[:, :, :], AX.X, ALU.add).then_inc(at["ss"], 1)
                dve.wait_ge(at["r"], r + 1)
                for rows, block in diagonals(n_z, GRID):
                    inv = n_small[rows, N_R, :].unsqueeze(2).to_broadcast([GRID, NP, GRID])
                    ins = nc.vector.tensor_tensor(block, block, inv, ALU.mult)
                ins.then_inc(at["zs"], 1)

            na_rows(dve, row)

        HQ, KV, GQ, HD, WIN = 8, 2, 4, 64, 128
        sop = Region(arena, ops_end)
        s_q = sop.take("s_q", [P, GQ, T])
        s_k = sop.take("s_k", [P, WIN + T])
        s_v = sop.take("s_v", [P, TC + 1, P])
        s_bias = [sop.take(f"s_bias{j}", [P, HQ, 2 * WIN]) for j in range(2)]
        s_zq = sop.take("s_zq", [P, GQ, KV, P])
        s_s = sop.take("s_s", [P, HQ, 2 * WIN])
        s_pt = [sop.take(f"s_pt{j}", [P, 4, P]) for j in range(2)]
        s_a = sop.take("s_a", [P, HQ, HD])
        s_small = sop.take("s_small", [P, 12, HQ])
        S_MAX, S_NEG, S_SUM, S_SINK, S_INV, S_SS, S_LN, S_R, S_M = range(9)
        swk = Region(ops_end, ops_end + 4 * T * 4)
        s_qsq = [swk.take(f"s_qsq{j}", [P, T]) for j in range(2)]
        s_qrs = [swk.take(f"s_qrs{j}", [P, T]) for j in range(2)]
        cwk = Region(mix_end, end)
        s_mask = Region(mix_end, end).take("s_mask", [P, 2, 2 * WIN])
        s_vT = Region(mix_end + 2048, end).take("s_vT", [P, T])
        s_t5 = Region(mix_end + 2048 + 4 * T, end).take("s_t5", [32, 384])
        s_rel = Region(mix_end + 2048 + 4 * T + 1536, end).take("s_rel", [32, HQ])
        s_rows = Region(mix_end + 2048 + 4 * T + 1536 + 32, end).take("s_rows", [HQ, 384])

        a0 = {name: 0 for name in at_names}
        a0.update({"load": 48, "prep": ROWS - 1, "prepc": ROWS - 1, "bias": 16 * (NH1 + 2) + 1, "end": ROWS + 1})
        a0.update({name: ROWS for name in ["zq", "max", "neg", "rs", "z", "sq", "ss", "ln", "r", "zs", "o"]})
        a0.update({name: NP * ROWS for name in ["s", "sc", "p", "pt", "ptc", "av"]})
        sq_sq, sq_sum, sq_ln, sq_rs, sq_done = (sem(f"sq_{name}") for name in ["sq", "sum", "ln", "rs", "done"])
        s_pads = sem("s_pads")
        s_rowed = sem("s_rowed")
        NQK = GQ + 1

        def swa_sp(sp):
            proj_stored(sp, proj2)
            layer_read(sp, proj2)
            h2 = g["h2"]
            sp.dma_start(s_t5[:, :], g["t5"]).then_inc(at["load"], 16)
            sp.dma_start(s_rel[:, :], g["rel_bias"]).then_inc(at["load"], 16)
            for v in range(KV):
                sp.dma_start(s_q[HD * v:HD * v + HD, :, :],
                             h2[v * GQ * HD:(v + 1) * GQ * HD, :].rearrange("(g p) t -> p g t", p=HD)).then_inc(at["load"], 16)
            sp.dma_start(s_k[:, WIN:WIN + T], h2[HQ * HD:HQ * HD + P, :]).then_inc(at["load"], 16)
            sp.dma_start(s_vT[:, :], h2[HQ * HD + P:HQ * HD + 2 * P, :]).then_inc(at["load"], 16)
            sp.dma_start(s_mask[:, :, :], g["swa_mask"]).then_inc(at["load"], 16)
            sp.wait_ge(s_rowed, 2)
            sp.dma_start(g["t5_rows"], s_rows[:, :].unsqueeze(1).to_broadcast([HQ, P, 384])).then_inc(s_rowed, 16)
            sp.wait_ge(s_rowed, 18)
            for j in range(2):
                src = bass.AP(g["t5_rows"].tensor, g["t5_rows"].offset + P - 1, [[384 - 1, P], [P * 384, HQ], [1, 2 * WIN]])
                sp.dma_start(s_bias[j][:, :, :], src).then_inc(at["bias"], 16)

        def swa_prep_pe(pe):
            pe.wait_ge(at["load"], a0["load"] + 112)
            nc.tensor.matmul(ps[0:HQ, 7, 0:384], s_rel[:, :], s_t5[:, :], start=True, stop=True).then_inc(s_rowed, 1)
            for c in range(TC):
                last = nc.tensor.transpose(banks(4)[:, c * P:(c + 1) * P], s_vT[:, c * P:(c + 1) * P], const("ident"))
            last.then_inc(at["prep"], 1)
            for j in range(NQK):
                pe.wait_ge(sq_sq, j + 1)
                if j >= 2:
                    pe.wait_ge(sq_ln, j - 1)
                for b in range(2):
                    last = nc.tensor.matmul(ps[:, 2 * (j % 2) + b, :], const("ones_half"), s_qsq[j % 2][:, b * HALF:(b + 1) * HALF],
                                            start=True, stop=True)
                last.then_inc(sq_sum, 1)

        def swa_x(j):
            return s_q[:, j, :] if j < GQ else s_k[:, WIN:WIN + T]

        def swa_prep_act(act):
            act.wait_ge(at["load"], a0["load"] + 112)
            act.wait_ge(s_rowed, 1)
            nc.scalar.activation(s_rows[:, :], ps[0:HQ, 7, 0:384], ACT.Copy).then_inc(s_rowed, 1)
            act.wait_ge(at["prep"], a0["prep"] + 1)
            nc.scalar.activation(s_v[:, 1:TC + 1, :].rearrange("p c x -> p (c x)"), banks(4), ACT.Copy).then_inc(at["prepc"], 1)
            for j in range(NQK):
                if j >= 2:
                    act.wait_ge(sq_sum, j - 1)
                nc.scalar.activation(s_qsq[j % 2][:, :], swa_x(j), ACT.Square).then_inc(sq_sq, 1)
                act.wait_ge(sq_sum, j + 1)
                if j >= 2:
                    act.wait_ge(sq_done, j - 1)
                nc.scalar.activation(s_qrs[j % 2][:, :], banks(2 * (j % 2)), ACT.Ln, bias=param("eps6"), scale=1.0 / HD)\
                    .then_inc(sq_ln, 1)
                act.wait_ge(sq_ln, j + 1)
                nc.scalar.activation(s_qrs[j % 2][:, :], s_qrs[j % 2][:, :], ACT.Exp, scale=-0.5).then_inc(sq_rs, 1)

        def swa_prep_dve(dve):
            proj_stored(dve, proj2)
            layer_read(dve, proj2)
            nc.vector.memset(s_k[:, 0:WIN], 0.0)
            nc.vector.memset(s_v[:, 0, :], 0.0)
            nc.vector.memset(s_zq[:, :, :, :], 0.0).then_inc(s_pads, 1)
            for j in range(NQK):
                dve.wait_ge(sq_rs, j + 1)
                nc.vector.scalar_tensor_tensor(swa_x(j), swa_x(j), param("q_g" if j < GQ else "k_g"), s_qrs[j % 2][:, :],
                                               op0=ALU.mult, op1=ALU.mult).then_inc(sq_done, 1)
            dve.wait_ge(at["bias"], a0["bias"] + 16 * 2)
            dve.wait_ge(at["load"], a0["load"] + 112)
            for j in range(2):
                nc.vector.tensor_tensor(s_bias[j][:, :, :], s_bias[j][:, :, :],
                                        s_mask[:, j, :].unsqueeze(1).to_broadcast([P, HQ, 2 * WIN]), ALU.add).then_inc(at["bias"], 1)
            dve.wait_ge(at["bias"], a0["bias"] + 16 * 2 + 2)

        def swa_blocks(eng, block):
            block(0, True)
            with eng.Fori(1, TC) as n:
                block(n, False)

        def att(name, n, per=1, j=0):
            return per * n + (a0[name] + j + 1)

        def swa_pe(pe):
            pe.wait_ge(sq_done, NQK)
            pe.wait_ge(at["prepc"], a0["prepc"] + 1)

            def block(n, first):
                pe.wait_ge(at["zq"], att("zq", n))
                for h in range(HQ):
                    last = nc.tensor.matmul(ps[:, h // 2, (h % 2) * 256:(h % 2) * 256 + 256], s_zq[:, h % GQ, h // GQ, :],
                                            s_k[:, bass.ds(n * P, 2 * WIN)], start=True, stop=True)
                    if h % 2:
                        last.then_inc(at["s"], 1)

                def turn(c):
                    pe.wait_ge(at["p"], att("p", n, HQ, 2 * c + 1))
                    if c >= 2:
                        pe.wait_ge(at["ptc"], att("ptc", n, 4, c - 2))
                    for j in range(4):
                        last = nc.tensor.transpose(ps[:, 4 + c % 2, j * P:(j + 1) * P],
                                                   s_s[:, 2 * c + j // 2, (j % 2) * P:(j % 2) * P + P], const("ident"))
                    last.then_inc(at["pt"], 1)

                def weigh(c):
                    pe.wait_ge(at["ptc"], att("ptc", n, 4, c))
                    for j in range(4):
                        h = 2 * c + j // 2
                        v = s_v[:, bass.ds(n + j % 2, 1), (h // GQ) * HD:(h // GQ + 1) * HD].rearrange("p o x -> p (o x)")
                        last = nc.tensor.matmul(ps[:, 6, h * HD:(h + 1) * HD], s_pt[c % 2][:, j, :], v,
                                                start=(j % 2 == 0), stop=(j % 2 == 1))
                    last.then_inc(at["av"], 1)

                turn(0)
                turn(1)
                for c in range(4):
                    weigh(c)
                    if c + 2 < 4:
                        turn(c + 2)
                pe.wait_ge(at["zs"], att("zs", n))
                for c in range(4):
                    last = nc.tensor.transpose(ps[:, 7, c * P:(c + 1) * P],
                                               s_a[:, 2 * c:2 * c + 2, :].rearrange("p h x -> p (h x)"), const("ident"))
                last.then_inc(at["o"], 1)

            swa_blocks(pe, block)

        def swa_act(act):
            act.wait_ge(s_pads, 1)
            act.wait_ge(sq_done, NQK)

            def block(n, first):
                for v in range(KV):
                    ins = nc.scalar.activation(s_zq[HD * v:HD * v + HD, :, v, :], s_q[HD * v:HD * v + HD, :, bass.ds(n * P, P)], ACT.Copy)
                ins.then_inc(at["zq"], 1)
                act.wait_ge(at["neg"], att("neg", n, 2, 1))
                for h in range(HQ):
                    nc.scalar.activation(s_s[:, h, :], s_s[:, h, :], ACT.Exp, bias=s_small[:, S_NEG, h:h + 1],
                                         accum_out=s_small[:, S_SUM, h:h + 1]).then_inc(at["p"], 1)
                nc.scalar.activation(s_small[:, S_SINK, :], s_small[:, S_SINK, :], ACT.Exp).then_inc(at["sq"], 1)
                for c in range(4):
                    act.wait_ge(at["pt"], att("pt", n, 4, c))
                    if c >= 2:
                        act.wait_ge(at["av"], att("av", n, 4, c - 2))
                    nc.scalar.activation(s_pt[c % 2][:, :, :].rearrange("p t x -> p (t x)"), ps[:, 4 + c % 2, :], ACT.Copy)\
                        .then_inc(at["ptc"], 1)
                act.wait_ge(at["ss"], att("ss", n))
                nc.scalar.activation(s_small[:, S_LN, 0:1], s_small[:, S_SS, 0:1], ACT.Ln, bias=param("eps6"), scale=1.0 / (HQ * HD))\
                    .then_inc(at["ln"], 1)
                act.wait_ge(at["ln"], att("ln", n))
                nc.scalar.activation(s_small[:, S_R, 0:1], s_small[:, S_LN, 0:1], ACT.Exp, scale=-0.5).then_inc(at["r"], 1)

            swa_blocks(act, block)

        def swa_dve(dve):
            sinks = param("sinks", 0, HQ)

            def block(n, first):
                for c in range(4):
                    dve.wait_ge(at["s"], att("s", n, 4, c))
                    nc.vector.scalar_tensor_tensor(
                        s_s[:, 2 * c:2 * c + 2, :], ps[:, c, :].rearrange("p (h x) -> p h x", h=2), float(HD) ** -0.5,
                        s_bias[0 if first else 1][:, 2 * c:2 * c + 2, :], op0=ALU.mult, op1=ALU.add).then_inc(at["sc"], 1)
                dve.wait_ge(at["sc"], att("sc", n, 4, 3))
                nc.vector.tensor_reduce(s_small[:, S_M, :], s_s[:, :, :], AX.X, ALU.max).then_inc(at["max"], 1)
                dve.wait_ge(at["max"], att("max", n, 2, 0))
                nc.vector.tensor_tensor(s_small[:, S_MAX, :], s_small[:, S_M, :], sinks, ALU.max).then_inc(at["max"], 1)
                dve.wait_ge(at["max"], att("max", n, 2, 1))
                nc.vector.tensor_tensor(s_small[:, S_SINK, :], sinks, s_small[:, S_MAX, :], ALU.subtract).then_inc(at["neg"], 1)
                nc.vector.tensor_scalar(s_small[:, S_NEG, :], s_small[:, S_MAX, :], -1.0, None, ALU.mult).then_inc(at["neg"], 1)
                dve.wait_ge(at["sq"], att("sq", n))
                nc.vector.tensor_tensor(s_small[:, S_INV, :], s_small[:, S_SUM, :], s_small[:, S_SINK, :], ALU.add).then_inc(at["rs"], 1)
                dve.wait_ge(at["rs"], att("rs", n, 2, 0))
                nc.vector.reciprocal(s_small[:, S_INV, :], s_small[:, S_INV, :]).then_inc(at["rs"], 1)
                dve.wait_ge(at["rs"], att("rs", n, 2, 1))
                dve.wait_ge(at["av"], att("av", n, 4, 3))
                nc.vector.tensor_tensor(s_a[:, :, :], ps[:, 6, :].rearrange("p (h x) -> p h x", h=HQ),
                                        s_small[:, S_INV, :].unsqueeze(2).to_broadcast([P, HQ, HD]), ALU.mult).then_inc(at["z"], 1)
                dve.wait_ge(at["z"], att("z", n, 2, 0))
                flat = s_a[:, :, :].rearrange("p h x -> p (h x)")
                nc.vector.tensor_tensor_reduce(s_sqa[:, :], flat, flat, 1.0, 0.0, ALU.mult, ALU.add, s_small[:, S_SS, 0:1])\
                    .then_inc(at["ss"], 1)
                dve.wait_ge(at["r"], att("r", n))
                nc.vector.tensor_scalar(flat, flat, s_small[:, S_R, 0:1], None, ALU.mult).then_inc(at["zs"], 1)
                dve.wait_ge(at["o"], att("o", n))
                nc.vector.tensor_tensor(mixT[:, 0:4, bass.ds(n * P, P)], ps[:, 7, :].rearrange("p (c x) -> p c x", c=4),
                                        param("attn_g", 0, 4).unsqueeze(2).to_broadcast([P, 4, P]), ALU.mult).then_inc(at["z"], 1)

            swa_blocks(dve, block)

        CK, CC = 31, 4
        CW = 4 * P
        c_pad = [cwk.take(f"c_pad{j}", [P, CK - 1 + T]) for j in range(CC)]
        c_gate = [cwk.take(f"c_gate{j}", [P, T]) for j in range(CC)]
        s_sqa = cwk.take("s_sqa", [P, HQ * HD])
        c_rs = cwk.take("c_rs", [P, T])
        c_load, c_sig, c_tap, c_conv, c_sum, c_cen, c_sq, c_sqs, c_ln, c_rstd, c_norm, c_silu, c_end = (
            sem(f"c_{name}") for name in ["load", "sig", "tap", "conv", "sum", "cen", "sq", "sqs", "ln", "rstd", "norm", "silu", "end"])
        c_sqt = c_gate[0:2]

        def conv_sp(sp):
            sp.wait_ge(at["bias"], a0["bias"] + 16 * 2 + 2)
            sp.wait_ge(sq_done, NQK)
            for j in range(CC):
                row = HQ * HD + 2 * P + j * P
                sp.dma_start(c_pad[j][:, CK - 1:], g["h2"][row:row + P, :]).then_inc(c_load, 16)
                sp.dma_start(c_gate[j][:, :], g["h2"][row + CW:row + CW + P, :]).then_inc(c_load, 16)

        def conv_act(act):
            act.wait_ge(c_load, 32 * CC)
            for j in range(CC):
                nc.scalar.activation(c_gate[j][:, :], c_gate[j][:, :], ACT.Sigmoid).then_inc(c_sig, 1)

        def conv_dve(dve):
            for j in range(CC):
                nc.vector.memset(c_pad[j][:, 0:CK - 1], 0.0)
            for j in range(CC):
                dve.wait_ge(c_sig, j + 1)
                nc.vector.tensor_tensor(c_pad[j][:, CK - 1:], c_pad[j][:, CK - 1:], c_gate[j][:, :], ALU.mult).then_inc(c_conv, 1)
            n = 0
            for tap in range(CK):
                for j in range(CC):
                    y, src, w = mixT[:, CC + j, :], c_pad[j][:, tap:tap + T], param("conv_w_2", j * CK + tap)
                    if tap == 0:
                        dve.wait_ge(c_conv, j + 1)
                        nc.vector.tensor_scalar(y, src, w, param("conv_b_2", j), ALU.mult, ALU.add).then_inc(c_tap, 1)
                    else:
                        dve.wait_ge(c_tap, CC * (tap - 1) + j + 1)
                        nc.vector.scalar_tensor_tensor(y, src, w, y, op0=ALU.mult, op1=ALU.add).then_inc(c_tap, 1)

        def conv_norm_pe(pe):
            pe.wait_ge(at["z"], a0["z"] + 2 * TC)
            pe.wait_ge(c_tap, CK * CC)
            for j in range(CC):
                for b in range(2):
                    last = nc.tensor.matmul(ps[:, b, :], const("ones"), mixT[:, CC + j, b * HALF:(b + 1) * HALF],
                                            start=(j == 0), stop=(j == CC - 1))
            last.then_inc(c_sum, 1)
            for i in range(2):
                for j in range(CC):
                    pe.wait_ge(c_sq, CC * i + j + 1)
                    for b in range(2):
                        last = nc.tensor.matmul(ps[:, 2 + 2 * i + b, :], const("ones"), c_sqt[j % 2][:, b * HALF:(b + 1) * HALF],
                                                start=(j == 0), stop=(j == CC - 1))
                    last.then_inc(c_sqs, 1)

        def conv_norm_act(act):
            for i in range(2):
                for j in range(CC):
                    act.wait_ge(c_cen if i == 0 else c_silu, j + 1)
                    if CC * i + j >= 2:
                        act.wait_ge(c_sqs, CC * i + j - 1)
                    nc.scalar.activation(c_sqt[j % 2][:, :], mixT[:, CC + j, :], ACT.Square).then_inc(c_sq, 1)
                act.wait_ge(c_sqs, CC * i + CC)
                nc.scalar.activation(c_rs[:, :], banks(2 + 2 * i), ACT.Ln, bias=param("eps6"), scale=1.0 / CW).then_inc(c_ln, 1)
                act.wait_ge(c_ln, i + 1)
                nc.scalar.activation(c_rs[:, :], c_rs[:, :], ACT.Exp, scale=-0.5).then_inc(c_rstd, 1)
                if i == 0:
                    for j in range(CC):
                        act.wait_ge(c_norm, j + 1)
                        nc.scalar.activation(mixT[:, CC + j, :], mixT[:, CC + j, :], ACT.Silu, bias=param("cln_b", j)).then_inc(c_silu, 1)

        def conv_norm_dve(dve):
            dve.wait_ge(c_sum, 1)
            for j in range(CC):
                y = mixT[:, CC + j, :]
                nc.vector.scalar_tensor_tensor(y, banks(0), -1.0 / CW, y, op0=ALU.mult, op1=ALU.add).then_inc(c_cen, 1)
            for i in range(2):
                dve.wait_ge(c_rstd, i + 1)
                for j in range(CC):
                    y = mixT[:, CC + j, :]
                    nc.vector.scalar_tensor_tensor(y, y, param("cln_g" if i == 0 else "cout_g", j), c_rs[:, :],
                                                   op0=ALU.mult, op1=ALU.mult).then_inc(c_norm if i == 0 else c_end, 1)

        LP, LK, LV = 2, 64, P
        GATE = 1.0 / 16.0
        LQ0, LK0, LV0, LG0, LR0 = 0, 256, 512, 1024, 1536
        LC0 = (1552, 2064, 2576)
        LL = 7
        lop = Region(arena, ops_end)
        l_q = lop.take("l_q", [P, LP, T])
        l_k = lop.take("l_k", [P, LP, TM])
        l_vt = lop.take("l_vt", [P, TC, GH * LV])
        l_g = lop.take("l_g", [P, GH, T])
        l_b = lop.take("l_b", [P, LP, TM])
        l_gr = lop.take("l_gr", [16, TM])
        l_wg = lop.take("l_wg", [16, LP * P])
        l_vm = lop.take("l_vm", [META, GH * LV])
        lwk = Region(mix_end, end)
        l_mask = lwk.take("l_mask", [P, LL + 1, P], I32)
        l_run = lwk.take("l_run", [P, TM])
        l_v = Region(lwk.at, end).take("l_v", [P, GH, TM])
        l_e = [lwk.take(f"l_e{j}", [P, LP, P]) for j in range(2)]
        l_ql = [lwk.take(f"l_ql{j}", [P, LP, P]) for j in range(2)]
        l_kl = [lwk.take(f"l_kl{j}", [P, LP, P]) for j in range(2)]
        l_A = lwk.take("l_A", [P, GH, P])
        l_eb, l_qd, l_ke, l_S = (lwk.take(f"l_{name}", [P, LP, P]) for name in ["eb", "qd", "ke", "S"])
        l_kc = lwk.take("l_kc", [P, LP, P])
        l_ket = lwk.take("l_ket", [P, LP, P])
        l_o = lwk.take("l_o", [P, GH, LV])
        l_osq = lwk.take("l_osq", [P, GH, LV])
        l_small = lwk.take("l_small", [P, 8, GH])
        L_LAST, L_SS, L_LN, L_R, L_WAIT = range(5)
        l_t = lwk.take("l_t", [P, LP, TM])
        l_a = lwk.take("l_a", [P, LP, TM])
        kwk = Region(lwk.at - 2 * LP * TM * 4, end)
        k_c = [kwk.take(f"k_c{j}", [P, TM]) for j in range(2)]
        k_x = [kwk.take(f"k_x{j}", [P, TM]) for j in range(2)]
        k_b = kwk.take("k_b", [P, T])
        (l_load, l_tr, l_trc, l_gate, l_scan, l_meta, l_diff, l_exp, l_lq, l_lk, l_lA, l_pred, l_dec, l_qdd, l_ked, l_ket_, l_ketc,
         l_out, l_osc, l_sum, l_ln, l_r, l_turn, l_su, l_kcd, l_end) = (
            sem(f"l_{name}") for name in [
                "load", "tr", "trc", "gate", "scan", "meta", "diff", "exp", "lq", "lk", "lA", "pred", "dec", "qd", "ke", "ket",
                "ketc", "out", "osc", "sum", "ln", "r", "turn", "su", "kcd", "end"])

        def gla_sp(sp):
            proj_stored(sp, proj3)
            layer_read(sp, proj3)
            h3 = g["h3"]

            def rows(first, chunks, t0=0):
                return h3[first:first + chunks * P, t0:].rearrange("(c p) t -> p c t", p=P)

            sp.dma_start(l_gr[:, :], h3[LR0:LR0 + 16, :]).then_inc(l_load, 16)
            sp.dma_start(l_wg[:, :], g["w_gate"]).then_inc(l_load, 16)
            sp.dma_start(l_v[:, :, :], rows(LV0, GH)).then_inc(l_load, 16)
            sp.dma_start(l_k[:, :, :], rows(LK0, LP)).then_inc(l_load, 16)
            sp.dma_start(l_q[:, :, :], rows(LQ0, LP, META)).then_inc(l_load, 16)
            sp.dma_start(l_g[:, :, :], rows(LG0, GH, META)).then_inc(l_load, 16)
            sp.dma_start(l_mask[:, :, :], g["gla_consts"]).then_inc(l_load, 16)

        def gla_prep_pe(pe):
            pe.wait_ge(l_load, 112)
            for j in range(LP):
                for b, (t0, t1) in enumerate([(META, META + HALF), (META + HALF, TM), (0, META)]):
                    last = nc.tensor.matmul(ps[:, 3 * j + b, 0:t1 - t0], l_wg[:, j * P:(j + 1) * P], l_gr[:, t0:t1],
                                            start=True, stop=True)
            last.then_inc(l_gate, 1)
            for c in range(TC):
                if c >= 2:
                    pe.wait_ge(l_trc, c - 1)
                for h in range(GH):
                    last = nc.tensor.transpose(ps[:, 6 + c % 2, h * P:(h + 1) * P], l_v[:, h, META + c * P:META + (c + 1) * P],
                                               const("ident"))
                last.then_inc(l_tr, 1)
            pe.wait_ge(l_trc, TC)
            for h in range(GH):
                last = nc.tensor.transpose(ps[0:META, 6, h * P:(h + 1) * P], l_v[:, h, 0:META], const("ident"))
            last.then_inc(l_tr, 1)
            pe.wait_ge(l_meta, 3)
            for j in range(LP):
                last = nc.tensor.transpose(ps[0:META, 7, j * P:(j + 1) * P], l_ke[:, j, 0:META], const("ident"))
            last.then_inc(l_meta, 1)
            pe.wait_ge(l_meta, 5)
            pe.wait_ge(l_trc, TC + 1)
            for j in range(LP):
                last = nc.tensor.matmul(ps[:, 0, j * 256:(j + 1) * 256], l_ket[0:META, j, :], l_vm[:, j * 256:(j + 1) * 256],
                                        start=True, stop=True)
            last.then_inc(l_meta, 1)

        def gla_prep_act(act):
            act.wait_ge(l_load, 112)
            act.wait_ge(l_gate, 1)
            for j in range(LP):
                nc.scalar.activation(l_t[:, j, META:TM], banks(3 * j), ACT.Identity, bias=param("b_gate", j))
                nc.scalar.activation(l_t[:, j, 0:META], ps[:, 3 * j + 2, 0:META], ACT.Identity, bias=param("b_gate", j)).then_inc(l_gate, 1)
            for c in range(TC):
                act.wait_ge(l_tr, c + 1)
                nc.scalar.activation(l_vt[:, c, :], ps[:, 6 + c % 2, :], ACT.Copy).then_inc(l_trc, 1)
            act.wait_ge(l_tr, TC + 1)
            nc.scalar.activation(l_vm[:, :], ps[0:META, 6, :], ACT.Copy).then_inc(l_trc, 1)
            act.wait_ge(l_gate, 4)
            nc.scalar.activation(l_a[:, :, :], l_a[:, :, :], ACT.Exp).then_inc(l_gate, 1)
            act.wait_ge(l_gate, 5)
            nc.scalar.activation(l_a[:, :, :], l_a[:, :, :], ACT.Ln, bias=param("one")).then_inc(l_gate, 1)
            for h in range(GH):
                nc.scalar.activation(l_g[:, h, :], l_g[:, h, :], ACT.Silu)
            act.wait_ge(l_meta, 1)
            nc.scalar.activation(l_ke[:, :, 0:META], l_ke[:, :, 0:META], ACT.Exp, scale=GATE).then_inc(l_meta, 1)
            act.wait_ge(l_meta, 4)
            nc.scalar.activation(l_ket[0:META, :, :].rearrange("p j x -> p (j x)"), ps[0:META, 7, 0:LP * P], ACT.Copy).then_inc(l_meta, 1)

        def gla_prep_dve(dve):
            proj_stored(dve, proj3)
            layer_read(dve, proj3)
            nc.vector.memset(l_run[:, :], 1.0).then_inc(l_scan, 1)
            dve.wait_ge(l_scan, 1)
            nc.vector.memset(l_run[:, 0:1], 0.0)
            nc.vector.memset(l_run[:, META:TM].rearrange("p (c x) -> p c x", x=P)[:, :, 0:1], 0.0).then_inc(l_scan, 1)
            dve.wait_ge(l_gate, 3)
            nc.vector.scalar_tensor_tensor(l_a[:, :, :], l_t[:, :, :], -1.0, l_t[:, :, :], op0=ALU.mult, op1=ALU.min).then_inc(l_gate, 1)
            dve.wait_ge(l_gate, 6)
            nc.vector.scalar_tensor_tensor(l_t[:, :, :], l_t[:, :, :], 0.0, l_a[:, :, :], op0=ALU.min, op1=ALU.subtract).then_inc(l_gate, 1)
            dve.wait_ge(l_gate, 7)
            dve.wait_ge(l_scan, 2)
            for j in range(LP):
                nc.vector.tensor_tensor_scan(l_b[:, j, :], l_run[:, :], l_t[:, j, :], 0.0, ALU.mult, ALU.add).then_inc(l_scan, 1)
            dve.wait_ge(l_scan, 4)
            dve.wait_ge(l_trc, TC + 1)
            nc.vector.tensor_tensor(l_ke[:, :, 0:META], l_b[:, :, META - 1:META].to_broadcast([P, LP, META]), l_b[:, :, 0:META],
                                    ALU.subtract).then_inc(l_meta, 1)
            dve.wait_ge(l_meta, 2)
            nc.vector.tensor_tensor(l_ke[:, :, 0:META], l_ke[:, :, 0:META], l_k[:, :, 0:META], ALU.mult).then_inc(l_meta, 1)
            dve.wait_ge(l_meta, 6)
            for j in range(LP):
                for i in range(2):
                    rows = slice(LK * i, LK * i + LK)
                    nc.vector.tensor_copy(l_S[rows, j, :], ps[rows, 0, j * 256 + i * LV:j * 256 + (i + 1) * LV])
            nc.vector.memset(l_A[:, :, :], 0.0).then_inc(l_end, 1)

        def each(n, per=1, j=0):
            return per * n + (j + 1)

        def l_chunk(t, n, first=0):
            return t[:, :, bass.ds(n * P + first, P)]

        def head_bank(b, h):
            return ps[:, b + h % 2, (h // 2) * P:(h // 2 + 1) * P]

        def two_banks(b):
            return ps[:, b:b + 2, 0:LP * P].rearrange("p i (j x) -> p i j x", j=LP)

        def by_bank(t):
            return t[:, :, :].rearrange("p (j i) x -> p i j x", i=2)

        def gla_pe(pe):
            pe.wait_ge(l_end, 1)
            with pe.Fori(0, TC) as n:
                for l in range(LL + 1):
                    pe.wait_ge(l_lq, each(n, LL + 1, l))
                    if l < LL:
                        pe.wait_ge(l_lk, each(n, LL, l))
                    else:
                        pe.wait_ge(l_kcd, each(n))
                    keys = l_kl[l % 2] if l < LL else l_kc
                    if l >= 2:
                        pe.wait_ge(l_pred, each(n, LL + 1, l - 2))
                    for h in range(GH):
                        rows = slice(LK * (h % 2), LK * (h % 2) + LK)
                        last = nc.tensor.matmul(head_bank(2 * (l % 2), h), keys[rows, h // 2, :], l_ql[l % 2][rows, h // 2, :],
                                                start=True, stop=True)
                    last.then_inc(l_lA, 1)
                pe.wait_ge(l_ked, each(n))
                for j in range(LP):
                    last = nc.tensor.transpose(ps[:, 6, j * P:(j + 1) * P], l_ke[:, j, :], const("ident"))
                last.then_inc(l_ket_, 1)
                pe.wait_ge(l_pred, each(n, LL + 1, LL))
                pe.wait_ge(l_qdd, each(n))
                pe.wait_ge(l_end, each(n))
                for h in range(GH):
                    rows = slice(LK * (h % 2), LK * (h % 2) + LK)
                    v = l_vt[:, bass.ds(n, 1), h * LV:(h + 1) * LV].rearrange("p o x -> p (o x)")
                    nc.tensor.matmul(head_bank(4, h), l_A[:, h, :], v, start=True, stop=False)
                    last = nc.tensor.matmul(head_bank(4, h), l_qd[rows, h // 2, :], l_S[rows, h // 2, :],
                                            start=False, stop=True)
                last.then_inc(l_out, 1)
                pe.wait_ge(l_ketc, each(n))
                for j in range(LP):
                    v = l_vt[:, bass.ds(n, 1), j * 256:(j + 1) * 256].rearrange("p o x -> p (o x)")
                    last = nc.tensor.matmul(ps[:, 7, j * 256:(j + 1) * 256], l_ket[:, j, :], v, start=True, stop=True)
                last.then_inc(l_su, 1)
                pe.wait_ge(l_osc, each(n, 2, 1))
                for h in range(GH):
                    last = nc.tensor.transpose(ps[:, 6, h * P:(h + 1) * P], l_o[:, h, :], const("ident"))
                last.then_inc(l_turn, 1)

        def gla_act(act):
            act.wait_ge(l_end, 1)
            with act.Fori(0, TC) as n:
                b = l_chunk(l_b, n, META)
                act.wait_ge(l_end, each(n))
                nc.scalar.activation(l_eb[:, :, :], b, ACT.Exp, scale=GATE).then_inc(l_dec, 1)
                nc.scalar.activation(l_small[:, L_LAST, 0:LP].unsqueeze(2), l_b[:, :, bass.ds(n * P + (META + P - 1), 1)], ACT.Exp,
                                     scale=GATE).then_inc(l_dec, 1)
                act.wait_ge(l_diff, each(n, 2 * LL + 1, 0))
                nc.scalar.activation(l_ke[:, :, :], l_ke[:, :, :], ACT.Exp, scale=GATE).then_inc(l_dec, 1)
                for l in range(LL):
                    act.wait_ge(l_diff, each(n, 2 * LL + 1, 2 * l + 2))
                    nc.scalar.activation(l_e[l % 2][:, :, :], l_e[l % 2][:, :, :], ACT.Exp, scale=GATE).then_inc(l_exp, 1)
                act.wait_ge(l_ket_, each(n))
                nc.scalar.activation(l_ket[:, :, :].rearrange("p j x -> p (j x)"), ps[:, 6, 0:LP * P], ACT.Copy).then_inc(l_ketc, 1)
                act.wait_ge(l_sum, each(n, 2, 1))
                nc.scalar.activation(l_small[:, L_LN, :], l_small[:, L_SS, :], ACT.Ln, bias=param("eps6"), scale=1.0 / LV).then_inc(l_ln, 1)
                act.wait_ge(l_ln, each(n))
                nc.scalar.activation(l_small[:, L_R, :], l_small[:, L_LN, :], ACT.Exp, scale=-0.5).then_inc(l_r, 1)

        def gla_pool(pool):
            pool.wait_ge(l_end, 1)
            with pool.Fori(0, TC) as n:
                pool.wait_ge(l_end, each(n))
                nc.gpsimd.tensor_copy(l_kc[:, :, :], l_chunk(l_k, n, META)).then_inc(l_kcd, 1)
                pool.wait_ge(l_kcd, each(n))
                pool.wait_ge(l_dec, each(n, 3, 2))
                nc.gpsimd.tensor_tensor(l_ke[:, :, :], l_ke[:, :, :], l_kc[:, :, :], ALU.mult).then_inc(l_ked, 1)
                for l in range(LL):
                    if l >= 2:
                        pool.wait_ge(l_lA, each(n, LL + 1, l - 2))
                    pool.wait_ge(l_exp, each(n, LL, l))
                    nc.gpsimd.tensor_tensor(l_kl[l % 2][:, :, :], l_e[l % 2][:, :, :], l_kc[:, :, :], ALU.mult).then_inc(l_lk, 1)

        def gla_dve(dve):
            scale = float(LK) ** -0.5
            dve.wait_ge(l_end, 1)
            with dve.Fori(0, TC) as n:
                q, b = l_chunk(l_q, n), l_chunk(l_b, n, META)
                tok = bass.ds(n * P, P)
                dve.wait_ge(l_end, each(n))
                b_end = l_b[:, :, bass.ds(n * P + (META + P - 1), 1)].to_broadcast([P, LP, P])
                nc.vector.tensor_tensor(l_ke[:, :, :], b_end, b, ALU.subtract).then_inc(l_diff, 1)
                dve.wait_ge(l_dec, each(n, 3, 0))
                nc.vector.scalar_tensor_tensor(l_qd[:, :, :], q, scale, l_eb[:, :, :], op0=ALU.mult, op1=ALU.mult).then_inc(l_qdd, 1)

                def away(l):
                    m = (P // 2) >> l
                    if l >= 2:
                        dve.wait_ge(l_lk, each(n, LL, l - 2))
                        dve.wait_ge(l_lq, each(n, LL + 1, l - 2))
                    e = l_e[l % 2]
                    for j in range(LP):
                        view = b[:, j, :].rearrange("p (n x) -> p n x", x=2 * m)
                        r = view[:, :, m - 1:m].to_broadcast([P, P // (2 * m), 2 * m])
                        ins = nc.vector.tensor_tensor(e[:, j, :].rearrange("p (n x) -> p n x", x=2 * m), view, r, ALU.subtract)
                    ins.then_inc(l_diff, 1)
                    dve.wait_ge(l_diff, each(n, 2 * LL + 1, 2 * l + 1))
                    nc.vector.scalar_tensor_tensor(e[:, :, :], e[:, :, :], -1.0, e[:, :, :], op0=ALU.mult, op1=ALU.min).then_inc(l_diff, 1)

                def queries(l):
                    if l >= 2:
                        dve.wait_ge(l_lA, each(n, LL + 1, l - 2))
                    if l < LL:
                        dve.wait_ge(l_exp, each(n, LL, l))
                        nc.vector.scalar_tensor_tensor(l_ql[l % 2][:, :, :], q, scale, l_e[l % 2][:, :, :], op0=ALU.mult, op1=ALU.mult)\
                            .then_inc(l_lq, 1)
                    else:
                        nc.vector.tensor_scalar(l_ql[l % 2][:, :, :], q, scale, None, ALU.mult).then_inc(l_lq, 1)

                def pick(l):
                    dve.wait_ge(l_lA, each(n, LL + 1, l))
                    if l:
                        dve.wait_ge(l_pred, each(n, LL + 1, l - 1))
                    nc.vector.memset(l_small[:, L_WAIT, 0:1], 0.0)
                    nc.vector.copy_predicated(by_bank(l_A), l_mask[:, l, :].unsqueeze(1).unsqueeze(1).to_broadcast([P, 2, LP, P]),
                                              two_banks(2 * (l % 2))).then_inc(l_pred, 1)

                for l in range(LL + 3):
                    if l < LL:
                        away(l)
                    if 1 <= l <= LL + 1:
                        queries(l - 1)
                    if l >= 2:
                        pick(l - 2)
                dve.wait_ge(l_out, each(n))
                nc.vector.tensor_copy(by_bank(l_o), two_banks(4)).then_inc(l_osc, 1)
                dve.wait_ge(l_osc, each(n, 2, 0))
                nc.vector.tensor_tensor(l_osq[:, :, :], l_o[:, :, :], l_o[:, :, :], ALU.mult).then_inc(l_sum, 1)
                dve.wait_ge(l_sum, each(n, 2, 0))
                nc.vector.tensor_reduce(l_small[:, L_SS, :], l_osq[:, :, :], AX.X, ALU.add).then_inc(l_sum, 1)
                dve.wait_ge(l_su, each(n))
                dve.wait_ge(l_dec, each(n, 3, 1))
                for j in range(LP):
                    for i in range(2):
                        rows = slice(LK * i, LK * i + LK)
                        nc.vector.scalar_tensor_tensor(l_S[rows, j, :], l_S[rows, j, :], l_small[rows, L_LAST, j:j + 1],
                                                       ps[rows, 7, j * 256 + i * LV:j * 256 + (i + 1) * LV], op0=ALU.mult, op1=ALU.add)
                dve.wait_ge(l_r, each(n))
                nc.vector.tensor_tensor(l_o[:, :, :], l_o[:, :, :], l_small[:, L_R, :].unsqueeze(2).to_broadcast([P, GH, LV]), ALU.mult)\
                    .then_inc(l_osc, 1)
                dve.wait_ge(l_turn, each(n))
                nc.vector.scalar_tensor_tensor(mixT[:, 0:GH, tok], ps[:, 6, :].rearrange("p (h x) -> p h x", h=GH), param("gla_g"),
                                               l_g[:, :, tok], op0=ALU.mult, op1=ALU.mult).then_inc(l_end, 1)

        SK = 3
        k_load, K_LOAD = (c_load, l_load), (32 * CC, 112)
        K_CONV, K_TAP, K_END = CC, CK * CC, CC

        def short_sp(sp):
            sp.wait_ge(l_scan, 4)
            for j in range(CC):
                def rows(i):
                    return g["h3"][LC0[i] + j * P:LC0[i] + (j + 1) * P, :]

                if j >= 2:
                    sp.wait_ge(c_tap, K_TAP + SK * (j - 1))
                sp.dma_start(k_c[j % 2][:, :], rows(1)).then_inc(k_load[j % 2], 16)
                sp.dma_start(k_x[j % 2][:, :], rows(2)).then_inc(k_load[j % 2], 16)
                if j >= 1:
                    sp.wait_ge(c_end, K_END + j)
                sp.dma_start(k_b[:, :], rows(0)[:, META:]).then_inc(k_load[j % 2], 16)

        def short_dve(dve):
            for j in range(CC):
                y = mixT[:, CC + j, :]
                dve.wait_ge(k_load[j % 2], K_LOAD[j % 2] + 48 * (j // 2 + 1))
                nc.vector.tensor_tensor(k_c[j % 2][:, :], k_c[j % 2][:, :], k_x[j % 2][:, :], ALU.mult).then_inc(c_conv, 1)
                dve.wait_ge(c_conv, K_CONV + j + 1)
                for tap in range(SK):
                    src, w = k_c[j % 2][:, META - SK + 1 + tap:META - SK + 1 + tap + T], param("conv_w_3", j * SK + tap)
                    if tap == 0:
                        ins = nc.vector.tensor_scalar(y, src, w, None, ALU.mult)
                    else:
                        dve.wait_ge(c_tap, K_TAP + SK * j + tap)
                        ins = nc.vector.scalar_tensor_tensor(y, src, w, y, op0=ALU.mult, op1=ALU.add)
                    ins.then_inc(c_tap, 1)
                dve.wait_ge(c_tap, K_TAP + SK * j + SK)
                nc.vector.tensor_tensor(y, y, k_b[:, :], ALU.mult).then_inc(c_end, 1)

        block = ctx.enter_context(nc.Block())

        @block.sync
        def _(sp):
            sp.dma_start(params[:, :], g["params"]).then_inc(loaded, 16)
            sp.dma_start(consts[:, :], g["consts"]).then_inc(loaded, 16)
            sp.dma_start(xT[:, :, :], g["x"]).then_inc(loaded, 16)
            first_pair_sp(sp, proj1)
            linear_sp(sp, proj1)
            na_bias_sp(sp)
            gdn_sp(sp)
            gdn_out_sp(sp)
            na_sp(sp)
            linear_sp(sp, out1)
            linear_sp(sp, mlp1)
            linear_sp(sp, proj2)
            swa_sp(sp)
            conv_sp(sp)
            linear_sp(sp, out2)
            linear_sp(sp, mlp2)
            layer_read(sp, mlp2)
            sp.dma_start(metaT[:, :, :], g["meta"]).then_inc(loaded, 16)
            linear_sp(sp, proj3)
            gla_sp(sp)
            short_sp(sp)
            linear_sp(sp, out3)
            linear_sp(sp, mlp3)
            for c in range(DC):
                sp.wait_ge(n_scaled, DC * rms_final.i + c + 1)
                sp.dma_start(g["out"][c], xT[:, c, :]).then_inc(loaded, 16)
            sp.wait_ge(loaded, 16 * (4 + DC))

        @block.tensor
        def _(pe):
            pe.wait_ge(loaded, 48)
            for s in range(2):
                nc.tensor.matmul(ps[:, 6 + s, 0:P], const("ones"), const("ones"), start=True, stop=True).then_inc(mm_done[s], 1)
            norm_pe(pe, ln_in)
            norm_split(pe, ln_in)
            proj_pe(pe, proj1)
            layer_read(pe, proj1)
            gdn_gates_pe(pe)
            gdn_prep_pe(pe)
            gdn_loop_pe(pe)
            gdn_out_pe(pe)
            na_pe(pe)
            out_pe(pe, out1, 0)
            layer_read(pe, out1)
            norm_pe(pe, ln1)
            norm_split(pe, ln1)
            mlp_pe(pe, mlp1)
            layer_read(pe, mlp1)
            norm_pe(pe, ln2)
            norm_pe(pe, rms_mix2)
            norm_split(pe, rms_mix2)
            proj_pe(pe, proj2)
            layer_read(pe, proj2)
            swa_prep_pe(pe)
            swa_pe(pe)
            conv_norm_pe(pe)
            out_pe(pe, out2, 1)
            layer_read(pe, out2)
            norm_pe(pe, rms_mlp2)
            norm_split(pe, rms_mlp2)
            mlp_pe(pe, mlp2)
            layer_read(pe, mlp2)
            norm_pe(pe, rms_meta)
            norm_pe(pe, rms_mix3)
            norm_split(pe, rms_mix3)
            proj_pe(pe, proj3)
            layer_read(pe, proj3)
            gla_prep_pe(pe)
            gla_pe(pe)
            out_pe(pe, out3, 2)
            layer_read(pe, out3)
            norm_pe(pe, rms_mlp3)
            norm_split(pe, rms_mlp3)
            mlp_pe(pe, mlp3)
            layer_read(pe, mlp3)
            norm_pe(pe, rms_final)

        @block.scalar
        def _(act):
            act.wait_ge(loaded, 48)
            for s in range(2):
                split_hi(act, s, 0)
            norm_act(act, ln_in)
            proj_act(act, proj1)
            gdn_gates_act(act)
            gdn_prep_act(act)
            gdn_loop_act(act)
            gdn_out_act(act)
            na_act(act)
            act.wait_ge(go_end, GH)
            act.wait_ge(at["end"], ROWS + 1)
            mix_split_act(act, 0)
            out_act(act, out1)
            layer_read(act, out1)
            norm_act(act, ln1)
            mlp_act(act, mlp1)
            layer_read(act, mlp1)
            norm_act(act, ln2)
            norm_shifted(act, ln2)
            norm_act(act, rms_mix2)
            proj_act(act, proj2)
            layer_read(act, proj2)
            swa_prep_act(act)
            swa_act(act)
            conv_act(act)
            conv_norm_act(act)
            act.wait_ge(c_end, CC)
            mix_split_act(act, 1)
            out_act(act, out2)
            layer_read(act, out2)
            norm_act(act, rms_mlp2)
            mlp_act(act, mlp2)
            layer_read(act, mlp2)
            act.wait_ge(loaded, 64)
            norm_act(act, rms_meta)
            norm_act(act, rms_mix3)
            proj_act(act, proj3)
            layer_read(act, proj3)
            gla_prep_act(act)
            gla_act(act)
            act.wait_ge(l_end, TC + 1)
            act.wait_ge(c_end, 2 * CC)
            mix_split_act(act, 2)
            out_act(act, out3)
            layer_read(act, out3)
            norm_act(act, rms_mlp3)
            mlp_act(act, mlp3)
            layer_read(act, mlp3)
            norm_act(act, rms_final)

        @block.vector
        def _(dve):
            for s in range(2):
                nc.vector.memset(tick[:, s:s + 1], 0.0).then_inc(w_split[s], 1)
                nc.vector.memset(tick[:, 2 + s:3 + s], 0.0).then_inc(ps_free[s], 1)
                nc.vector.memset(tick[:, 4 + s:5 + s], 0.0).then_inc(stored[s], 16)
            nc.vector.memset(tick[:, 6:7], 0.0).then_inc(hid_sq, 2)
            for s in range(2):
                split_lo(dve, s, 0)
            dve.wait_ge(loaded, 48)
            norm_dve(dve, ln_in)
            proj_dve(dve, proj1)
            layer_read(dve, proj1)
            proj_stored(dve, proj1)
            gdn_gates_dve(dve)
            gdn_prep_dve(dve)
            gdn_loop_dve(dve)
            gdn_out_dve(dve)
            na_dve(dve)
            mix_split_dve(dve, 0)
            out_dve(dve, out1)
            layer_read(dve, out1)
            norm_dve(dve, ln1)
            mlp_dve(dve, mlp1)
            layer_read(dve, mlp1)
            norm_dve(dve, ln2)
            norm_shifted(dve, ln2)
            norm_dve(dve, rms_mix2)
            proj_dve(dve, proj2)
            swa_prep_dve(dve)
            swa_dve(dve)
            conv_dve(dve)
            conv_norm_dve(dve)
            mix_split_dve(dve, 1)
            out_dve(dve, out2)
            layer_read(dve, out2)
            norm_dve(dve, rms_mlp2)
            mlp_dve(dve, mlp2)
            layer_read(dve, mlp2)
            norm_dve(dve, rms_meta)
            norm_dve(dve, rms_mix3)
            proj_dve(dve, proj3)
            gla_prep_dve(dve)
            gla_dve(dve)
            short_dve(dve)
            mix_split_dve(dve, 2)
            out_dve(dve, out3)
            layer_read(dve, out3)
            norm_dve(dve, rms_mlp3)
            mlp_dve(dve, mlp3)
            layer_read(dve, mlp3)
            norm_dve(dve, rms_final)

        @block.gpsimd
        def _(pool):
            gdn_loop_pool(pool)
            gla_pool(pool)


def lay_t5():
    n = np.clip(255 - np.arange(384), 0, None)
    large = 16 + (np.log(np.maximum(n, 1) / 16) / np.log(128 / 16) * 16).astype(np.int32)
    bucket = np.where(n < 16, n, np.minimum(large, 31))
    return (np.arange(32)[:, None] == bucket[None, :]).astype(np.float32)


def lay_swa_mask():
    dist = np.arange(P)[:, None] + P - np.arange(2 * P)[None, :]
    seen = (dist >= 0) & (dist < P)
    first = seen & (np.arange(2 * P) >= P)
    return np.where(np.stack([first, seen], 1), 0.0, -1e30).astype(np.float32)


def lay_gla_consts():
    j, i = np.arange(P)[:, None], np.arange(P)[None, :]
    out = np.zeros((P, 8, P), np.int32)
    for l in range(7):
        m = 64 >> l
        out[:, l] = (j // (2 * m) == i // (2 * m)) & (j // m % 2 == 0) & (i // m % 2 == 1)
    out[:, 7] = j == i
    return out


def kernel(**inputs):
    import concourse.bacc as bacc
    from concourse.bass_utils import run_bass_kernel_spmd

    def feats(v):
        return np.asarray(v).reshape(-1, P).T

    def units(w):
        w = np.asarray(w)
        w = np.pad(w, ((0, 0), (0, padded(w.shape[1]) - w.shape[1])))
        return w.reshape(DC, P, -1, P).transpose(2, 1, 0, 3).reshape(-1, P, UNIT)

    def mlp_units(up, down):
        up = units(up).reshape(NG, 4, P, UNIT)
        down = np.asarray(down).reshape(NG, FG // P, P, 4, 256).transpose(0, 3, 2, 1, 4).reshape(NG, 4, P, UNIT)
        return np.concatenate([up, down], 1).reshape(-1, P, UNIT)

    def taps(w):
        w = np.asarray(w)
        return w.reshape(w.shape[0], -1, P).transpose(2, 1, 0).reshape(P, -1)

    def rows(v):
        return np.broadcast_to(np.asarray(v).reshape(1, -1), (P, np.asarray(v).size))

    i = inputs
    twice = lambda v: np.tile(np.asarray(v).reshape(-1), 2).reshape(P, 1)
    full = lambda c: np.full((P, 1), c, np.float32)
    by_name = {
        "ln_in_g": feats(i["ln_in_g"]), "ln_in_b": feats(i["ln_in_b"]), "ln1_g": feats(i["ln1_g"]),
        "ln1_b": feats(i["ln1_b"]), "ln2_g": feats(i["ln2_g"]), "ln2_b": feats(i["ln2_b"]), "b1": feats(i["b1"]),
        "b2": feats(i["b2"]), "gdn_g": feats(i["gdn_norm_g"]), "na_g": twice(i["na_norm_g"]),
        "conv_w": taps(i["conv_w"][0]), "a_log": rows(i["a_log"]), "dt_bias": rows(i["dt_bias"]),
        "mix_g_2": feats(i["norm_mix_g_2"]), "q_g": twice(i["q_norm_g_2"]), "k_g": twice(i["k_norm_g_2"]),
        "conv_w_2": taps(i["conv_w_2"][0]), "conv_b_2": feats(i["conv_b_2"]), "cln_g": feats(i["conv_ln_g_2"]),
        "cln_b": feats(i["conv_ln_b_2"]), "attn_g": feats(i["attn_out_g_2"]), "cout_g": feats(i["conv_out_g_2"]),
        "mlp_g_2": feats(i["norm_mlp_g_2"]), "sinks": rows(i["sinks_2"]), "mix_g_3": feats(i["norm_mix_w_3"]),
        "b_gate": feats(i["b_gate_3"]), "gla_g": feats(i["gla_norm_w_3"]), "conv_w_3": taps(i["conv_w_3"][0]),
        "mlp_g_3": feats(i["norm_mlp_w_3"]), "final_g": feats(i["norm_final_w_3"]),
        "eps5": full(1e-5), "eps6": full(1e-6), "zero": full(0.0), "one": full(1.0),
    }
    arrays = {
        "x": np.asarray(i["x"])[0].T.reshape(DC, P, T).transpose(1, 0, 2),
        "meta": np.asarray(i["meta_tokens_3"]).T.reshape(DC, P, META).transpose(1, 0, 2),
        "params": np.concatenate([by_name[name] for name in PARAMS], 1),
        "consts": lay_consts(), "gdn_consts": lay_gdn_consts(), "na_mask": lay_na_mask(),
        "w_in1": units(i["w_in"][0]), "w_out1": units(i["w_out"][0]), "w_mlp1": mlp_units(i["w1"][0], i["w2"][0]),
        "w_in2": units(i["w_in_2"][0]), "w_out2": units(i["w_out_2"][0]),
        "w_mlp2": mlp_units(i["w_mlp_up_2"][0], i["w_mlp_down_2"][0]),
        "w_in3": units(i["w_in_3"][0]), "w_out3": units(i["w_out_3"][0]),
        "w_mlp3": mlp_units(i["w_up_3"][0], i["w_down_3"][0]),
        "rpb": np.pad(np.asarray(i["rpb"])[0], ((0, 0), (0, 0), (48, 48))).reshape(NH1, -1),
        "rel_bias": i["rel_bias_2"], "t5": lay_t5(), "swa_mask": lay_swa_mask(), "w_gate": np.asarray(i["w_gate_up_3"])[0], "gla_consts": lay_gla_consts(),
    }
    nc = bacc.Bacc("TRN2", target_bir_lowering=False, num_devices=1)
    feed, drams = {}, {}
    for name, a in arrays.items():
        a = np.ascontiguousarray(a)
        feed["in_" + name] = a
        drams[name] = nc.dram_tensor("in_" + name, a.shape, mybir.dt.from_np(a.dtype), kind="ExternalInput").ap()
    for name, shape in {"h1": [padded(COLS1), T], "h2": [padded(COLS2), T], "h3": [padded(COLS3), TM], 
                        "rpb_rows": [NH1, GRID, (2 * KR - 1) * (2 * KC - 1 + 96)],
                        "t5_rows": [8, P, 384]}.items():
        drams[name] = nc.dram_tensor(name, shape, F32, kind="Internal").ap()
    drams["out"] = nc.dram_tensor("out", [DC, P, T], F32, kind="ExternalOutput").ap()
    build_program(nc, drams)
    r = run_bass_kernel_spmd(nc, [feed], core_ids=[0])
    return r.results[0]["out"].reshape(1, D, T).transpose(0, 2, 1)
```

```python
from contextlib import ExitStack

import numpy as np

import concourse.bass as bass
from concourse import mybir

F32 = mybir.dt.float32
F32R = mybir.dt.float32r
I32 = mybir.dt.int32
ALU = mybir.AluOpType
ACT = mybir.ActivationFunctionType
AX = mybir.AxisListType

P = 128
D = 1024
DC = D // P
T = 1024
HALF = 512
TC = T // P
FF = 4 * D
FG = 512
NG = FF // FG
META = 16
TM = META + T
ALPHA = 2.0 ** 0.25
UNIT = 1024

LOG_EXP = "natural_log_exp_and_others"
GH = 4
NH1 = 8
GRID = 64
ROWS = T // GRID
KR, KC = 8, 16
COLS1, COLS2, COLS3 = 3600, 1792, 3088

ORDER3 = {}
_n = 0
for _name, _w in [("b", 512), ("q", 256), ("g", 512), ("c", 512), ("x", 512), ("k", 256), ("v", 512), ("r", 16)]:
    ORDER3[_name] = (_n, _w)
    _n += _w
THIRDS = [(0, 352), (352, 704), (704, TM)]
EARLY1 = 13
CONV3 = (ORDER3["c"][0] // 256, ORDER3["k"][0] // 256)


def padded(cols):
    return -(-cols // 256) * 256


PARAMS = {}
_n = 0
for _name, _w in [
    ("ln_in_g", 8), ("ln_in_b", 8), ("ln1_g", 8), ("ln1_b", 8), ("ln2_g", 8), ("ln2_b", 8), ("b1", 32), ("b2", 8),
    ("gdn_g", 1), ("na_g", 1), ("conv_w", 60), ("a_log", 8), ("dt_bias", 8),
    ("mix_g_2", 8), ("q_g", 1), ("k_g", 1), ("conv_w_2", 124), ("conv_b_2", 4), ("cln_g", 4), ("cln_b", 4),
    ("attn_g", 4), ("cout_g", 4), ("mlp_g_2", 8), ("sinks", 8),
    ("mix_g_3", 8), ("b_gate", 2), ("gla_g", 1), ("conv_w_3", 12), ("mlp_g_3", 8), ("final_g", 8),
    ("eps5", 1), ("eps6", 1), ("zero", 1), ("one", 1),
]:
    PARAMS[_name] = (_n, _w)
    _n += _w
NPARAM = _n

CONSTS = {}
_n = 0
for _name, _w in [("ident", 128), ("ones", 128), ("ones_half", 128), ("fold", 64)]:
    CONSTS[_name] = (_n, _w)
    _n += _w
NCONST = _n
GDN_LEVELS = 7


def lay_consts():
    i = np.arange(P)
    c = np.zeros((P, NCONST), np.float32)
    by_name = {
        "ident": np.eye(P), "ones": np.ones((P, P)), 
        "ones_half": (i[:, None] // 64) == (i[None, :] // 64),
        "fold": (i[:, None] % 64) == np.arange(64)[None, :],
    }
    for name, (first, width) in CONSTS.items():
        c[:, first:first + width] = by_name[name]
    return c


def lay_gdn_consts():
    r, s = np.arange(P)[:, None], np.arange(P)[None, :]
    out = np.zeros((P, 20, P), np.float32)
    for d in range(2):
        below = (r > s) if d == 0 else (r < s)
        out[:, 10 * d] = (r <= s) if d == 0 else (r >= s)
        out[:, 10 * d + 1] = np.where((r <= s) if d == 0 else (r >= s), 0.0, -1e30)
        out[:, 10 * d + 2] = np.where(below, 0.0, -1e30)
        for l in range(GDN_LEVELS):
            b = 1 << l
            out[:, 10 * d + 3 + l] = below & (r // (2 * b) == s // (2 * b)) & (r // b != s // b)
    return out


def lay_na_mask():
    q, k = np.arange(GRID)[:, None], np.arange(GRID)[None, :]
    start = np.clip(q - KC // 2, 0, GRID - KC)
    m = np.where((k >= start) & (k < start + KC), 0.0, -1e30).astype(np.float32)
    return np.concatenate([m, m], 0)


def build_program(nc, g):
    ctx = ExitStack()
    with ctx:
        base = -(-nc.sbuf_base // 64) * 64
        end = nc.sbuf_usable_end // 64 * 64

        class Region:

            def __init__(self, start, stop):
                self.at, self.stop = start, stop

            def take(self, name, shape, dt=F32):
                size = -(-4 * int(np.prod(shape[1:])) // 32) * 32
                assert self.at + size <= self.stop, (name, self.at + size - self.stop)
                t = nc.alloc_sbuf_tensor_at(name, shape, dt, offset=self.at)
                self.at += size
                return t

        def sem(name):
            return ctx.enter_context(nc.semaphore(name))

        def param(name, j=0, n=1):
            return params[:, bass.ds(j + PARAMS[name][0], n)]

        def const(name):
            return consts[:, CONSTS[name][0]:CONSTS[name][0] + CONSTS[name][1]]

        keep = Region(base, end)
        xT = keep.take("xT", [P, DC, T])
        w_raw = [keep.take(f"w_raw{s}", [P, UNIT]) for s in range(2)]
        w_hi = [keep.take(f"w_hi{s}", [P, UNIT], F32R) for s in range(2)]
        w_lo = [keep.take(f"w_lo{s}", [P, UNIT], F32R) for s in range(2)]
        params = keep.take("params", [P, NPARAM])
        consts = keep.take("consts", [P, NCONST])
        tick = keep.take("tick", [P, 16])
        arena = keep.at
        ops_end = arena + 2 * DC * TM * 4
        lin = Region(arena, ops_end)
        a_hi = lin.take("a_hi", [P, DC, TM], F32R)
        a_lo = lin.take("a_lo", [P, DC, TM], F32R)
        mix_end = ops_end + DC * T * 4
        hid = Region(ops_end, mix_end)
        h_hi = hid.take("h_hi", [P, FG // P, T], F32R)
        h_lo = hid.take("h_lo", [P, FG // P, T], F32R)
        mixT = Region(ops_end, mix_end).take("mixT", [P, DC, T])
        tmp = Region(mix_end, end)
        metaT = tmp.take("metaT", [P, DC, META])
        n_sq = [tmp.take(f"n_sq{s}", [P, T]) for s in range(2)]
        n_rs = tmp.take("n_rs", [P, T])
        n_y = [tmp.take(f"n_y{s}", [P, T]) for s in range(2)]
        n_acc = tmp.take("n_acc", [P, T])
        n_asq = tmp.take("n_asq", [P, T])
        m_sq, m_y = (tmp.take(name, [P, DC, META]) for name in ["m_sq", "m_y"])
        m_rs = tmp.take("m_rs", [P, META])
        u_act = [tmp.take(f"u_act{s}", [P, T]) for s in range(2)]
        u_sq = [tmp.take(f"u_sq{s}", [P, T]) for s in range(2)]
        stage_tiles = Region(ops_end, mix_end)
        staged = [stage_tiles.take(f"staged{s}", [P, TM]) for s in range(2)]

        ps = ctx.enter_context(nc.psum_tensor("ps", [P, 8, HALF], F32))

        def banks(b, n=2):
            return ps[:, b:b + n, :].rearrange("p b n -> p (b n)")

        w_landed = [sem(f"w_landed{s}") for s in range(2)]
        w_hi_done = [sem(f"w_hi_done{s}") for s in range(2)]
        w_split = [sem(f"w_split{s}") for s in range(2)]
        mm_done = [sem(f"mm_done{s}") for s in range(2)]
        ps_free = [sem(f"ps_free{s}") for s in range(2)]
        stored = [sem(f"stored{s}") for s in range(2)]
        loaded = sem("loaded")
        hid_sq = sem("hid_sq")
        hid_hi = sem("hid_hi")
        hid_ready = sem("hid_ready")
        mix_hi = sem("mix_hi")
        mix_ready = sem("mix_ready")

        class Stage:
            pass

        counts = {"pairs": 0, "stores": [0, 0], "mlps": 0}

        def linear(kind, weights, pairs, h=None, tail=False, n=T, bias=False, parts=()):
            st = Stage()
            st.kind, st.w, st.pairs, st.next = kind, weights, pairs, None
            st.h, st.tail, st.n, st.bias = h, tail, n, bias
            st.parts = parts or [(0, pairs - tail, n)]
            st.k0, st.m0 = counts["pairs"], counts["mlps"]
            st.q0 = list(counts["stores"])
            counts["pairs"] += pairs
            if kind == "proj":
                counts["stores"] = [st.q0[0] + pairs, st.q0[1] + pairs - tail]
            counts["mlps"] += kind == "mlp"
            return st

        proj1 = linear("proj", g["w_in1"], padded(COLS1) // 256, h=g["h1"], tail=True, parts=[(0, EARLY1, T), (EARLY1, padded(COLS1) // 256 - 1, T)])
        out1 = linear("out", g["w_out1"], 4)
        mlp1 = linear("mlp", g["w_mlp1"], 4 * NG, bias=True)
        proj2 = linear("proj", g["w_in2"], padded(COLS2) // 256, h=g["h2"])
        out2 = linear("out", g["w_out2"], 4)
        mlp2 = linear("mlp", g["w_mlp2"], 4 * NG, bias=False)
        proj3 = linear("proj", g["w_in3"], padded(COLS3) // 256, h=g["h3"], tail=True, n=TM,
                       parts=[(0, CONV3[0], T), (CONV3[0], CONV3[1], TM), (CONV3[1], padded(COLS3) // 256 - 1, TM)])
        out3 = linear("out", g["w_out3"], 4)
        mlp3 = linear("mlp", g["w_mlp3"], 4 * NG, bias=False)
        linears = [proj1, out1, mlp1, proj2, out2, mlp2, proj3, out3, mlp3]
        for a, b in zip(linears, linears[1:]):
            a.next = b

        def layer_read(eng, st):
            for s in range(2):
                eng.wait_ge(ps_free[s], st.k0 + st.pairs + 1)

        def first_pair_sp(sp, st):
            for s in range(2):
                sp.wait_ge(w_split[s], st.k0 + 1)
                sp.dma_start(w_raw[s][:, :], st.w[s]).then_inc(w_landed[s], 16)

        def linear_sp(sp, st, then=None):
            def store(s, row, k, n):
                sp.wait_ge(ps_free[s], k + 2)
                sp.dma_start(st.h[bass.ds(row, P), st.n - n:st.n], staged[s][:, TM - n:TM]).then_inc(stored[s], 16)

            for p0, p1, n in st.parts:
                with sp.Fori(p0 + 1, min(p1 + 1, st.pairs)) as p:
                    units = [sp.snap(2 * p + s) for s in range(2)]
                    rows = [sp.snap(2 * P * p + (s - 2) * P) for s in range(2)]
                    for s in range(2):
                        sp.wait_ge(w_split[s], p + (st.k0 + 1))
                        sp.dma_start(w_raw[s][:, :], st.w[bass.ds(units[s], 1)].rearrange("o p n -> (o p) n"))\
                            .then_inc(w_landed[s], 16)
                    if st.kind == "proj":
                        for s in range(2):
                            store(s, rows[s], p + (st.k0 - 1), n)
                if then is not None and p1 == then[0]:
                    for s in range(2):
                        sp.wait_ge(stored[s], 16 * (st.q0[s] + p1) + 16)
                    then[1](sp)
            if st.next is not None:
                first_pair_sp(sp, st.next)
            if st.kind == "proj":
                store(0, 2 * P * (st.pairs - 1), st.k0 + st.pairs - 1, st.parts[-1][2])
                if not st.tail:
                    store(1, 2 * P * (st.pairs - 1) + P, st.k0 + st.pairs - 1, st.parts[-1][2])

        def split_hi(act, s, k):
            act.wait_ge(w_landed[s], 16 * k + 16)
            act.wait_ge(mm_done[s], k + 1)
            nc.scalar.activation(w_hi[s][:, :], w_raw[s][:, :], ACT.Copy).then_inc(w_hi_done[s], 1)

        def split_lo(dve, s, k):
            dve.wait_ge(w_hi_done[s], k + 1)
            nc.vector.tensor_tensor(w_lo[s][:, :], w_raw[s][:, :], w_hi[s][:, :].bitcast(F32),
                                    ALU.subtract).then_inc(w_split[s], 1)

        def three(s, hi, lo):
            return (w_hi[s], hi), (w_hi[s], lo), (w_lo[s], hi)

        def unit_mm(s, n, chunk=None):
            spans = [(META, META + HALF), (META + HALF, TM)] if n == T else THIRDS
            for k in range(DC):
                if chunk is not None:
                    chunk(k)
                for j, (w, a) in enumerate(three(s, a_hi, a_lo)):
                    for b, (t0, t1) in enumerate(spans):
                        last = nc.tensor.matmul(ps[:, 4 * s + b, 0:t1 - t0], w[:, k * P:(k + 1) * P], a[:, k, t0:t1],
                                                start=(k == 0 and j == 0), stop=(k == DC - 1 and j == 2))
            return last

        def norm_chunk(pe, st):
            m = st.norm
            return lambda k: pe.wait_ge(n_done, DC * m.io + k + 1)

        def mix_chunk(pe, i):
            return lambda k: pe.wait_ge(mix_ready, DC * i + k + 1)

        def unit_wait(pe, s, k):
            pe.wait_ge(w_split[s], k + 2)
            pe.wait_ge(ps_free[s], k + 1)

        def proj_pe(pe, st):
            for p0, p1, n in st.parts:
                with pe.Fori(p0, p1) as p:
                    for s in range(2):
                        unit_wait(pe, s, p + st.k0)
                        unit_mm(s, n, None if s or p0 else norm_chunk(pe, st)).then_inc(mm_done[s], 1)
            if st.tail:
                k = st.k0 + st.pairs - 1
                unit_wait(pe, 0, k)
                unit_mm(0, st.n).then_inc(mm_done[0], 1)
                unit_wait(pe, 1, k)
                nc.tensor.matmul(ps[:, 4, 0:P], w_hi[1][:, 0:P], a_hi[:, 0, META:META + P], start=True, stop=True)\
                    .then_inc(mm_done[1], 1)

        def proj_act(act, st):
            def unit(s, k, q, n, whole=True):
                split_hi(act, s, k + 1)
                act.wait_ge(mm_done[s], k + 2)
                if not whole:
                    nc.scalar.activation(tick[:, 7:8], param("zero"), ACT.Copy).then_inc(ps_free[s], 1)
                    return
                act.wait_ge(stored[s], 16 * q + 16)
                if n == T:
                    nc.scalar.activation(staged[s][:, META:TM], banks(4 * s), ACT.Copy).then_inc(ps_free[s], 1)
                    return
                (_, a), (_, b), (_, c) = THIRDS
                nc.scalar.activation(staged[s][:, 0:b].rearrange("p (b n) -> p b n", b=2), ps[:, 4 * s:4 * s + 2, 0:a], ACT.Copy)
                nc.scalar.activation(staged[s][:, b:c], ps[:, 4 * s + 2, 0:c - b], ACT.Copy).then_inc(ps_free[s], 1)

            for p0, p1, n in st.parts:
                with act.Fori(p0, p1) as p:
                    for s in range(2):
                        unit(s, p + st.k0, p + st.q0[s], n)
            if st.tail:
                for s in range(2):
                    unit(s, st.k0 + st.pairs - 1, st.q0[s] + st.pairs - 1, st.n, whole=(s == 0))

        def proj_dve(dve, st, beside=(1, 1, None)):
            first, last, work = beside
            for p0, p1 in [(0, first), (first, last), (last, st.pairs)]:
                if p0 < p1:
                    with dve.Fori(p0, p1) as p:
                        for s in range(2):
                            split_lo(dve, s, p + (st.k0 + 1))
                        if p0 == first and p1 == last:
                            work(dve, p)

        def proj_stored(eng, st):
            for s in range(2):
                eng.wait_ge(stored[s], 16 * (st.q0[s] + st.pairs - (st.tail and s == 1)) + 16)

        def mix_split_act(act, i, chunks=range(DC)):
            for c in chunks:
                nc.scalar.activation(a_hi[:, c, META:TM], mixT[:, c, :], ACT.Copy).then_inc(mix_hi, 1)

        def mix_split_dve(dve, i, chunks=range(DC)):
            for c in chunks:
                dve.wait_ge(mix_hi, DC * i + c + 1)
                nc.vector.tensor_tensor(a_lo[:, c, META:TM], mixT[:, c, :], a_hi[:, c, META:TM].bitcast(F32),
                                        ALU.subtract).then_inc(mix_ready, 1)

        def out_pe(pe, st, i):
            with pe.Fori(0, st.pairs) as p:
                for s in range(2):
                    unit_wait(pe, s, p + st.k0)
                    unit_mm(s, T, None if s else mix_chunk(pe, i)).then_inc(mm_done[s], 1)

        def out_act(act, st):
            with act.Fori(0, st.pairs) as p:
                for s in range(2):
                    split_hi(act, s, p + (st.k0 + 1))

        def out_dve(dve, st):
            with dve.Fori(0, st.pairs) as p:
                for s in range(2):
                    chunk = xT[:, bass.ds(2 * p + s, 1), :].rearrange("p o t -> p (o t)")
                    split_lo(dve, s, p + (st.k0 + 1))
                    dve.wait_ge(mm_done[s], p + (st.k0 + 2))
                    nc.vector.tensor_tensor(chunk, chunk, banks(4 * s), ALU.add).then_inc(ps_free[s], 1)

        def mlp_pe(pe, st):
            with pe.Fori(0, NG) as gr:
                for j in range(4):
                    unit_wait(pe, j % 2, 4 * gr + (st.k0 + j // 2))
                    unit_mm(j % 2, T, None if j else norm_chunk(pe, st)).then_inc(mm_done[j % 2], 1)
                for j in range(4):
                    s = j % 2
                    unit_wait(pe, s, 4 * gr + (st.k0 + 2 + j // 2))
                    for k in range(FG // P):
                        if j == 0:
                            pe.wait_ge(hid_ready, 4 * gr + (4 * NG * st.m0 + k + 1))
                        for c in range(2):
                            for i, (w, a) in enumerate(three(s, h_hi, h_lo)):
                                for b in range(2):
                                    last = nc.tensor.matmul(
                                        ps[:, 4 * s + 2 * c + b, :], w[:, k * 256 + c * P:k * 256 + (c + 1) * P],
                                        a[:, k, b * HALF:(b + 1) * HALF], start=(k == 0 and i == 0),
                                        stop=(k == FG // P - 1 and i == 2))
                    last.then_inc(mm_done[s], 1)

        def mlp_act(act, st):
            def group(gr, final=False):
                for j in range(4):
                    s = j % 2
                    k, q = 4 * gr + (st.k0 + j // 2), 4 * gr + (4 * NG * st.m0 + j)
                    split_hi(act, s, k + 1)
                    act.wait_ge(mm_done[s], k + 2)
                    act.wait_ge(hid_sq, q + 1)
                    bias = param("b1", 4 * gr + j) if st.bias else 0.0
                    nc.scalar.activation(u_act[s][:, :], banks(4 * s), ACT.Relu, bias=bias).then_inc(ps_free[s], 1)
                    act.wait_ge(ps_free[s], k + 2)
                    nc.scalar.activation(h_hi[:, j, :], u_act[s][:, :], ACT.Square).then_inc(hid_hi, 1)
                for j in range(4):
                    if not (final and j >= 2):
                        split_hi(act, j % 2, 4 * gr + (st.k0 + 2 + j // 2 + 1))

            with act.Fori(0, NG - (st.next is None)) as gr:
                group(gr)
            if st.next is None:
                group(NG - 1, final=True)

        def mlp_dve(dve, st):
            def group(gr, final=False):
                for j in range(4):
                    s = j % 2
                    k, q = 4 * gr + (st.k0 + j // 2), 4 * gr + (4 * NG * st.m0 + j)
                    split_lo(dve, s, k + 1)
                    dve.wait_ge(ps_free[s], k + 2)
                    nc.vector.tensor_tensor(u_sq[s][:, :], u_act[s][:, :], u_act[s][:, :], ALU.mult).then_inc(hid_sq, 1)
                    dve.wait_ge(hid_sq, q + 3)
                    dve.wait_ge(hid_hi, q + 1)
                    nc.vector.tensor_tensor(h_lo[:, j, :], u_sq[s][:, :], h_hi[:, j, :].bitcast(F32),
                                            ALU.subtract).then_inc(hid_ready, 1)
                for j in range(4):
                    s = j % 2
                    k = 4 * gr + (st.k0 + 2 + j // 2)
                    if not (final and j >= 2):
                        split_lo(dve, s, k + 1)
                    dve.wait_ge(mm_done[s], k + 2)
                    two = xT[:, 2 * j:2 * j + 2, :].rearrange("p c t -> p (c t)")
                    nc.vector.tensor_tensor(two, two, banks(4 * s, 4), ALU.add).then_inc(ps_free[s], 1)

            with dve.Fori(0, NG - (st.next is None)) as gr:
                group(gr)
            if st.next is None:
                group(NG - 1, final=True)

        n_step = sem("n_step")
        n_sum = sem("n_sum")
        n_centred = sem("n_centred")
        n_squared = sem("n_squared")
        n_summed = sem("n_summed")
        n_ln = sem("n_ln")
        n_rstd = sem("n_rstd")
        n_scaled = sem("n_scaled")
        n_hi = sem("n_hi")
        n_done = sem("n_done")
        res_scaled = sem("res_scaled")
        norms = {"all": 0, "centred": 0, "squares": 0, "steps": 0, "hi": 0, "split": 0}

        class Norm:

            def __init__(self, x, n, at, gamma, beta=None, eps="eps6", scale=None, plus=None, split=True, after=None, chained=False):
                self.x, self.n, self.at, self.gamma, self.beta, self.eps = x, n, at, gamma, beta, eps
                self.scale, self.plus, self.split, self.after, self.chained = scale, plus, split, after, chained
                self.shift = beta is not None
                self.pre = 0 if after is None else DC - 1 if after.kind == "out" else DC - 2
                self.steps = self.pre and (self.pre - 1 if self.shift else 2 * self.pre - 1)
                self.squares = DC if self.shift else DC - self.pre
                self.i, self.ic, self.iq, self.ip, self.ih, self.io = (
                    norms[key] for key in ("all", "centred", "squares", "steps", "hi", "split"))
                norms["all"] += 1
                norms["centred"] += self.shift
                norms["squares"] += self.squares
                norms["steps"] += self.steps
                norms["hi"] += self.shift or split
                norms["split"] += split
                self.spans = [(0, HALF), (HALF, T)] if n == T else [(0, n)]

        def chunk_final(eng, st, c):
            if st.kind == "out":
                eng.wait_ge(ps_free[c % 2], st.k0 + c // 2 + 2)
            else:
                eng.wait_ge(ps_free[c // 2 % 2], st.k0 + st.pairs + c // 4)

        def norm_pool(pool, m):
            done = [m.ip]

            def step(out, a, b, op):
                nc.gpsimd.tensor_tensor(out[:, :], a, b, op).then_inc(n_step, 1)
                done[0] += 1
                pool.wait_ge(n_step, done[0])

            if m.shift:
                for c in range(m.pre):
                    chunk_final(pool, m.after, c)
                    if c:
                        step(n_acc, m.x[:, 0, :] if c == 1 else n_acc[:, :], m.x[:, c, :], ALU.add)
                return
            for c in range(m.pre):
                chunk_final(pool, m.after, c)
                step(n_asq if c else n_acc, m.x[:, c, :], m.x[:, c, :], ALU.mult)
                if c:
                    step(n_acc, n_acc[:, :], n_asq[:, :], ALU.add)

        def norm_pe(pe, m):
            def sums(bank, tile, first, last):
                for b, (t0, t1) in enumerate(m.spans):
                    ins = nc.tensor.matmul(ps[:, bank + b, 0:t1 - t0], const("ones"), tile[:, t0:t1], start=first, stop=last)
                return ins

            if m.pre:
                pe.wait_ge(n_step, m.ip + m.steps)
                sums(0 if m.shift else 2, n_acc, True, False)
            if m.shift:
                for c in range(m.pre, DC):
                    last = sums(0, m.x[:, c, :], c == 0, c == DC - 1)
                last.then_inc(n_sum, 1)
            for q in range(m.squares):
                pe.wait_ge(n_squared, m.iq + q + 1)
                sums(2, n_sq[q % 2], q == 0 and (m.shift or not m.pre), q == m.squares - 1).then_inc(n_summed, 1)

        def square(act, m, q):
            c = DC - m.squares + q
            if q >= 2:
                act.wait_ge(n_summed, m.iq + q - 1)
            nc.scalar.activation(n_sq[q % 2][:, 0:m.n], m.x[:, c, :], ACT.Square).then_inc(n_squared, 1)

        def norm_act(act, m, then=None):
            norm_rstd_act(act, m)
            norm_high_act(act, m, then)

        def norm_rstd_act(act, m):
            if not m.chained:
                for q in range(m.squares):
                    if m.shift:
                        act.wait_ge(n_centred, DC * m.ic + q + 1)
                    square(act, m, q)
            act.wait_ge(n_summed, m.iq + m.squares)
            nc.scalar.activation(n_rs[:, 0:m.n], banks(2)[:, 0:m.n], ACT.Ln, bias=param(m.eps), scale=1.0 / D).then_inc(n_ln, 1)
            act.wait_ge(n_ln, m.i + 1)
            nc.scalar.activation(n_rs[:, 0:m.n], n_rs[:, 0:m.n], ACT.Exp, scale=-0.5).then_inc(n_rstd, 1)

        def norm_high_act(act, m, then=None):
            if not (m.split or m.shift):
                return
            for c in range(DC):
                act.wait_ge(n_scaled, DC * m.i + c + 1)
                hi = a_hi[:, c, m.at:m.at + m.n]
                if m.shift:
                    if m.split:
                        nc.scalar.activation(hi, m.x[:, c, :], ACT.Identity, bias=param(m.beta, c))
                    nc.scalar.activation(m.x[:, c, :], m.x[:, c, :], ACT.Identity, bias=param(m.beta, c)).then_inc(n_hi, 1)
                    if then is not None:
                        act.wait_ge(n_hi, DC * m.ih + c + 1)
                        square(act, then, c)
                else:
                    nc.scalar.activation(hi, n_y[c % 2][:, 0:m.n], ACT.Copy).then_inc(n_hi, 1)

        def norm_dve(dve, m):
            if m.shift:
                dve.wait_ge(n_sum, m.ic + 1)
                for c in range(DC):
                    nc.vector.scalar_tensor_tensor(m.x[:, c, :], banks(0)[:, 0:m.n], -1.0 / D, m.x[:, c, :],
                                                   op0=ALU.mult, op1=ALU.add).then_inc(n_centred, 1)
            dve.wait_ge(n_rstd, m.i + 1)

            def scale(c):
                out = m.x[:, c, :] if m.shift or not m.split else n_y[c % 2][:, 0:m.n]
                if m.shift:
                    dve.wait_ge(n_centred, DC * m.ic + c + 1)
                elif m.split:
                    dve.wait_ge(n_done, DC * m.io + max(c - 1, 0))
                nc.vector.scalar_tensor_tensor(out, m.x[:, c, :], param(m.gamma, c), n_rs[:, 0:m.n],
                                               op0=ALU.mult, op1=ALU.mult).then_inc(n_scaled, 1)

            def low(c):
                dve.wait_ge(n_hi, DC * m.ih + c + 1)
                val = m.x[:, c, :] if m.shift else n_y[c % 2][:, 0:m.n]
                nc.vector.tensor_tensor(a_lo[:, c, m.at:m.at + m.n], val, a_hi[:, c, m.at:m.at + m.n].bitcast(F32),
                                        ALU.subtract).then_inc(n_done, 1)
                if m.scale:
                    plus = param(m.plus, c) if m.plus else param("zero")
                    nc.vector.tensor_scalar(val, val, m.scale, plus, ALU.mult, ALU.add).then_inc(res_scaled, 1)

            if not m.split:
                for c in range(DC):
                    scale(c)
                return
            scale(0)
            for c in range(1, DC):
                scale(c)
                low(c - 1)
            low(DC - 1)

        meta = sem("meta")

        def meta_square_act(act):
            act.wait_ge(loaded, 64)
            nc.scalar.activation(m_sq[:, :, :], metaT[:, :, :], ACT.Square).then_inc(meta, 1)

        def meta_pe(pe):
            pe.wait_ge(meta, 1)
            for c in range(DC):
                last = nc.tensor.matmul(ps[:, 1, 0:META], const("ones"), m_sq[:, c, :], start=(c == 0), stop=(c == DC - 1))
            last.then_inc(meta, 1)

        def meta_rstd_act(act):
            act.wait_ge(meta, 2)
            nc.scalar.activation(m_rs[:, :], ps[:, 1, 0:META], ACT.Ln, bias=param("eps6"), scale=1.0 / D).then_inc(meta, 1)
            act.wait_ge(meta, 3)
            nc.scalar.activation(m_rs[:, :], m_rs[:, :], ACT.Exp, scale=-0.5).then_inc(meta, 1)

        def meta_dve(dve):
            dve.wait_ge(meta, 4)
            nc.vector.tensor_tensor(m_y[:, :, :], metaT[:, :, :], m_rs[:, :].unsqueeze(1).to_broadcast([P, DC, META]), ALU.mult)\
                .then_inc(meta, 1)
            dve.wait_ge(meta, 5)
            nc.vector.tensor_tensor(m_y[:, :, :], m_y[:, :, :], param("mix_g_3", 0, DC).unsqueeze(2).to_broadcast([P, DC, META]), ALU.mult)\
                .then_inc(meta, 1)
            dve.wait_ge(meta, 7)
            nc.vector.tensor_tensor(a_lo[:, :, 0:META], m_y[:, :, :], a_hi[:, :, 0:META].bitcast(F32), ALU.subtract).then_inc(meta, 1)

        def meta_high_act(act):
            act.wait_ge(meta, 6)
            nc.scalar.activation(a_hi[:, :, 0:META], m_y[:, :, :], ACT.Copy).then_inc(meta, 1)

        def norm_shifted(eng, m):
            eng.wait_ge(n_hi, DC * m.ih + DC)

        ln_in = Norm(xT, T, META, "ln_in_g", "ln_in_b", eps="eps5", scale=ALPHA)
        ln1 = Norm(xT, T, META, "ln1_g", "ln1_b", eps="eps5", scale=ALPHA, plus="b2", after=out1)
        ln2 = Norm(xT, T, META, "ln2_g", "ln2_b", eps="eps5", split=False, after=mlp1)
        rms_mix2 = Norm(xT, T, META, "mix_g_2", chained=True)
        rms_mlp2 = Norm(xT, T, META, "mlp_g_2", after=out2)
        rms_mix3 = Norm(xT, T, META, "mix_g_3", after=mlp2)
        rms_mlp3 = Norm(xT, T, META, "mlp_g_3", after=out3)
        rms_final = Norm(xT, T, META, "final_g", split=False, after=mlp3)
        for st, m in [(proj1, ln_in), (mlp1, ln1), (proj2, rms_mix2), (mlp2, rms_mlp2), (proj3, rms_mix3), (mlp3, rms_mlp3)]:
            st.norm = m
        gop = Region(arena, ops_end)
        g_qT = gop.take("g_qT", [P, GH, T])
        g_kT = gop.take("g_kT", [P, GH, T])
        g_kt = gop.take("g_kt", [P, TC, GH, P])
        g_vt = gop.take("g_vt", [P, TC, GH, P])
        gwork = [Region(mix_end, end - 64), Region(ops_end + 4 * T * 4, mix_end)]
        g_const = gwork[0].take("g_const", [P, 20, P])
        g_gates = gwork[0].take("g_gates", [P, 8, 2, TC, GH])
        G_LOG, G_CUM, G_TOT, G_BETA, G_NEGDEC, G_KDEC, G_LAST, G_TMP = range(8)

        def gate(i):
            return g_gates[:, i].rearrange("p d c h -> p (d c h)")

        prep = Region(gwork[0].at, end - 64)
        g_in = [prep.take(f"g_in{j}", [P, T]) for j in range(3)]
        g_act = [prep.take(f"g_act{j}", [P, T]) for j in range(3)]
        g_kn = prep.take("g_kn", [P, T])
        prep2 = Region(ops_end + 4 * T * 4, mix_end)
        g_sq = [prep2.take(f"g_sq{j}", [P, T]) for j in range(2)]
        g_rs = [prep2.take(f"g_rs{j}", [P, T]) for j in range(2)]
        gconv = Region(mix_end, end)
        g_raw = gconv.take("g_raw", [P, T + 4])
        g_conv = gconv.take("g_conv", [P, T])
        g_ab = prep.take("g_ab", [16, T])
        g_alog = prep.take("g_alog", [P, 8])

        def work(d, name, shape):
            r = gwork[d]
            if r.at + 4 * int(np.prod(shape[1:])) > r.stop:
                r = gwork[0]
            return r.take(f"{name}{d}", shape)

        g_S = [work(d, "g_S", [P, GH, P]) for d in range(2)]
        g_gu = [work(d, "g_gu", [P, GH, P]) for d in range(2)]
        g_qd = [work(d, "g_qd", [P, GH, P]) for d in range(2)]
        g_D = [work(d, "g_D", [P, GH, P]) for d in range(2)]
        g_Dt = [work(d, "g_Dt", [P, GH, P]) for d in range(2)]
        g_A = [work(d, "g_A", [P, GH, P]) for d in range(2)]
        g_kd = [work(d, "g_kd", [P, GH, P]) for d in range(2)]
        g_vn = [work(d, "g_vn", [P, GH, P]) for d in range(2)]
        g_kc = [work(d, "g_kc", [P, GH, P]) for d in range(2)]
        g_gam = [work(d, "g_gam", [P, 2, GH, P]) for d in range(2)]
        g_off = [work(d, "g_off", [P, 2, GH, P]) for d in range(2)]

        gp_in = [sem(f"gp_in{j}") for j in range(3)]
        gc_in = sem("gc_in")
        gc_tap = sem("gc_tap")
        gc_out = sem("gc_out")
        gp_silu = sem("gp_silu")
        gp_sq = sem("gp_sq")
        gp_sum = sem("gp_sum")
        gp_ln = sem("gp_ln")
        gp_rs = sem("gp_rs")
        gp_norm = sem("gp_norm")
        gp_tr = sem("gp_tr")
        gp_end = sem("gp_end")
        gg_in = sem("gg_in")
        gg = sem("gg")
        gg_tr = sem("gg_tr")
        gg_trc = sem("gg_trc")
        gg_act = sem("gg_act")
        gg_sum = sem("gg_sum")
        gg_ready = sem("gg_ready")
        NT = 5

        def gdn_early_sp(sp):
            sp.wait_ge(gc_out, 16 * GCH)
            sp.dma_start(g_const[:, :, :], g["gdn_consts"]).then_inc(gg_in, 16)
            for j in range(3):
                sp.dma_start(g_in[j][:, :], g["conv1"][j * GH * P:j * GH * P + P, :]).then_inc(gp_in[j], 16)

        def gdn_sp(sp):
            proj_stored(sp, proj1)
            sp.dma_start(g_ab[:, :], g["h1"][4 * GH * P:4 * GH * P + 16, :]).then_inc(gg_in, 16)
            with sp.Fori(1, GH) as h:
                rows = [sp.snap(h * P + j * GH * P) for j in range(3)]
                for j in range(3):
                    sp.wait_ge(gp_silu, 3 * h + (j - 2))
                    sp.dma_start(g_in[j][:, :], g["conv1"][bass.ds(rows[j], P), :]).then_inc(gp_in[j], 16)

        GCH = 3 * GH

        def gdn_conv_pool(pool):
            pool.wait_ge(n_done, DC)
            for i in range(GCH):
                pool.wait_ge(stored[i % 2], 16 * (proj1.q0[i % 2] + i // 2 + 1) + 16)
                if i:
                    pool.wait_ge(gc_out, 16 * i)
                nc.gpsimd.dma_start(g_raw[:, 2:T + 2], g["h1"][i * P:(i + 1) * P, :]).then_inc(gc_in, 16)
                pool.wait_ge(gc_tap, NT * (i + 1) + 1)
                nc.gpsimd.dma_start(g["conv1"][i * P:(i + 1) * P, :], g_conv[:, :]).then_inc(gc_out, 16)

        def gdn_pad_dve(dve):
            dve.wait_ge(n_done, DC)
            nc.vector.memset(g_raw[:, 0:2], 0.0)
            nc.vector.memset(g_raw[:, T + 2:T + 4], 0.0).then_inc(gc_tap, 1)

        def gdn_conv_dve(dve, p):
            dve.wait_ge(gc_in, 16 * p)
            for tap in range(NT):
                w = param("conv_w", NT * p + (tap - NT))
                dve.wait_ge(gc_tap, NT * p + (tap + 1 - NT))
                if tap == 0:
                    ins = nc.vector.tensor_scalar(g_conv[:, :], g_raw[:, 0:T], w, None, ALU.mult)
                else:
                    ins = nc.vector.scalar_tensor_tensor(g_conv[:, :], g_raw[:, tap:tap + T], w, g_conv[:, :], op0=ALU.mult, op1=ALU.add)
                ins.then_inc(gc_tap, 1)

        def gdn_gates_pe(pe):
            pe.wait_ge(gg_in, 32)
            for c in range(TC):
                last = nc.tensor.transpose(ps[:, 0, c * 16:(c + 1) * 16], g_ab[:, c * P:(c + 1) * P], const("ident")[0:16, 0:16])
            last.then_inc(gg_tr, 1)
            pe.wait_ge(gg, 8)
            for d in range(2):
                nc.tensor.matmul(ps[:, 1, 32 * d:32 * d + 32], g_const[:, 10 * d, :], gate(G_LOG)[:, 32 * d:32 * d + 32],
                                 start=True, stop=True)
            nc.tensor.matmul(ps[:, 2, 0:64], const("ones"), gate(G_LOG), start=True, stop=True).then_inc(gg_sum, 1)

        def gdn_gates_dve(dve):
            steps = [0]

            def step(ins):
                steps[0] += 1
                ins.then_inc(gg, 1)
                dve.wait_ge(gg, steps[0])

            dve.wait_ge(gg_tr, 1)
            a_part = ps[:, 0, 0:P].rearrange("p (c x) -> p c x", x=16)[:, :, 0:8].rearrange("p c (d h) -> p d c h", d=2)
            b_part = ps[:, 0, 0:P].rearrange("p (c x) -> p c x", x=16)[:, :, 8:16].rearrange("p c (d h) -> p d c h", d=2)
            bias = param("dt_bias", 0, 8).rearrange("p (d h) -> p d h", d=2)
            for d in range(2):
                step(nc.vector.tensor_tensor(g_gates[:, G_LOG, d], a_part[:, d],
                                             bias[:, d].unsqueeze(1).to_broadcast([P, TC, GH]), ALU.add))
            step(nc.vector.tensor_scalar(gate(G_TMP), gate(G_LOG), -1.0, None, ALU.mult))
            step(nc.vector.tensor_tensor(gate(G_TMP), gate(G_TMP), gate(G_LOG), ALU.min))
            for d in range(2):
                step(nc.vector.tensor_scalar(g_gates[:, G_BETA, d], b_part[:, d], -1.0, 85.0, ALU.mult, ALU.min))
            dve.wait_ge(gg_act, 3)
            step(nc.vector.scalar_tensor_tensor(gate(G_TMP), gate(G_LOG), 0.0, gate(G_TMP), op0=ALU.max, op1=ALU.add))
            nexp = g_alog[:, :].rearrange("p (d h) -> p d h", d=2)
            for d in range(2):
                ins = nc.vector.scalar_tensor_tensor(g_gates[:, G_LOG, d], g_gates[:, G_TMP, d], -1.0,
                                                     nexp[:, d].unsqueeze(1).to_broadcast([P, TC, GH]),
                                                     op0=ALU.mult, op1=ALU.mult)
                if d == 1:
                    step(ins)
            step(nc.vector.tensor_scalar(gate(G_BETA), gate(G_BETA), 1.0, None, ALU.add))
            step(nc.vector.reciprocal(gate(G_BETA), gate(G_BETA)))
            dve.wait_ge(gg_sum, 1)
            step(nc.vector.tensor_copy(gate(G_CUM), ps[:, 1, 0:64]))
            step(nc.vector.tensor_copy(gate(G_TOT), ps[:, 2, 0:64]))
            step(nc.vector.tensor_tensor(gate(G_KDEC), gate(G_TOT), gate(G_CUM), ALU.subtract))
            dve.wait_ge(gg_act, 6)
            step(nc.vector.tensor_scalar(gate(G_NEGDEC), gate(G_NEGDEC), -1.0, None, ALU.mult))
            nc.vector.memset(mixT[:, 0:GH, :], 0.0).then_inc(gg_ready, 1)

        def gdn_gates_act(act):
            act.wait_ge(gg, 6)
            nc.scalar.activation(gate(G_TMP), gate(G_TMP), ACT.Exp).then_inc(gg_trc, 1)
            nc.scalar.activation(gate(G_BETA), gate(G_BETA), ACT.Exp).then_inc(gg_act, 1)
            nc.scalar.activation(g_alog[:, :], param("a_log", 0, 8), ACT.Exp).then_inc(gg_act, 1)
            act.wait_ge(gg_trc, 1)
            nc.scalar.activation(gate(G_TMP), gate(G_TMP), ACT.Ln, bias=param("one")).then_inc(gg_act, 1)
            act.wait_ge(gg, 13)
            nc.scalar.activation(gate(G_NEGDEC), gate(G_CUM), ACT.Exp).then_inc(gg_act, 1)
            nc.scalar.activation(gate(G_KDEC), gate(G_KDEC), ACT.Exp).then_inc(gg_act, 1)
            nc.scalar.activation(gate(G_LAST), gate(G_TOT), ACT.Exp).then_inc(gg_act, 1)

        def gdn_prep_dve(dve):
            with dve.Fori(0, GH) as h:
                for j in range(2):
                    dve.wait_ge(gp_rs, 2 * h + (j + 1))
                    out = g_qT[:, bass.ds(h, 1), :].rearrange("p o t -> p (o t)") if j == 0 else g_kn[:, :]
                    nc.vector.scalar_tensor_tensor(out, g_act[j][:, :], float(P) ** -0.5 if j == 0 else 1.0, g_rs[j][:, :],
                                                   op0=ALU.mult, op1=ALU.mult).then_inc(gp_norm, 1)

        def gdn_prep_act(act):
            nc.scalar.activation(g_rs[0][:, 0:1], param("zero"), ACT.Copy).then_inc(gp_end, 1)
            with act.Fori(0, GH) as h:
                for j in range(3):
                    act.wait_ge(gp_in[j], 16 * h + 16)
                    nc.scalar.activation(g_act[j][:, :], g_in[j][:, :], ACT.Silu).then_inc(gp_silu, 1)
                act.preload_act_table_set(LOG_EXP)
                for j in range(2):
                    act.wait_ge(gp_silu, 3 * h + (j + 1))
                    nc.scalar.activation(g_sq[j][:, :], g_act[j][:, :], ACT.Square).then_inc(gp_sq, 1)
                for j in range(2):
                    act.wait_ge(gp_sum, 2 * h + (j + 1))
                    nc.scalar.activation(g_rs[j][:, :], banks(2 * j), ACT.Ln, bias=param("eps6")).then_inc(gp_ln, 1)
                for j in range(2):
                    act.wait_ge(gp_ln, 2 * h + (j + 1))
                    nc.scalar.activation(g_rs[j][:, :], g_rs[j][:, :], ACT.Exp, scale=-0.5).then_inc(gp_rs, 1)
                head = bass.ds(h, 1)
                act.wait_ge(gp_tr, 2 * h + 1)
                nc.scalar.activation(g_vt[:, :, head, :].rearrange("p c o t -> p c (o t)"),
                                     banks(6).rearrange("p (c t) -> p c t", t=P), ACT.Copy)
                act.wait_ge(gp_norm, 2 * h + 2)
                nc.scalar.activation(g_kT[:, head, :].rearrange("p o t -> p (o t)"), g_kn[:, :], ACT.Copy)
                act.wait_ge(gp_tr, 2 * h + 2)
                nc.scalar.activation(g_kt[:, :, head, :].rearrange("p c o t -> p c (o t)"),
                                     banks(4).rearrange("p (c t) -> p c t", t=P), ACT.Copy).then_inc(gp_end, 1)

        def gdn_prep_pe(pe):
            with pe.Fori(0, GH) as h:
                for j in range(2):
                    pe.wait_ge(gp_end, h + 1)
                    pe.wait_ge(gp_sq, 2 * h + (j + 1))
                    for b in range(2):
                        last = nc.tensor.matmul(ps[:, 2 * j + b, :], const("ones"), g_sq[j][:, b * HALF:(b + 1) * HALF],
                                                start=True, stop=True)
                    last.then_inc(gp_sum, 1)
                pe.wait_ge(gp_silu, 3 * h + 3)
                for c in range(TC):
                    last = nc.tensor.transpose(banks(6)[:, c * P:(c + 1) * P], g_act[2][:, c * P:(c + 1) * P], const("ident"))
                last.then_inc(gp_tr, 1)
                pe.wait_ge(gp_norm, 2 * h + 2)
                for c in range(TC):
                    last = nc.tensor.transpose(banks(4)[:, c * P:(c + 1) * P], g_kn[:, c * P:(c + 1) * P], const("ident"))
                last.then_inc(gp_tr, 1)

        gs_names = ["gu", "kc", "row", "diff", "dec", "gam", "eg", "kk", "kq", "A", "qk", "qd", "kd", "off", "D", "Dt", "Q", "Qs",
                    "X1", "X2", "kS", "r1", "R", "V", "vn", "o", "su", "end"]
        gs = {name: sem(f"gs_{name}") for name in gs_names}
        NL = GDN_LEVELS

        def chunk_of(n, d):
            return n if d == 0 else n * -1 + (TC - 1)

        def gate_of(n, d):
            return 4 * n if d == 0 else n * -4 + (32 + 4 * (TC - 1))

        def once(n, d):
            return 2 * n + (d + 1)

        def level(n, d, l):
            return 2 * NL * n + (2 * l + d + 1)

        def four(t):
            return t.rearrange("p h x -> p (h x)")

        def pbank(b):
            return ps[:, b, :].rearrange("p (h x) -> p h x", h=GH)

        def gmask(d, j):
            return g_const[:, 10 * d + j, :].unsqueeze(1).to_broadcast([P, GH, P])

        def gcols(i, n, d):
            return gate(i)[:, bass.ds(gate_of(n, d), GH)].unsqueeze(2).to_broadcast([P, GH, P])

        def gcol(i, n, d, h):
            return gate(i)[:, bass.ds(gate_of(n, d) + h, 1)]

        def halves(t, l, which):
            return t.rearrange("p h (n a b) -> p h n a b", a=2, b=1 << l)[:, :, :, which, :]

        ident4 = const("ident").unsqueeze(1).to_broadcast([P, GH, P])

        def gdn_loop_pe(pe):
            def heads(b, lhsT, rhs, start=True, stop=True):
                for h in range(GH):
                    last = nc.tensor.matmul(pbank(b)[:, h, :], lhsT[:, h, :], rhs[:, h, :], start=start, stop=stop)
                return last

            def half_heads(b, lhsT, rhs, l, which):
                for h in range(GH):
                    last = nc.tensor.matmul(halves(pbank(b), l, which)[:, h], lhsT[:, h, :], halves(rhs[:, :, :], l, which)[:, h],
                                            start=True, stop=True)
                return last

            with pe.Fori(0, TC) as n:
                toks = [bass.ds(P * chunk_of(n, d), P) for d in range(2)]
                for d in range(2):
                    pe.wait_ge(gs["gu"], once(n, d))
                    nc.tensor.matmul(ps[:, 4 * d, :], const("ones"), four(g_gu[d][:, :, :]), start=True, stop=True)\
                        .then_inc(gs["row"], 1)
                    pe.wait_ge(gs["kc"], once(n, d))
                    heads(4 * d + 1, g_kc[d], g_kc[d]).then_inc(gs["kk"], 1)
                    heads(4 * d + 2, g_kc[d], g_qT[:, :, toks[d]]).then_inc(gs["kq"], 1)
                for l in range(NL):
                    for d in range(2):
                        pe.wait_ge(gs["off"], level(n, d, l))
                        if l:
                            pe.wait_ge(gs["Dt"], level(n, d, l - 1))
                        for h in range(GH):
                            rhs = g_Dt[d][:, h, :] if l else const("ident")
                            last = nc.tensor.matmul(pbank(4 * d + 1)[:, h, :], g_off[d][:, l % 2, h, :], rhs, start=True, stop=True)
                        last.then_inc(gs["Q"], 1)
                    if l == 0:
                        continue
                    for d in range(2):
                        pe.wait_ge(gs["Qs"], 2 * (NL - 1) * n + (2 * (l - 1) + d + 1))
                        pe.wait_ge(gs["D"], 2 * (NL - 1) * n + (2 * (l - 1) + d + 1))
                        if l == 1:
                            pe.wait_ge(gs["qk"], once(n, d))
                        half_heads(4 * d + 2, g_D[d], g_gu[d], l, 1 - d).then_inc(gs["X1"], 1)
                        if l < NL - 1:
                            half_heads(4 * d + 3, g_gu[d], g_D[d], l, d).then_inc(gs["X2"], 1)
                for d in range(2):
                    pe.wait_ge(gs["qd"], once(n, d))
                    heads(4 * d, g_kc[d], g_S[d]).then_inc(gs["kS"], 1)
                for d in range(2):
                    pe.wait_ge(gs["R"], once(n, d))
                    pe.wait_ge(gs["Dt"], level(n, d, NL - 1))
                    heads(4 * d + 1, g_Dt[d], g_A[d]).then_inc(gs["V"], 1)
                for d in range(2):
                    pe.wait_ge(gs["vn"], once(n, d))
                    pe.wait_ge(gs["kd"], once(n, d))
                    for h in range(GH):
                        o = pbank(4 * d + 2)[:, h, :]
                        nc.tensor.matmul(o, g_S[d][:, h, :], g_qd[d][:, h, :], start=True, stop=False)
                        last = nc.tensor.matmul(o, g_vn[d][:, h, :], g_gam[d][:, 0, h, :], start=False, stop=True)
                    last.then_inc(gs["o"], 1)
                    heads(4 * d + 3, g_kd[d], g_vn[d]).then_inc(gs["su"], 1)

        def gdn_loop_act(act):
            with act.Fori(0, TC) as n:
                for d in range(2):
                    act.wait_ge(gs["end"], once(n, d))
                    nc.scalar.activation(g_kc[d][:, :, :], g_kT[:, :, bass.ds(P * chunk_of(n, d), P)], ACT.Copy)\
                        .then_inc(gs["kc"], 1)
                for d in range(2):
                    act.wait_ge(gs["row"], once(n, d))
                    nc.scalar.activation(four(g_qd[d][:, :, :]), ps[:, 4 * d, :], ACT.Exp).then_inc(gs["eg"], 1)
                for d in range(2):
                    act.wait_ge(gs["dec"], once(n, d))
                    nc.scalar.activation(g_gam[d][:, :, :, :].rearrange("p a h x -> p (a h x)"),
                                         g_gam[d][:, :, :, :].rearrange("p a h x -> p (a h x)"), ACT.Exp).then_inc(gs["gam"], 1)
                for l in range(1, NL):
                    for d in range(2):
                        act.wait_ge(gs["Q"], level(n, d, l))
                        nc.scalar.activation(four(g_gu[d][:, :, :]), ps[:, 4 * d + 1, :], ACT.Copy).then_inc(gs["Qs"], 1)
                for d in range(2):
                    act.wait_ge(gs["V"], once(n, d))
                    nc.scalar.activation(four(g_vn[d][:, :, :]), ps[:, 4 * d + 1, :], ACT.Copy).then_inc(gs["vn"], 1)

        def gdn_loop_pool(pool):
            with pool.Fori(0, TC) as n:
                for l in range(NL):
                    for d in range(2):
                        if l == 0:
                            pool.wait_ge(gs["A"], once(n, d))
                        if l >= 2:
                            pool.wait_ge(gs["Q"], level(n, d, l - 2))
                        if l == 2:
                            pool.wait_ge(gs["D"], 2 * (NL - 1) * n + (d + 1))
                        nc.gpsimd.tensor_tensor(g_off[d][:, l % 2], g_A[d][:, :, :], gmask(d, 3 + l), ALU.mult)\
                            .then_inc(gs["off"], 1)

        def gdn_loop_dve(dve):
            dve.wait_ge(gp_end, GH + 1)
            for d in range(2):
                nc.vector.memset(g_S[d][:, :, :], 0.0).then_inc(gs["end"], 1)
            with dve.Fori(0, TC) as n:
                toks = [bass.ds(P * chunk_of(n, d), P) for d in range(2)]
                for d in range(2):
                    dve.wait_ge(gs["end"], once(n, d))
                    nc.vector.tensor_tensor(g_gu[d][:, :, :], gmask(d, 0), gcols(G_LOG, n, d), ALU.mult).then_inc(gs["gu"], 1)
                for d in range(2):
                    nc.vector.tensor_tensor(g_kd[d][:, :, :], g_kt[:, bass.ds(chunk_of(n, d), 1)].rearrange("p o h x -> p (o h) x"),
                                            gcols(G_KDEC, n, d), ALU.mult).then_inc(gs["kd"], 1)
                for d in range(2):
                    dve.wait_ge(gs["eg"], once(n, d))
                    nc.vector.tensor_tensor(g_gam[d][:, 0], pbank(4 * d), gcols(G_CUM, n, d), ALU.subtract).then_inc(gs["diff"], 1)
                    dve.wait_ge(gs["diff"], 2 * once(n, d) - 1)
                    nc.vector.tensor_tensor(g_gam[d][:, 1], gmask(d, 2), g_gam[d][:, 0], ALU.subtract).then_inc(gs["diff"], 1)
                    dve.wait_ge(gs["diff"], 2 * once(n, d))
                    nc.vector.tensor_tensor(g_gam[d][:, 0], g_gam[d][:, 0], gmask(d, 1), ALU.add).then_inc(gs["dec"], 1)
                for d in range(2):
                    dve.wait_ge(gs["gam"], once(n, d))
                    dve.wait_ge(gs["kk"], once(n, d))
                    for h in range(GH):
                        ins = nc.vector.scalar_tensor_tensor(g_A[d][:, h, :], pbank(4 * d + 1)[:, h, :], gcol(G_BETA, n, d, h),
                                                             g_gam[d][:, 1, h, :], op0=ALU.mult, op1=ALU.mult)
                    ins.then_inc(gs["A"], 1)
                for d in range(2):
                    dve.wait_ge(gs["kq"], once(n, d))
                    nc.vector.tensor_tensor(g_gam[d][:, 0], pbank(4 * d + 2), g_gam[d][:, 0], ALU.mult).then_inc(gs["qk"], 1)
                    nc.vector.tensor_tensor(g_qd[d][:, :, :], g_qd[d][:, :, :], g_qT[:, :, toks[d]], ALU.mult).then_inc(gs["qd"], 1)
                for d in range(2):
                    dve.wait_ge(gs["off"], level(n, d, 0))
                    nc.vector.tensor_tensor(g_D[d][:, :, :], ident4, g_off[d][:, 0], ALU.subtract).then_inc(gs["D"], 1)
                for d in range(2):
                    dve.wait_ge(gs["Q"], level(n, d, 0))
                    nc.vector.tensor_tensor(g_Dt[d][:, :, :], ident4, pbank(4 * d + 1), ALU.subtract).then_inc(gs["Dt"], 1)
                for l in range(1, NL):
                    for d in range(2):
                        dve.wait_ge(gs["X1"], 2 * (NL - 1) * n + (2 * (l - 1) + d + 1))
                        part = halves(g_Dt[d][:, :, :], l, 1 - d)
                        nc.vector.tensor_tensor(part, part, halves(pbank(4 * d + 2), l, 1 - d), ALU.subtract).then_inc(gs["Dt"], 1)
                        if l < NL - 1:
                            dve.wait_ge(gs["X2"], 2 * (NL - 2) * n + (2 * (l - 1) + d + 1))
                            part = halves(g_D[d][:, :, :], l, d)
                            nc.vector.tensor_tensor(part, part, halves(pbank(4 * d + 3), l, d), ALU.subtract).then_inc(gs["D"], 1)
                for d in range(2):
                    dve.wait_ge(gs["kS"], once(n, d))
                    dve.wait_ge(gs["off"], level(n, d, NL - 1))
                    v = g_vt[:, bass.ds(chunk_of(n, d), 1)].rearrange("p o h x -> p (o h) x")
                    for h in range(GH):
                        ins = nc.vector.scalar_tensor_tensor(g_A[d][:, h, :], pbank(4 * d)[:, h, :], gcol(G_NEGDEC, n, d, h),
                                                             v[:, h, :], op0=ALU.mult, op1=ALU.add)
                    ins.then_inc(gs["r1"], 1)
                    dve.wait_ge(gs["r1"], once(n, d))
                    nc.vector.tensor_tensor(g_A[d][:, :, :], g_A[d][:, :, :], gcols(G_BETA, n, d), ALU.mult).then_inc(gs["R"], 1)
                for d in range(2):
                    dve.wait_ge(gs["o"], once(n, d))
                    out = mixT[:, 0:GH, toks[d]]
                    nc.vector.tensor_tensor(out, out, pbank(4 * d + 2), ALU.add)
                    dve.wait_ge(gs["su"], once(n, d))
                    for h in range(GH):
                        ins = nc.vector.scalar_tensor_tensor(g_S[d][:, h, :], g_S[d][:, h, :], gcol(G_LAST, n, d, h),
                                                             pbank(4 * d + 3)[:, h, :], op0=ALU.mult, op1=ALU.add)
                    ins.then_inc(gs["end"], 1)

        go_z = sem("go_z")
        go_silu = sem("go_silu")
        go_sq = sem("go_sq")
        go_sum = sem("go_sum")
        go_ln = sem("go_ln")
        go_rs = sem("go_rs")
        go_norm = sem("go_norm")
        go_end = sem("go_end")
        gout = Region(arena + 2 * GH * T * 4, ops_end)
        g_z = gout.take("g_z", [P, GH, T])
        g_osq = [gout.take(f"g_osq{j}", [P, T]) for j in range(2)]
        g_ors = [gout.take(f"g_ors{j}", [P, T]) for j in range(2)]

        def gdn_out_sp(sp):
            sp.wait_ge(gs["end"], 2 * TC + 2)
            sp.dma_start(g_z[:, :, :], g["h1"][3 * GH * P:4 * GH * P, :].rearrange("(h p) t -> p h t", p=P)).then_inc(go_z, 16)

        def gdn_out_pe(pe):
            for h in range(GH):
                pe.wait_ge(go_sq, h + 1)
                if h >= 2:
                    pe.wait_ge(go_ln, h - 1)
                for b in range(2):
                    last = nc.tensor.matmul(ps[:, 2 * (h % 2) + b, :], const("ones"), g_osq[h % 2][:, b * HALF:(b + 1) * HALF],
                                            start=True, stop=True)
                last.then_inc(go_sum, 1)

        def gdn_out_act(act):
            act.wait_ge(go_z, 16)
            for h in range(GH):
                nc.scalar.activation(g_z[:, h, :], g_z[:, h, :], ACT.Silu).then_inc(go_silu, 1)
            act.preload_act_table_set(LOG_EXP)
            act.wait_ge(gs["end"], 2 * TC + 2)
            def square(h):
                if h >= 2:
                    act.wait_ge(go_sum, h - 1)
                nc.scalar.activation(g_osq[h % 2][:, :], mixT[:, h, :], ACT.Square).then_inc(go_sq, 1)

            square(0)
            for h in range(GH):
                if h + 1 < GH:
                    square(h + 1)
                act.wait_ge(go_sum, h + 1)
                if h >= 2:
                    act.wait_ge(go_norm, h - 1)
                nc.scalar.activation(g_ors[h % 2][:, :], banks(2 * (h % 2)), ACT.Ln, bias=param("eps6"), scale=1.0 / P)\
                    .then_inc(go_ln, 1)
                act.wait_ge(go_ln, h + 1)
                nc.scalar.activation(g_ors[h % 2][:, :], g_ors[h % 2][:, :], ACT.Exp, scale=-0.5).then_inc(go_rs, 1)

        def gdn_out_dve(dve):
            for h in range(GH):
                dve.wait_ge(go_rs, h + 1)
                nc.vector.scalar_tensor_tensor(mixT[:, h, :], mixT[:, h, :], param("gdn_g"), g_ors[h % 2][:, :],
                                               op0=ALU.mult, op1=ALU.mult).then_inc(go_norm, 1)
                dve.wait_ge(go_norm, h + 1)
                dve.wait_ge(go_silu, h + 1)
                nc.vector.tensor_tensor(mixT[:, h, :], mixT[:, h, :], g_z[:, h, :], ALU.mult).then_inc(go_end, 1)

        at_names = ["load", "prep", "prepc", "zq", "s", "sc", "max", "neg", "p", "pt", "ptc", "av", "rs", "z", "sq", "ss", "ln", "r",
                    "zs", "o", "end", "bias"]
        at = {name: sem(f"at_{name}") for name in at_names}

        NP = NH1 // 2
        BAND = KR * GRID
        NA0 = 4 * GH * P + 16
        nop = Region(arena, ops_end)
        n_q = nop.take("n_q", [P, NP, T])
        n_k = nop.take("n_k", [P, NP, T])
        n_v = nop.take("n_v", [P, ROWS - 1, NP * P])
        nwk = Region(mix_end, end)
        n_bias = nwk.take("n_bias", [P, NP, 2 * KR - 1, GRID])
        n_mask = nwk.take("n_mask", [P, GRID])
        n_zq = nwk.take("n_zq", [P, NP, P])
        n_z = nwk.take("n_z", [P, NP, P])
        n_zsq = nwk.take("n_zsq", [P, NP, GRID])
        n_pt = [nwk.take(f"n_pt{j}", [P, KR // 2, P]) for j in range(2)]
        n_small = nwk.take("n_small", [P, 8, NP])
        N_MAX, N_NEG, N_SUM, N_INV, N_SS, N_LN, N_R = range(7)
        scores = Region(nwk.at, end)
        n_s = scores.take("n_s", [P, NP, BAND])
        n_p = scores.take("n_p", [P, NP, BAND])
        n_vT = Region(nwk.at, end).take("n_vT", [P, NP, T])
        NA_END = {}

        RPB_W = 2 * KC - 1 + 2 * 48
        RPB = (2 * KR - 1) * RPB_W

        def na_bias_sp(sp):
            sp.dma_start(g["rpb_rows"], g["rpb"].unsqueeze(1).to_broadcast([NH1, GRID, RPB])).then_inc(at["bias"], 16)

        def na_sp(sp):
            def rows(first):
                return g["h1"][first:first + NP * P, :].rearrange("(c p) t -> p c t", p=P)

            sp.dma_start(n_vT[:, :, :], rows(NA0 + 2 * NP * P)).then_inc(at["load"], 16)
            sp.dma_start(n_q[:, :, :], rows(NA0)).then_inc(at["load"], 16)
            sp.dma_start(n_k[:, :, :], rows(NA0 + NP * P)).then_inc(at["load"], 16)
            sp.dma_start(n_mask[:, :], g["na_mask"]).then_inc(at["bias"], 16)
            sp.wait_ge(at["bias"], 32)
            for h in range(NH1):
                src = bass.AP(g["rpb_rows"].tensor, g["rpb_rows"].offset + h * GRID * RPB + GRID - 1,
                              [[RPB - 1, GRID], [RPB_W, 2 * KR - 1], [1, GRID]])
                sp.dma_start(n_bias[GRID * (h % 2):GRID * (h % 2) + GRID, h // 2], src).then_inc(at["bias"], 16)

        def na_pe(pe):
            pe.wait_ge(at["load"], 48)
            for i in range(ROWS - 1):
                if i >= 2:
                    pe.wait_ge(at["prepc"], i - 1)
                for c in range(NP):
                    last = nc.tensor.transpose(ps[:, 4 + i % 2, c * P:(c + 1) * P], n_vT[:, c, GRID * i:GRID * i + P], const("ident"))
                last.then_inc(at["prep"], 1)
            pe.wait_ge(at["prepc"], ROWS - 1)

            def scores_of(r, r0, first):
                pe.wait_ge(at["zq"], r + 1)
                if not first:
                    pe.wait_ge(at["sc"], NP * r)
                for c in range(NP):
                    nc.tensor.matmul(ps[:, c, :], n_zq[:, c, :], n_k[:, c, bass.ds(r0 * GRID, BAND)], start=True, stop=True)\
                        .then_inc(at["s"], 1)

            def turn(r, c):
                pe.wait_ge(at["p"], NP * r + (c + 1))
                if c >= 2:
                    pe.wait_ge(at["ptc"], NP * r + (c - 1))
                for t in range(KR // 2):
                    last = nc.tensor.transpose(ps[:, 4 + c % 2, t * P:(t + 1) * P], n_p[:, c, t * P:(t + 1) * P], const("ident"))
                last.then_inc(at["pt"], 1)

            def weigh(r, r0, c):
                pe.wait_ge(at["ptc"], NP * r + (c + 1))
                for t in range(KR // 2):
                    v = n_v[:, bass.ds(r0 + 2 * t, 1), c * P:(c + 1) * P].rearrange("p o x -> p (o x)")
                    last = nc.tensor.matmul(ps[:, 6, c * P:(c + 1) * P], n_pt[c % 2][:, t, :], v,
                                            start=(t == 0), stop=(t == KR // 2 - 1))
                last.then_inc(at["av"], 1)

            def rows(new, old, older):
                if old is not None:
                    turn(old[0], 0)
                    turn(old[0], 1)
                if new is not None:
                    scores_of(new[0], new[1], old is None)
                if older is not None:
                    pe.wait_ge(at["zs"], older + 1)
                    for c in range(NP):
                        last = nc.tensor.matmul(ps[:, 7, c * GRID:(c + 1) * GRID], n_z[:, c, :], const("fold"), start=True, stop=True)
                    last.then_inc(at["o"], 1)
                if old is None:
                    return
                for c in range(NP):
                    weigh(old[0], old[1], c)
                    if c + 2 < NP:
                        turn(old[0], c + 2)

            na_rows(pe, rows)

        def na_rows(eng, rows):
            def top(r):
                return (r, r * 0, r * -1 + (KR - 1))

            def middle(r):
                return (r, r + -(KR // 2), r * 0 + (KR // 2 - 1))

            def bottom(r):
                return (r, r * 0 + (ROWS - KR), r * -1 + (ROWS - 1))

            first, last = KR // 2, ROWS - KR // 2
            rows(top(0), None, None)
            rows(top(1), top(0), None)
            with eng.Fori(2, first) as r:
                rows(top(r), top(r + -1), r + -2)
            rows(middle(first), top(first - 1), first - 2)
            with eng.Fori(first + 1, last) as r:
                rows(middle(r), middle(r + -1), r + -2)
            rows(bottom(last), middle(last - 1), last - 2)
            with eng.Fori(last + 1, ROWS) as r:
                rows(bottom(r), bottom(r + -1), r + -2)
            rows(None, bottom(ROWS - 1), ROWS - 2)
            rows(None, None, ROWS - 1)

        def diagonals(t, width):
            return [(slice(GRID * j, GRID * j + GRID), t[GRID * j:GRID * j + GRID, :, width * j:width * (j + 1)]) for j in range(2)]

        def na_act(act):
            act.wait_ge(go_end, GH)
            for i in range(ROWS - 1):
                act.wait_ge(at["prep"], i + 1)
                nc.scalar.activation(n_v[:, i, :], ps[:, 4 + i % 2, :], ACT.Copy).then_inc(at["prepc"], 1)
            act.wait_ge(at["end"], 1)

            def queries(r, first):
                if not first:
                    act.wait_ge(at["s"], NP * r)
                for j, (part, block) in enumerate(diagonals(n_zq, GRID)):
                    ins = nc.scalar.activation(block, n_q[part, :, bass.ds(r * GRID, GRID)], ACT.Copy)
                ins.then_inc(at["zq"], 1)

            def features(older):
                act.wait_ge(at["o"], older + 1)
                nc.scalar.activation(mixT[:, GH:DC, bass.ds(older * GRID, GRID)], ps[:, 7, 0:NP * GRID].rearrange("p (c x) -> p c x", c=NP),
                                     ACT.Copy, scale=param("na_g")).then_inc(at["end"], 1)

            def rows(new, old, older):
                if new is not None:
                    queries(new[0], old is None)
                if old is None and older is not None:
                    features(older)
                if old is not None:
                    r = old[0]
                    for c in range(NP):
                        act.wait_ge(at["pt"], NP * r + (c + 1))
                        if c >= 2:
                            act.wait_ge(at["av"], NP * r + (c - 1))
                        nc.scalar.activation(n_pt[c % 2][:, :, :].rearrange("p t x -> p (t x)"), ps[:, 4 + c % 2, :], ACT.Copy)\
                            .then_inc(at["ptc"], 1)
                        if c == 1 and older is not None:
                            features(older)
                if new is not None:
                    act.wait_ge(at["neg"], new[0] + 1)
                    for c in range(NP):
                        nc.scalar.activation(n_p[:, c, :], n_s[:, c, :], ACT.Exp, bias=n_small[:, N_NEG, c:c + 1],
                                             accum_out=n_small[:, N_SUM, c:c + 1]).then_inc(at["p"], 1)
                if old is None:
                    return
                act.wait_ge(at["ss"], r + 1)
                nc.scalar.activation(n_small[:, N_LN, :], n_small[:, N_SS, :], ACT.Ln, bias=param("eps6"), scale=1.0 / GRID)\
                    .then_inc(at["ln"], 1)
                act.wait_ge(at["ln"], r + 1)
                nc.scalar.activation(n_small[:, N_R, :], n_small[:, N_LN, :], ACT.Exp, scale=-0.5).then_inc(at["r"], 1)

            na_rows(act, rows)

        def na_dve(dve):
            dve.wait_ge(go_end, GH)
            nc.vector.memset(n_zq[:, :, :], 0.0)
            nc.vector.memset(n_z[:, :, :], 0.0).then_inc(at["end"], 1)
            dve.wait_ge(at["bias"], 16 * (NH1 + 2))
            flat = n_bias[:, :, :, :].rearrange("p c r x -> p (c r) x")
            nc.vector.tensor_tensor(flat, flat, n_mask[:, :].unsqueeze(1).to_broadcast([P, NP * (2 * KR - 1), GRID]), ALU.add)\
                .then_inc(at["bias"], 1)
            dve.wait_ge(at["bias"], 16 * (NH1 + 2) + 1)
            dve.wait_ge(at["prepc"], ROWS - 1)

            def rows(new, old, older):
                if old is not None:
                    r = old[0]
                    dve.wait_ge(at["p"], NP * r + NP)
                    nc.vector.reciprocal(n_small[:, N_INV, :], n_small[:, N_SUM, :]).then_inc(at["rs"], 1)
                if new is not None:
                    for c in range(NP):
                        dve.wait_ge(at["s"], NP * new[0] + (c + 1))
                        nc.vector.scalar_tensor_tensor(
                            n_s[:, c, :], ps[:, c, :], float(GRID) ** -0.5,
                            n_bias[:, c, bass.ds(new[2], KR), :].rearrange("p r x -> p (r x)"), op0=ALU.mult, op1=ALU.add)\
                            .then_inc(at["sc"], 1)
                    dve.wait_ge(at["sc"], NP * new[0] + NP)
                    nc.vector.tensor_reduce(n_small[:, N_MAX, :], n_s[:, :, :], AX.X, ALU.max).then_inc(at["max"], 1)
                    dve.wait_ge(at["max"], new[0] + 1)
                    nc.vector.tensor_scalar(n_small[:, N_NEG, :], n_small[:, N_MAX, :], -1.0, None, ALU.mult).then_inc(at["neg"], 1)
                if old is None:
                    return
                dve.wait_ge(at["rs"], r + 1)
                dve.wait_ge(at["av"], NP * r + NP)
                dve.wait_ge(at["end"], r + 1)
                out = ps[:, 6, :].rearrange("p (c x) -> p c x", c=NP)
                for j, (part, block) in enumerate(diagonals(n_z, GRID)):
                    inv = n_small[part, N_INV, :].unsqueeze(2).to_broadcast([GRID, NP, GRID])
                    ins = nc.vector.tensor_tensor(block, out[part, :, GRID * j:GRID * j + GRID], inv, ALU.mult)
                ins.then_inc(at["z"], 1)
                dve.wait_ge(at["z"], r + 1)
                for part, block in diagonals(n_z, GRID):
                    ins = nc.vector.tensor_tensor(n_zsq[part, :, :], block, block, ALU.mult)
                ins.then_inc(at["sq"], 1)
                dve.wait_ge(at["sq"], r + 1)
                nc.vector.tensor_reduce(n_small[:, N_SS, :], n_zsq[:, :, :], AX.X, ALU.add).then_inc(at["ss"], 1)
                dve.wait_ge(at["r"], r + 1)
                for part, block in diagonals(n_z, GRID):
                    inv = n_small[part, N_R, :].unsqueeze(2).to_broadcast([GRID, NP, GRID])
                    ins = nc.vector.tensor_tensor(block, block, inv, ALU.mult)
                ins.then_inc(at["zs"], 1)

            na_rows(dve, rows)

        HQ, KV, GQ, HD, WIN = 8, 2, 4, 64, 128
        sop = Region(arena, ops_end)
        s_q = sop.take("s_q", [P, GQ, T])
        s_k = sop.take("s_k", [P, WIN + T])
        s_v = sop.take("s_v", [P, TC + 1, P])
        s_bias = [sop.take(f"s_bias{j}", [P, HQ, 2 * WIN]) for j in range(2)]
        s_zq = sop.take("s_zq", [P, GQ, KV, P])
        s_s = sop.take("s_s", [P, HQ, 2 * WIN])
        s_pt = [sop.take(f"s_pt{j}", [P, 4, P]) for j in range(2)]
        s_a = sop.take("s_a", [P, HQ, HD])
        s_small = sop.take("s_small", [P, 12, HQ])
        S_MAX, S_NEG, S_SUM, S_SINK, S_INV, S_SS, S_LN, S_R, S_M = range(9)
        swk = Region(ops_end, ops_end + 4 * T * 4)
        s_qsq = [swk.take(f"s_qsq{j}", [P, T]) for j in range(2)]
        s_qrs = [swk.take(f"s_qrs{j}", [P, T]) for j in range(2)]
        cwk = Region(mix_end, end)
        s_mask = cwk.take("s_mask", [P, 2, 2 * WIN])
        s_vT = cwk.take("s_vT", [P, T])
        s_t5 = cwk.take("s_t5", [32, 384])
        s_rel = cwk.take("s_rel", [32, HQ])
        s_rows = cwk.take("s_rows", [HQ, 384])

        a0 = {name: 0 for name in at_names}
        a0.update({"load": 48, "prep": ROWS - 1, "prepc": ROWS - 1, "bias": 16 * (NH1 + 2) + 1, "end": ROWS + 1})
        a0.update({name: ROWS for name in ["zq", "max", "neg", "rs", "z", "sq", "ss", "ln", "r", "zs", "o"]})
        a0.update({name: NP * ROWS for name in ["s", "sc", "p", "pt", "ptc", "av"]})
        sq_sq, sq_sum, sq_ln, sq_rs, sq_done = (sem(f"sq_{name}") for name in ["sq", "sum", "ln", "rs", "done"])
        s_pads = sem("s_pads")
        s_rowed = sem("s_rowed")
        NQK = GQ + 1

        def swa_sp(sp):
            proj_stored(sp, proj2)
            layer_read(sp, proj2)
            h2 = g["h2"]
            sp.dma_start(s_t5[:, :], g["t5"]).then_inc(at["load"], 16)
            sp.dma_start(s_rel[:, :], g["rel_bias"]).then_inc(at["load"], 16)
            for v in range(KV):
                sp.dma_start(s_q[HD * v:HD * v + HD, :, :],
                             h2[v * GQ * HD:(v + 1) * GQ * HD, :].rearrange("(g p) t -> p g t", p=HD)).then_inc(at["load"], 16)
            sp.dma_start(s_k[:, WIN:WIN + T], h2[HQ * HD:HQ * HD + P, :]).then_inc(at["load"], 16)
            sp.dma_start(s_vT[:, :], h2[HQ * HD + P:HQ * HD + 2 * P, :]).then_inc(at["load"], 16)
            sp.dma_start(s_mask[:, :, :], g["swa_mask"]).then_inc(at["load"], 16)
            conv_sp(sp)
            sp.wait_ge(s_rowed, 2)
            sp.dma_start(g["t5_rows"], s_rows[:, :].unsqueeze(1).to_broadcast([HQ, P, 384])).then_inc(s_rowed, 16)
            sp.wait_ge(s_rowed, 18)
            for j in range(2):
                src = bass.AP(g["t5_rows"].tensor, g["t5_rows"].offset + P - 1, [[384 - 1, P], [P * 384, HQ], [1, 2 * WIN]])
                sp.dma_start(s_bias[j][:, :, :], src).then_inc(at["bias"], 16)

        def swa_prep_pe(pe):
            pe.wait_ge(at["load"], a0["load"] + 112)
            nc.tensor.matmul(ps[0:HQ, 7, 0:384], s_rel[:, :], s_t5[:, :], start=True, stop=True).then_inc(s_rowed, 1)
            for c in range(TC):
                last = nc.tensor.transpose(banks(4)[:, c * P:(c + 1) * P], s_vT[:, c * P:(c + 1) * P], const("ident"))
            last.then_inc(at["prep"], 1)
            for j in range(NQK):
                pe.wait_ge(sq_sq, j + 1)
                if j >= 2:
                    pe.wait_ge(sq_ln, j - 1)
                for b in range(2):
                    last = nc.tensor.matmul(ps[:, 2 * (j % 2) + b, :], const("ones_half"), s_qsq[j % 2][:, b * HALF:(b + 1) * HALF],
                                            start=True, stop=True)
                last.then_inc(sq_sum, 1)

        def swa_x(j):
            return s_q[:, j, :] if j < GQ else s_k[:, WIN:WIN + T]

        def swa_prep_act(act):
            act.wait_ge(at["load"], a0["load"] + 112)
            act.wait_ge(s_rowed, 1)
            nc.scalar.activation(s_rows[:, :], ps[0:HQ, 7, 0:384], ACT.Copy).then_inc(s_rowed, 1)
            act.wait_ge(at["prep"], a0["prep"] + 1)
            nc.scalar.activation(s_v[:, 1:TC + 1, :].rearrange("p c x -> p (c x)"), banks(4), ACT.Copy).then_inc(at["prepc"], 1)
            def square(j):
                if j >= 2:
                    act.wait_ge(sq_sum, j - 1)
                nc.scalar.activation(s_qsq[j % 2][:, :], swa_x(j), ACT.Square).then_inc(sq_sq, 1)

            square(0)
            for j in range(NQK):
                if j + 1 < NQK:
                    square(j + 1)
                act.wait_ge(sq_sum, j + 1)
                if j >= 2:
                    act.wait_ge(sq_done, j - 1)
                nc.scalar.activation(s_qrs[j % 2][:, :], banks(2 * (j % 2)), ACT.Ln, bias=param("eps6"), scale=1.0 / HD)\
                    .then_inc(sq_ln, 1)
                act.wait_ge(sq_ln, j + 1)
                nc.scalar.activation(s_qrs[j % 2][:, :], s_qrs[j % 2][:, :], ACT.Exp, scale=-0.5).then_inc(sq_rs, 1)

        def swa_prep_dve(dve):
            proj_stored(dve, proj2)
            layer_read(dve, proj2)
            nc.vector.memset(s_k[:, 0:WIN], 0.0)
            nc.vector.memset(s_v[:, 0, :], 0.0)
            nc.vector.memset(s_zq[:, :, :, :], 0.0).then_inc(s_pads, 1)
            for j in range(NQK):
                dve.wait_ge(sq_rs, j + 1)
                nc.vector.scalar_tensor_tensor(swa_x(j), swa_x(j), param("q_g" if j < GQ else "k_g"), s_qrs[j % 2][:, :],
                                               op0=ALU.mult, op1=ALU.mult).then_inc(sq_done, 1)
            dve.wait_ge(at["bias"], a0["bias"] + 16 * 2)
            dve.wait_ge(at["load"], a0["load"] + 112)
            for j in range(2):
                nc.vector.tensor_tensor(s_bias[j][:, :, :], s_bias[j][:, :, :],
                                        s_mask[:, j, :].unsqueeze(1).to_broadcast([P, HQ, 2 * WIN]), ALU.add).then_inc(at["bias"], 1)
            dve.wait_ge(at["bias"], a0["bias"] + 16 * 2 + 2)

        def swa_blocks(eng, blocks):
            blocks(0, None)
            with eng.Fori(1, TC) as n:
                blocks(n, n + -1)
            blocks(None, TC - 1)

        def att(name, n, per=1, j=0):
            return per * n + (a0[name] + j + 1)

        def swa_pe(pe):
            pe.wait_ge(sq_done, NQK)
            pe.wait_ge(at["prepc"], a0["prepc"] + 1)

            def scores_of(n, first):
                pe.wait_ge(at["zq"], att("zq", n))
                if not first:
                    pe.wait_ge(at["sc"], att("sc", n, 4, -1))
                for h in range(HQ):
                    last = nc.tensor.matmul(ps[:, h // 2, (h % 2) * 256:(h % 2) * 256 + 256], s_zq[:, h % GQ, h // GQ, :],
                                            s_k[:, bass.ds(n * P, 2 * WIN)], start=True, stop=True)
                    if h % 2:
                        last.then_inc(at["s"], 1)

            def turn(n, c):
                pe.wait_ge(at["p"], att("p", n, HQ, 2 * c + 1))
                if c >= 2:
                    pe.wait_ge(at["ptc"], att("ptc", n, 4, c - 2))
                for j in range(4):
                    last = nc.tensor.transpose(ps[:, 4 + c % 2, j * P:(j + 1) * P],
                                               s_p[:, 2 * c + j // 2, (j % 2) * P:(j % 2) * P + P], const("ident"))
                last.then_inc(at["pt"], 1)

            def weigh(n, c):
                pe.wait_ge(at["ptc"], att("ptc", n, 4, c))
                for j in range(4):
                    h = 2 * c + j // 2
                    v = s_v[:, bass.ds(n + j % 2, 1), (h // GQ) * HD:(h // GQ + 1) * HD].rearrange("p o x -> p (o x)")
                    last = nc.tensor.matmul(ps[:, 6, h * HD:(h + 1) * HD], s_pt[c % 2][:, j, :], v,
                                            start=(j % 2 == 0), stop=(j % 2 == 1))
                last.then_inc(at["av"], 1)

            def blocks(new, old):
                if old is not None:
                    turn(old, 0)
                    turn(old, 1)
                if new is not None:
                    scores_of(new, old is None)
                if old is None:
                    return
                for c in range(4):
                    weigh(old, c)
                    if c + 2 < 4:
                        turn(old, c + 2)
                pe.wait_ge(at["zs"], att("zs", old))
                for c in range(4):
                    last = nc.tensor.transpose(ps[:, 7, c * P:(c + 1) * P],
                                               s_a[:, 2 * c:2 * c + 2, :].rearrange("p h x -> p (h x)"), const("ident"))
                last.then_inc(at["o"], 1)

            swa_blocks(pe, blocks)

        def swa_act(act):
            act.wait_ge(s_pads, 1)
            act.wait_ge(sq_done, NQK)

            def blocks(new, old):
                if new is not None:
                    if old is not None:
                        act.wait_ge(at["s"], att("s", new, 4, -1))
                    for v in range(KV):
                        ins = nc.scalar.activation(s_zq[HD * v:HD * v + HD, :, v, :], s_q[HD * v:HD * v + HD, :, bass.ds(new * P, P)], ACT.Copy)
                    ins.then_inc(at["zq"], 1)
                if old is not None:
                    for c in range(4):
                        act.wait_ge(at["pt"], att("pt", old, 4, c))
                        if c >= 2:
                            act.wait_ge(at["av"], att("av", old, 4, c - 2))
                        nc.scalar.activation(s_pt[c % 2][:, :, :].rearrange("p t x -> p (t x)"), ps[:, 4 + c % 2, :], ACT.Copy)\
                            .then_inc(at["ptc"], 1)
                if new is not None:
                    act.wait_ge(at["neg"], att("neg", new, 2, 1))
                    for h in range(HQ):
                        nc.scalar.activation(s_p[:, h, :], s_s[:, h, :], ACT.Exp, bias=s_small[:, S_NEG, h:h + 1],
                                             accum_out=s_small[:, S_SUM, h:h + 1]).then_inc(at["p"], 1)
                    nc.scalar.activation(s_small[:, S_SINK, :], s_small[:, S_SINK, :], ACT.Exp).then_inc(at["sq"], 1)
                if old is None:
                    return
                act.wait_ge(at["ss"], att("ss", old))
                nc.scalar.activation(s_small[:, S_LN, 0:1], s_small[:, S_SS, 0:1], ACT.Ln, bias=param("eps6"), scale=1.0 / (HQ * HD))\
                    .then_inc(at["ln"], 1)
                act.wait_ge(at["ln"], att("ln", old))
                nc.scalar.activation(s_small[:, S_R, 0:1], s_small[:, S_LN, 0:1], ACT.Exp, scale=-0.5).then_inc(at["r"], 1)

            swa_blocks(act, blocks)

        def swa_dve(dve):
            sinks = param("sinks", 0, HQ)

            def blocks(new, old):
                taps = None if new is None else [4 * new + (i - 1) for i in range(4)]
                if old is not None:
                    dve.wait_ge(at["sq"], att("sq", old))
                    nc.vector.tensor_tensor(s_small[:, S_INV, :], s_small[:, S_SUM, :], s_small[:, S_SINK, :], ALU.add).then_inc(at["rs"], 1)
                    dve.wait_ge(at["rs"], att("rs", old, 2, 0))
                    nc.vector.reciprocal(s_small[:, S_INV, :], s_small[:, S_INV, :]).then_inc(at["rs"], 1)
                if new is not None:
                    if old is not None:
                        conv_tap(dve, taps[0])
                    for c in range(4):
                        dve.wait_ge(at["s"], att("s", new, 4, c))
                        nc.vector.scalar_tensor_tensor(
                            s_s[:, 2 * c:2 * c + 2, :], ps[:, c, :].rearrange("p (h x) -> p h x", h=2), float(HD) ** -0.5,
                            s_bias[0 if old is None else 1][:, 2 * c:2 * c + 2, :], op0=ALU.mult, op1=ALU.add).then_inc(at["sc"], 1)
                    dve.wait_ge(at["sc"], att("sc", new, 4, 3))
                    nc.vector.tensor_reduce(s_small[:, S_M, :], s_s[:, :, :], AX.X, ALU.max).then_inc(at["max"], 1)
                    dve.wait_ge(at["max"], att("max", new, 2, 0))
                    nc.vector.tensor_tensor(s_small[:, S_MAX, :], s_small[:, S_M, :], sinks, ALU.max).then_inc(at["max"], 1)
                    dve.wait_ge(at["max"], att("max", new, 2, 1))
                    nc.vector.tensor_tensor(s_small[:, S_SINK, :], sinks, s_small[:, S_MAX, :], ALU.subtract).then_inc(at["neg"], 1)
                    nc.vector.tensor_scalar(s_small[:, S_NEG, :], s_small[:, S_MAX, :], -1.0, None, ALU.mult).then_inc(at["neg"], 1)
                if old is not None:
                    dve.wait_ge(at["rs"], att("rs", old, 2, 1))
                    dve.wait_ge(at["av"], att("av", old, 4, 3))
                    nc.vector.tensor_tensor(s_a[:, :, :], ps[:, 6, :].rearrange("p (h x) -> p h x", h=HQ),
                                            s_small[:, S_INV, :].unsqueeze(2).to_broadcast([P, HQ, HD]), ALU.mult).then_inc(at["z"], 1)
                    dve.wait_ge(at["z"], att("z", old, 2, 0))
                    flat = s_a[:, :, :].rearrange("p h x -> p (h x)")
                    nc.vector.tensor_tensor_reduce(s_sqa[:, :], flat, flat, 1.0, 0.0, ALU.mult, ALU.add, s_small[:, S_SS, 0:1])\
                        .then_inc(at["ss"], 1)
                if new is not None:
                    conv_tap(dve, taps[1])
                    conv_tap(dve, taps[2])
                if old is not None:
                    dve.wait_ge(at["r"], att("r", old))
                    nc.vector.tensor_scalar(flat, flat, s_small[:, S_R, 0:1], None, ALU.mult).then_inc(at["zs"], 1)
                if new is not None:
                    conv_tap(dve, taps[3])
                if old is not None:
                    dve.wait_ge(at["o"], att("o", old))
                    nc.vector.tensor_tensor(mixT[:, 0:4, bass.ds(old * P, P)], ps[:, 7, :].rearrange("p (c x) -> p c x", c=4),
                                            param("attn_g", 0, 4).unsqueeze(2).to_broadcast([P, 4, P]), ALU.mult).then_inc(at["z"], 1)

            swa_blocks(dve, blocks)

        CK, CC, CP = 31, 4, 3
        CW = 4 * P
        c_pad = [cwk.take(f"c_pad{j}", [P, CK - 1 + T]) for j in range(CC)]
        c_gate = [cwk.take(f"c_gate{j}", [P, T]) for j in range(CC)]
        s_p = Region(cwk.at - 2 * T * 4, cwk.at).take("s_p", [P, HQ, 2 * WIN])
        s_sqa = cwk.take("s_sqa", [P, HQ * HD])
        c_rs = cwk.take("c_rs", [P, T])
        c_load, c_sig, c_tap, c_ptap, c_conv, c_sum, c_cen, c_sq, c_sqs, c_ln, c_rstd, c_norm, c_silu, c_end = (
            sem(f"c_{name}") for name in ["load", "sig", "tap", "ptap", "conv", "sum", "cen", "sq", "sqs", "ln", "rstd", "norm", "silu", "end"])
        c_sqt = c_gate[0:2]

        def conv_sp(sp):
            for j in range(CC):
                row = HQ * HD + 2 * P + j * P
                sp.dma_start(c_pad[j][:, CK - 1:], g["h2"][row:row + P, :]).then_inc(c_load, 16)
                sp.dma_start(c_gate[j][:, :], g["h2"][row + CW:row + CW + P, :]).then_inc(c_load, 16)

        def conv_act(act):
            act.wait_ge(c_load, 32 * CC)
            for j in range(CC):
                nc.scalar.activation(c_gate[j][:, :], c_gate[j][:, :], ACT.Sigmoid).then_inc(c_sig, 1)
            act.preload_act_table_set(LOG_EXP)

        def conv_gate_dve(dve):
            for j in range(CC):
                nc.vector.memset(c_pad[j][:, 0:CK - 1], 0.0)
            for j in range(CC):
                dve.wait_ge(c_sig, j + 1)
                nc.vector.tensor_tensor(c_pad[j][:, CK - 1:], c_pad[j][:, CK - 1:], c_gate[j][:, :], ALU.mult).then_inc(c_conv, 1)

        def conv_tap(dve, tap):
            for j in range(CP):
                y, w = mixT[:, CC + j, :], param("conv_w_2", tap + j * CK)
                if type(tap) is int and tap == 0:
                    dve.wait_ge(c_conv, j + 1)
                    nc.vector.tensor_scalar(y, c_pad[j][:, 0:T], w, param("conv_b_2", j), ALU.mult, ALU.add).then_inc(c_tap, 1)
                else:
                    dve.wait_ge(c_tap, CP * tap + (j + 1 - CP))
                    nc.vector.scalar_tensor_tensor(y, c_pad[j][:, bass.ds(tap, T)], w, y, op0=ALU.mult, op1=ALU.add).then_inc(c_tap, 1)

        def conv_pool(pool):
            j = CP
            for tap in range(CK):
                y, src, w = mixT[:, CC + j, :], c_pad[j][:, tap:tap + T], param("conv_w_2", j * CK + tap)
                if tap == 0:
                    pool.wait_ge(c_conv, j + 1)
                    nc.gpsimd.tensor_scalar(y, src, w, param("conv_b_2", j), ALU.mult, ALU.add).then_inc(c_ptap, 1)
                else:
                    pool.wait_ge(c_ptap, 2 * tap - 1)
                    nc.gpsimd.tensor_scalar(s_vT[:, :], src, w, None, ALU.mult).then_inc(c_ptap, 1)
                    pool.wait_ge(c_ptap, 2 * tap)
                    nc.gpsimd.tensor_tensor(y, y, s_vT[:, :], ALU.add).then_inc(c_ptap, 1)

        def conv_norm_pe(pe):
            pe.wait_ge(at["z"], a0["z"] + 2 * TC)
            pe.wait_ge(c_tap, CK * CP)
            pe.wait_ge(c_ptap, 2 * CK - 1)
            for j in range(CC):
                for b in range(2):
                    last = nc.tensor.matmul(ps[:, b, :], const("ones"), mixT[:, CC + j, b * HALF:(b + 1) * HALF],
                                            start=(j == 0), stop=(j == CC - 1))
            last.then_inc(c_sum, 1)
            for i in range(2):
                for j in range(CC):
                    pe.wait_ge(c_sq, CC * i + j + 1)
                    for b in range(2):
                        last = nc.tensor.matmul(ps[:, 2 + 2 * i + b, :], const("ones"), c_sqt[j % 2][:, b * HALF:(b + 1) * HALF],
                                                start=(j == 0), stop=(j == CC - 1))
                    last.then_inc(c_sqs, 1)

        def conv_norm_act(act):
            for i in range(2):
                for j in range(CC):
                    act.wait_ge(c_cen if i == 0 else c_silu, j + 1)
                    if CC * i + j >= 2:
                        act.wait_ge(c_sqs, CC * i + j - 1)
                    nc.scalar.activation(c_sqt[j % 2][:, :], mixT[:, CC + j, :], ACT.Square).then_inc(c_sq, 1)
                act.wait_ge(c_sqs, CC * i + CC)
                nc.scalar.activation(c_rs[:, :], banks(2 + 2 * i), ACT.Ln, bias=param("eps6"), scale=1.0 / CW).then_inc(c_ln, 1)
                act.wait_ge(c_ln, i + 1)
                nc.scalar.activation(c_rs[:, :], c_rs[:, :], ACT.Exp, scale=-0.5).then_inc(c_rstd, 1)
                if i == 0:
                    for j in range(CC):
                        act.wait_ge(c_norm, j + 1)
                        nc.scalar.activation(mixT[:, CC + j, :], mixT[:, CC + j, :], ACT.Silu, bias=param("cln_b", j)).then_inc(c_silu, 1)
                    act.preload_act_table_set(LOG_EXP)

        def conv_norm_dve(dve):
            dve.wait_ge(c_sum, 1)
            for j in range(CC):
                y = mixT[:, CC + j, :]
                nc.vector.scalar_tensor_tensor(y, banks(0), -1.0 / CW, y, op0=ALU.mult, op1=ALU.add).then_inc(c_cen, 1)
            for i in range(2):
                dve.wait_ge(c_rstd, i + 1)
                for j in range(CC):
                    y = mixT[:, CC + j, :]
                    nc.vector.scalar_tensor_tensor(y, y, param("cln_g" if i == 0 else "cout_g", j), c_rs[:, :],
                                                   op0=ALU.mult, op1=ALU.mult).then_inc(c_norm if i == 0 else c_end, 1)

        LP, LK, LV = 2, 64, P
        GATE = 1.0 / 16.0
        LQ0, LK0, LV0, LG0, LR0 = (ORDER3[name][0] for name in "qkvgr")
        LL = 7
        lop = Region(arena, ops_end)
        l_q = lop.take("l_q", [P, LP, T])
        l_k = lop.take("l_k", [P, LP, TM])
        l_vt = lop.take("l_vt", [P, TC, GH * LV])
        l_g = lop.take("l_g", [P, GH, T])
        l_b = lop.take("l_b", [P, LP, TM])
        l_gr = lop.take("l_gr", [16, TM])
        l_wg = lop.take("l_wg", [16, LP * P])
        l_vm = lop.take("l_vm", [META, GH * LV])
        lwk = Region(mix_end, end)
        l_mask = lwk.take("l_mask", [P, LL + 1, P], I32)
        l_run = lwk.take("l_run", [P, TM])
        l_t = lwk.take("l_t", [P, LP, TM])
        l_a = lwk.take("l_a", [P, LP, TM])
        l_v = Region(lwk.at, end).take("l_v", [P, GH, TM])
        l_e = [lwk.take(f"l_e{j}", [P, LP, P]) for j in range(2)]
        l_ql = [lwk.take(f"l_ql{j}", [P, LP, P]) for j in range(2)]
        l_kl = [lwk.take(f"l_kl{j}", [P, LP, P]) for j in range(2)]
        l_A = lwk.take("l_A", [P, GH, P])
        l_eb, l_qd, l_ke, l_S = (lwk.take(f"l_{name}", [P, LP, P]) for name in ["eb", "qd", "ke", "S"])
        l_kc = lwk.take("l_kc", [P, LP, P])
        l_ket = lwk.take("l_ket", [P, LP, P])
        l_o = lwk.take("l_o", [P, GH, LV])
        fin = Region(arena + LP * (T + TM) * 4, ops_end)
        l_sq = [fin.take(f"l_sq{j}", [P, T]) for j in range(2)]
        l_rs = [fin.take(f"l_rs{j}", [P, T]) for j in range(2)]
        l_small = lwk.take("l_small", [P, 8, GH])
        L_LAST, L_WAIT = range(2)
        (l_load, l_tr, l_trc, l_gate, l_scan, l_meta, l_diff, l_exp, l_lq, l_lk, l_lA, l_pred, l_dec, l_qdd, l_ked, l_ket_, l_ketc,
         l_out, l_osc, l_turn, l_mixed, l_su, l_kcd, l_end) = (
            sem(f"l_{name}") for name in [
                "load", "tr", "trc", "gate", "scan", "meta", "diff", "exp", "lq", "lk", "lA", "pred", "dec", "qd", "ke", "ket",
                "ketc", "out", "osc", "turn", "mixed", "su", "kcd", "end"])

        L_GATE = 32 * CC + 48 * CC + 32

        def gla_sp(sp):
            proj_stored(sp, proj3)
            layer_read(sp, proj3)
            sp.wait_ge(c_ptap, K_STEPS)
            h3 = g["h3"]

            def rows(first, chunks, t0=0):
                return h3[first:first + chunks * P, t0:].rearrange("(c p) t -> p c t", p=P)

            sp.dma_start(l_gr[:, :], h3[LR0:LR0 + 16, :]).then_inc(c_load, 16)
            sp.dma_start(l_wg[:, :], g["w_gate"]).then_inc(c_load, 16)
            sp.dma_start(l_v[:, :, :], rows(LV0, GH)).then_inc(l_load, 16)
            sp.dma_start(l_k[:, :, :], rows(LK0, LP)).then_inc(l_load, 16)
            sp.dma_start(l_q[:, :, :], rows(LQ0, LP, META)).then_inc(l_load, 16)
            sp.dma_start(l_g[:, :, :], rows(LG0, GH, META)).then_inc(l_load, 16)
            sp.dma_start(l_mask[:, :, :], g["gla_consts"]).then_inc(l_load, 16)

        def gla_prep_pe(pe):
            pe.wait_ge(c_load, L_GATE)
            for j in range(LP):
                for b, (t0, t1) in enumerate([(META, META + HALF), (META + HALF, TM), (0, META)]):
                    last = nc.tensor.matmul(ps[:, 3 * j + b, 0:t1 - t0], l_wg[:, j * P:(j + 1) * P], l_gr[:, t0:t1],
                                            start=True, stop=True)
            last.then_inc(l_gate, 1)
            pe.wait_ge(l_load, 80)
            for c in range(TC):
                if c >= 2:
                    pe.wait_ge(l_trc, c - 1)
                for h in range(GH):
                    last = nc.tensor.transpose(ps[:, 6 + c % 2, h * P:(h + 1) * P], l_v[:, h, META + c * P:META + (c + 1) * P],
                                               const("ident"))
                last.then_inc(l_tr, 1)
            pe.wait_ge(l_trc, TC)
            for h in range(GH):
                last = nc.tensor.transpose(ps[0:META, 6, h * P:(h + 1) * P], l_v[:, h, 0:META], const("ident"))
            last.then_inc(l_tr, 1)
            pe.wait_ge(l_meta, 3)
            for j in range(LP):
                last = nc.tensor.transpose(ps[0:META, 7, j * P:(j + 1) * P], l_ke[:, j, 0:META], const("ident"))
            last.then_inc(l_meta, 1)
            pe.wait_ge(l_meta, 5)
            pe.wait_ge(l_trc, TC + 1)
            for j in range(LP):
                last = nc.tensor.matmul(ps[:, 0, j * 256:(j + 1) * 256], l_ket[0:META, j, :], l_vm[:, j * 256:(j + 1) * 256],
                                        start=True, stop=True)
            last.then_inc(l_meta, 1)

        def gla_prep_act(act):
            act.wait_ge(l_gate, 1)
            for j in range(LP):
                nc.scalar.activation(l_t[:, j, META:TM], banks(3 * j), ACT.Identity, bias=param("b_gate", j))
                nc.scalar.activation(l_t[:, j, 0:META], ps[:, 3 * j + 2, 0:META], ACT.Identity, bias=param("b_gate", j)).then_inc(l_gate, 1)
            act.wait_ge(l_gate, 4)
            nc.scalar.activation(l_a[:, :, :], l_a[:, :, :], ACT.Exp).then_inc(l_gate, 1)
            act.wait_ge(l_gate, 5)
            nc.scalar.activation(l_a[:, :, :], l_a[:, :, :], ACT.Ln, bias=param("one")).then_inc(l_gate, 1)
            for c in range(TC):
                act.wait_ge(l_tr, c + 1)
                nc.scalar.activation(l_vt[:, c, :], ps[:, 6 + c % 2, :], ACT.Copy).then_inc(l_trc, 1)
            act.wait_ge(l_tr, TC + 1)
            nc.scalar.activation(l_vm[:, :], ps[0:META, 6, :], ACT.Copy).then_inc(l_trc, 1)
            act.wait_ge(l_meta, 1)
            nc.scalar.activation(l_ke[:, :, 0:META], l_ke[:, :, 0:META], ACT.Exp, scale=GATE).then_inc(l_meta, 1)
            act.wait_ge(l_meta, 4)
            nc.scalar.activation(l_ket[0:META, :, :].rearrange("p j x -> p (j x)"), ps[0:META, 7, 0:LP * P], ACT.Copy).then_inc(l_meta, 1)

        def gla_prep_dve(dve):
            proj_stored(dve, proj3)
            layer_read(dve, proj3)
            dve.wait_ge(c_ptap, K_STEPS)
            nc.vector.memset(l_run[:, :], 1.0).then_inc(l_scan, 1)
            dve.wait_ge(l_scan, 1)
            nc.vector.memset(l_run[:, 0:1], 0.0)
            nc.vector.memset(l_run[:, META:TM].rearrange("p (c x) -> p c x", x=P)[:, :, 0:1], 0.0).then_inc(l_scan, 1)
            dve.wait_ge(l_gate, 3)
            nc.vector.scalar_tensor_tensor(l_a[:, :, :], l_t[:, :, :], -1.0, l_t[:, :, :], op0=ALU.mult, op1=ALU.min).then_inc(l_gate, 1)
            dve.wait_ge(l_gate, 6)
            nc.vector.scalar_tensor_tensor(l_t[:, :, :], l_t[:, :, :], 0.0, l_a[:, :, :], op0=ALU.min, op1=ALU.subtract).then_inc(l_gate, 1)
            dve.wait_ge(l_gate, 7)
            dve.wait_ge(l_scan, 2)
            for j in range(LP):
                nc.vector.tensor_tensor_scan(l_b[:, j, :], l_run[:, :], l_t[:, j, :], 0.0, ALU.mult, ALU.add).then_inc(l_scan, 1)
            dve.wait_ge(l_scan, 4)
            dve.wait_ge(l_trc, TC + 1)
            nc.vector.tensor_tensor(l_ke[:, :, 0:META], l_b[:, :, META - 1:META].to_broadcast([P, LP, META]), l_b[:, :, 0:META],
                                    ALU.subtract).then_inc(l_meta, 1)
            dve.wait_ge(l_meta, 2)
            nc.vector.tensor_tensor(l_ke[:, :, 0:META], l_ke[:, :, 0:META], l_k[:, :, 0:META], ALU.mult).then_inc(l_meta, 1)
            dve.wait_ge(l_meta, 6)
            for j in range(LP):
                for i in range(2):
                    rows = slice(LK * i, LK * i + LK)
                    nc.vector.tensor_copy(l_S[rows, j, :], ps[rows, 0, j * 256 + i * LV:j * 256 + (i + 1) * LV])
            nc.vector.memset(l_A[:, :, :], 0.0).then_inc(l_end, 1)

        def each(n, per=1, j=0):
            return per * n + (j + 1)

        def l_chunk(t, n, first=0):
            return t[:, :, bass.ds(n * P + first, P)]

        def head_bank(b, h):
            return ps[:, b + h % 2, (h // 2) * P:(h // 2 + 1) * P]

        def two_banks(b):
            return ps[:, b:b + 2, 0:LP * P].rearrange("p i (j x) -> p i j x", j=LP)

        def by_bank(t):
            return t[:, :, :].rearrange("p (j i) x -> p i j x", i=2)

        def gla_pe(pe):
            pe.wait_ge(l_end, 1)
            with pe.Fori(0, TC) as n:
                for l in range(LL + 1):
                    pe.wait_ge(l_lq, each(n, LL + 1, l))
                    if l < LL:
                        pe.wait_ge(l_lk, each(n, LL, l))
                    else:
                        pe.wait_ge(l_kcd, each(n))
                    keys = l_kl[l % 2] if l < LL else l_kc
                    if l >= 2:
                        pe.wait_ge(l_pred, each(n, LL + 1, l - 2))
                    for h in range(GH):
                        rows = slice(LK * (h % 2), LK * (h % 2) + LK)
                        last = nc.tensor.matmul(head_bank(2 * (l % 2), h), keys[rows, h // 2, :], l_ql[l % 2][rows, h // 2, :],
                                                start=True, stop=True)
                    last.then_inc(l_lA, 1)
                pe.wait_ge(l_ked, each(n))
                for j in range(LP):
                    last = nc.tensor.transpose(ps[:, 6, j * P:(j + 1) * P], l_ke[:, j, :], const("ident"))
                last.then_inc(l_ket_, 1)
                pe.wait_ge(l_pred, each(n, LL + 1, LL))
                pe.wait_ge(l_qdd, each(n))
                pe.wait_ge(l_end, each(n))
                for h in range(GH):
                    rows = slice(LK * (h % 2), LK * (h % 2) + LK)
                    v = l_vt[:, bass.ds(n, 1), h * LV:(h + 1) * LV].rearrange("p o x -> p (o x)")
                    nc.tensor.matmul(head_bank(4, h), l_A[:, h, :], v, start=True, stop=False)
                    last = nc.tensor.matmul(head_bank(4, h), l_qd[rows, h // 2, :], l_S[rows, h // 2, :],
                                            start=False, stop=True)
                last.then_inc(l_out, 1)
                pe.wait_ge(l_ketc, each(n))
                for j in range(LP):
                    v = l_vt[:, bass.ds(n, 1), j * 256:(j + 1) * 256].rearrange("p o x -> p (o x)")
                    last = nc.tensor.matmul(ps[:, 7, j * 256:(j + 1) * 256], l_ket[:, j, :], v, start=True, stop=True)
                last.then_inc(l_su, 1)
                pe.wait_ge(l_osc, each(n))
                for h in range(GH):
                    last = nc.tensor.transpose(ps[:, 6, h * P:(h + 1) * P], l_o[:, h, :], const("ident"))
                last.then_inc(l_turn, 1)

        def gla_act(act):
            act.wait_ge(l_end, 1)
            with act.Fori(0, TC) as n:
                b = l_chunk(l_b, n, META)
                act.wait_ge(l_end, each(n))
                nc.scalar.activation(l_eb[:, :, :], b, ACT.Exp, scale=GATE).then_inc(l_dec, 1)
                nc.scalar.activation(l_small[:, L_LAST, 0:LP].unsqueeze(2), l_b[:, :, bass.ds(n * P + (META + P - 1), 1)], ACT.Exp,
                                     scale=GATE).then_inc(l_dec, 1)
                act.wait_ge(l_diff, each(n, 2 * LL + 1, 0))
                nc.scalar.activation(l_ke[:, :, :], l_ke[:, :, :], ACT.Exp, scale=GATE).then_inc(l_dec, 1)
                for l in range(LL):
                    act.wait_ge(l_diff, each(n, 2 * LL + 1, 2 * l + 2))
                    nc.scalar.activation(l_e[l % 2][:, :, :], l_e[l % 2][:, :, :], ACT.Exp, scale=GATE).then_inc(l_exp, 1)
                act.wait_ge(l_ket_, each(n))
                nc.scalar.activation(l_ket[:, :, :].rearrange("p j x -> p (j x)"), ps[:, 6, 0:LP * P], ACT.Copy).then_inc(l_ketc, 1)
                act.wait_ge(l_turn, each(n))
                nc.scalar.activation(mixT[:, 0:GH, bass.ds(n * P, P)], ps[:, 6, :].rearrange("p (h x) -> p h x", h=GH), ACT.Copy)\
                    .then_inc(l_mixed, 1)

        def gla_pool(pool):
            pool.wait_ge(l_end, 1)
            with pool.Fori(0, TC) as n:
                pool.wait_ge(l_end, each(n))
                nc.gpsimd.tensor_copy(l_kc[:, :, :], l_chunk(l_k, n, META)).then_inc(l_kcd, 1)
                pool.wait_ge(l_kcd, each(n))
                pool.wait_ge(l_dec, each(n, 3, 2))
                nc.gpsimd.tensor_tensor(l_ke[:, :, :], l_ke[:, :, :], l_kc[:, :, :], ALU.mult).then_inc(l_ked, 1)
                for l in range(LL):
                    if l >= 2:
                        pool.wait_ge(l_lA, each(n, LL + 1, l - 2))
                    pool.wait_ge(l_exp, each(n, LL, l))
                    nc.gpsimd.tensor_tensor(l_kl[l % 2][:, :, :], l_e[l % 2][:, :, :], l_kc[:, :, :], ALU.mult).then_inc(l_lk, 1)

        def gla_dve(dve):
            scale = float(LK) ** -0.5
            dve.wait_ge(l_end, 1)
            with dve.Fori(0, TC) as n:
                q, b = l_chunk(l_q, n), l_chunk(l_b, n, META)
                tok = bass.ds(n * P, P)
                dve.wait_ge(l_end, each(n))
                b_end = l_b[:, :, bass.ds(n * P + (META + P - 1), 1)].to_broadcast([P, LP, P])
                nc.vector.tensor_tensor(l_ke[:, :, :], b_end, b, ALU.subtract).then_inc(l_diff, 1)
                dve.wait_ge(l_dec, each(n, 3, 0))
                nc.vector.scalar_tensor_tensor(l_qd[:, :, :], q, scale, l_eb[:, :, :], op0=ALU.mult, op1=ALU.mult).then_inc(l_qdd, 1)

                def away(l):
                    m = (P // 2) >> l
                    if l >= 2:
                        dve.wait_ge(l_lk, each(n, LL, l - 2))
                        dve.wait_ge(l_lq, each(n, LL + 1, l - 2))
                    e = l_e[l % 2]
                    for j in range(LP):
                        view = b[:, j, :].rearrange("p (n x) -> p n x", x=2 * m)
                        r = view[:, :, m - 1:m].to_broadcast([P, P // (2 * m), 2 * m])
                        ins = nc.vector.tensor_tensor(e[:, j, :].rearrange("p (n x) -> p n x", x=2 * m), view, r, ALU.subtract)
                    ins.then_inc(l_diff, 1)
                    dve.wait_ge(l_diff, each(n, 2 * LL + 1, 2 * l + 1))
                    nc.vector.scalar_tensor_tensor(e[:, :, :], e[:, :, :], -1.0, e[:, :, :], op0=ALU.mult, op1=ALU.min).then_inc(l_diff, 1)

                def queries(l):
                    if l >= 2:
                        dve.wait_ge(l_lA, each(n, LL + 1, l - 2))
                    if l < LL:
                        dve.wait_ge(l_exp, each(n, LL, l))
                        nc.vector.scalar_tensor_tensor(l_ql[l % 2][:, :, :], q, scale, l_e[l % 2][:, :, :], op0=ALU.mult, op1=ALU.mult)\
                            .then_inc(l_lq, 1)
                    else:
                        nc.vector.tensor_scalar(l_ql[l % 2][:, :, :], q, scale, None, ALU.mult).then_inc(l_lq, 1)

                def pick(l):
                    dve.wait_ge(l_lA, each(n, LL + 1, l))
                    if l:
                        dve.wait_ge(l_pred, each(n, LL + 1, l - 1))
                    nc.vector.memset(l_small[:, L_WAIT, 0:1], 0.0)
                    nc.vector.copy_predicated(by_bank(l_A), l_mask[:, l, :].unsqueeze(1).unsqueeze(1).to_broadcast([P, 2, LP, P]),
                                              two_banks(2 * (l % 2))).then_inc(l_pred, 1)

                for l in range(LL + 3):
                    if l < LL:
                        away(l)
                    if 1 <= l <= LL + 1:
                        queries(l - 1)
                    if l >= 2:
                        pick(l - 2)
                dve.wait_ge(l_out, each(n))
                nc.vector.tensor_copy(by_bank(l_o), two_banks(4)).then_inc(l_osc, 1)
                dve.wait_ge(l_su, each(n))
                dve.wait_ge(l_dec, each(n, 3, 1))
                for j in range(LP):
                    for i in range(2):
                        rows = slice(LK * i, LK * i + LK)
                        ins = nc.vector.scalar_tensor_tensor(l_S[rows, j, :], l_S[rows, j, :], l_small[rows, L_LAST, j:j + 1],
                                                             ps[rows, 7, j * 256 + i * LV:j * 256 + (i + 1) * LV], op0=ALU.mult, op1=ALU.add)
                ins.then_inc(l_end, 1)

        def gla_out_pe(pe):
            for h in range(GH):
                pe.wait_ge(go_sq, GH + h + 1)
                if h >= 2:
                    pe.wait_ge(go_ln, GH + h - 1)
                for b in range(2):
                    last = nc.tensor.matmul(ps[:, 2 * (h % 2) + b, :], const("ones"), l_sq[h % 2][:, b * HALF:(b + 1) * HALF],
                                            start=True, stop=True)
                last.then_inc(go_sum, 1)

        def gla_out_act(act):
            def square(h):
                if h >= 2:
                    act.wait_ge(go_sum, GH + h - 1)
                nc.scalar.activation(l_sq[h % 2][:, :], mixT[:, h, :], ACT.Square).then_inc(go_sq, 1)

            act.wait_ge(l_mixed, TC)
            square(0)
            for h in range(GH):
                if h + 1 < GH:
                    square(h + 1)
                act.wait_ge(go_sum, GH + h + 1)
                if h >= 2:
                    act.wait_ge(go_norm, GH + h - 1)
                nc.scalar.activation(l_rs[h % 2][:, :], banks(2 * (h % 2)), ACT.Ln, bias=param("eps6"), scale=1.0 / LV).then_inc(go_ln, 1)
                act.wait_ge(go_ln, GH + h + 1)
                nc.scalar.activation(l_rs[h % 2][:, :], l_rs[h % 2][:, :], ACT.Exp, scale=-0.5).then_inc(go_rs, 1)
            for h in range(GH):
                nc.scalar.activation(l_g[:, h, :], l_g[:, h, :], ACT.Silu).then_inc(go_silu, 1)
            act.preload_act_table_set(LOG_EXP)

        def gla_out_dve(dve):
            for h in range(GH):
                dve.wait_ge(go_rs, GH + h + 1)
                nc.vector.scalar_tensor_tensor(mixT[:, h, :], mixT[:, h, :], param("gla_g"), l_rs[h % 2][:, :],
                                               op0=ALU.mult, op1=ALU.mult).then_inc(go_norm, 1)
            for h in range(GH):
                dve.wait_ge(go_norm, GH + h + 1)
                dve.wait_ge(go_silu, GH + h + 1)
                nc.vector.tensor_tensor(mixT[:, h, :], mixT[:, h, :], l_g[:, h, :], ALU.mult).then_inc(go_end, 1)

        SK = 3
        short = Region(mix_end, end)
        k_c, k_x = ([short.take(f"k_{name}{j}", [P, TM]) for j in range(CC)] for name in "cx")
        k_b = [short.take(f"k_b{j}", [P, T]) for j in range(CC)]
        K0 = 2 * CK - 1
        K_LOAD = 32 * CC
        K_OPS = 2 * SK + 1
        K_STEPS = K0 + K_OPS * CC

        def short_sp(sp):
            for j in range(CC):
                for name, tile in [("c", k_c), ("x", k_x), ("b", k_b)]:
                    row = ORDER3[name][0] + j * P
                    sp.dma_start(tile[j][:, :], g["h3"][row:row + P, META if name == "b" else 0:]).then_inc(c_load, 16)

        def short_pool(pool):
            pool.wait_ge(c_load, K_LOAD + 16 * 3 * CC)
            for step in range(K_OPS):
                for j in range(CC):
                    u, prod, y = k_c[j], k_x[j][:, 0:T], mixT[:, CC + j, :]
                    if step:
                        pool.wait_ge(c_ptap, K0 + CC * (step - 1) + j + 1)
                    if step == 0:
                        ins = nc.gpsimd.tensor_tensor(u[:, :], u[:, :], k_x[j][:, :], ALU.mult)
                    elif step == K_OPS - 1:
                        ins = nc.gpsimd.tensor_tensor(y, y, k_b[j][:, :], ALU.mult)
                    elif step % 2 and step > 1:
                        ins = nc.gpsimd.tensor_tensor(y, y, prod, ALU.add)
                    else:
                        tap = step // 2
                        ins = nc.gpsimd.tensor_scalar(prod if tap else y, u[:, META - SK + 1 + tap:META - SK + 1 + tap + T],
                                                      param("conv_w_3", j * SK + tap), None, ALU.mult)
                    ins.then_inc(c_ptap, 1)
        block = ctx.enter_context(nc.Block())

        @block.sync
        def _(sp):
            sp.dma_start(params[:, :], g["params"]).then_inc(loaded, 16)
            sp.dma_start(consts[:, :], g["consts"]).then_inc(loaded, 16)
            sp.dma_start(xT[:, :, :], g["x"]).then_inc(loaded, 16)
            first_pair_sp(sp, proj1)
            linear_sp(sp, proj1, then=(EARLY1, gdn_early_sp))
            na_bias_sp(sp)
            gdn_sp(sp)
            gdn_out_sp(sp)
            na_sp(sp)
            linear_sp(sp, out1)
            linear_sp(sp, mlp1)
            linear_sp(sp, proj2)
            swa_sp(sp)
            sp.wait_ge(c_end, CC)
            sp.dma_start(metaT[:, :, :], g["meta"]).then_inc(loaded, 16)
            linear_sp(sp, out2)
            linear_sp(sp, mlp2)
            linear_sp(sp, proj3, then=(CONV3[1], short_sp))
            gla_sp(sp)
            linear_sp(sp, out3)
            linear_sp(sp, mlp3)
            for c in range(DC):
                sp.wait_ge(n_scaled, DC * rms_final.i + c + 1)
                sp.dma_start(g["out"][c], xT[:, c, :]).then_inc(loaded, 16)
            sp.wait_ge(loaded, 16 * (4 + DC))

        @block.tensor
        def _(pe):
            pe.wait_ge(loaded, 48)
            for s in range(2):
                nc.tensor.matmul(ps[:, 6 + s, 0:P], const("ones"), const("ones"), start=True, stop=True).then_inc(mm_done[s], 1)
            norm_pe(pe, ln_in)
            proj_pe(pe, proj1)
            layer_read(pe, proj1)
            gdn_prep_pe(pe)
            gdn_gates_pe(pe)
            gdn_loop_pe(pe)
            gdn_out_pe(pe)
            na_pe(pe)
            out_pe(pe, out1, 0)
            layer_read(pe, out1)
            norm_pe(pe, ln1)
            mlp_pe(pe, mlp1)
            layer_read(pe, mlp1)
            norm_pe(pe, ln2)
            norm_pe(pe, rms_mix2)
            proj_pe(pe, proj2)
            layer_read(pe, proj2)
            swa_prep_pe(pe)
            swa_pe(pe)
            conv_norm_pe(pe)
            out_pe(pe, out2, 1)
            layer_read(pe, out2)
            meta_pe(pe)
            norm_pe(pe, rms_mlp2)
            pe.wait_ge(meta, 3)
            mlp_pe(pe, mlp2)
            layer_read(pe, mlp2)
            norm_pe(pe, rms_mix3)
            pe.wait_ge(meta, 8)
            proj_pe(pe, proj3)
            layer_read(pe, proj3)
            gla_prep_pe(pe)
            gla_pe(pe)
            gla_out_pe(pe)
            out_pe(pe, out3, 2)
            layer_read(pe, out3)
            norm_pe(pe, rms_mlp3)
            mlp_pe(pe, mlp3)
            layer_read(pe, mlp3)
            norm_pe(pe, rms_final)

        @block.scalar
        def _(act):
            act.preload_act_table_set(LOG_EXP)
            act.wait_ge(loaded, 48)
            for s in range(2):
                split_hi(act, s, 0)
            norm_act(act, ln_in)
            proj_act(act, proj1)
            gdn_prep_act(act)
            gdn_gates_act(act)
            gdn_loop_act(act)
            gdn_out_act(act)
            na_act(act)
            act.wait_ge(go_end, GH)
            act.wait_ge(at["end"], ROWS + 1)
            mix_split_act(act, 0)
            out_act(act, out1)
            layer_read(act, out1)
            norm_act(act, ln1)
            mlp_act(act, mlp1)
            layer_read(act, mlp1)
            norm_act(act, ln2, then=rms_mix2)
            norm_act(act, rms_mix2)
            proj_act(act, proj2)
            layer_read(act, proj2)
            swa_prep_act(act)
            conv_act(act)
            swa_act(act)
            act.wait_ge(at["z"], a0["z"] + 2 * TC)
            mix_split_act(act, 1, range(CC))
            conv_norm_act(act)
            act.wait_ge(c_end, CC)
            mix_split_act(act, 1, range(CC, DC))
            out_act(act, out2)
            meta_square_act(act)
            layer_read(act, out2)
            norm_rstd_act(act, rms_mlp2)
            meta_rstd_act(act)
            norm_high_act(act, rms_mlp2)
            meta_high_act(act)
            mlp_act(act, mlp2)
            layer_read(act, mlp2)
            norm_act(act, rms_mix3)
            proj_act(act, proj3)
            layer_read(act, proj3)
            gla_prep_act(act)
            gla_act(act)
            gla_out_act(act)
            act.wait_ge(go_end, 2 * GH)
            act.wait_ge(c_ptap, K_STEPS)
            mix_split_act(act, 2)
            out_act(act, out3)
            layer_read(act, out3)
            norm_act(act, rms_mlp3)
            mlp_act(act, mlp3)
            layer_read(act, mlp3)
            norm_act(act, rms_final)

        @block.vector
        def _(dve):
            for s in range(2):
                nc.vector.memset(tick[:, s:s + 1], 0.0).then_inc(w_split[s], 1)
                nc.vector.memset(tick[:, 2 + s:3 + s], 0.0).then_inc(ps_free[s], 1)
                nc.vector.memset(tick[:, 4 + s:5 + s], 0.0).then_inc(stored[s], 16)
            nc.vector.memset(tick[:, 6:7], 0.0).then_inc(hid_sq, 2)
            for s in range(2):
                split_lo(dve, s, 0)
            dve.wait_ge(loaded, 48)
            norm_dve(dve, ln_in)
            gdn_pad_dve(dve)
            proj_dve(dve, proj1, beside=(1, GCH + 1, gdn_conv_dve))
            layer_read(dve, proj1)
            gdn_prep_dve(dve)
            proj_stored(dve, proj1)
            gdn_gates_dve(dve)
            gdn_loop_dve(dve)
            gdn_out_dve(dve)
            na_dve(dve)
            mix_split_dve(dve, 0)
            out_dve(dve, out1)
            layer_read(dve, out1)
            norm_dve(dve, ln1)
            mlp_dve(dve, mlp1)
            layer_read(dve, mlp1)
            norm_dve(dve, ln2)
            norm_shifted(dve, ln2)
            norm_dve(dve, rms_mix2)
            proj_dve(dve, proj2)
            swa_prep_dve(dve)
            conv_gate_dve(dve)
            swa_dve(dve)
            mix_split_dve(dve, 1, range(CC))
            conv_norm_dve(dve)
            mix_split_dve(dve, 1, range(CC, DC))
            out_dve(dve, out2)
            layer_read(dve, out2)
            norm_dve(dve, rms_mlp2)
            meta_dve(dve)
            mlp_dve(dve, mlp2)
            layer_read(dve, mlp2)
            norm_dve(dve, rms_mix3)
            proj_dve(dve, proj3)
            gla_prep_dve(dve)
            gla_dve(dve)
            gla_out_dve(dve)
            mix_split_dve(dve, 2)
            out_dve(dve, out3)
            layer_read(dve, out3)
            norm_dve(dve, rms_mlp3)
            mlp_dve(dve, mlp3)
            layer_read(dve, mlp3)
            norm_dve(dve, rms_final)

        @block.gpsimd
        def _(pool):
            gdn_conv_pool(pool)
            gdn_loop_pool(pool)
            norm_pool(pool, ln1)
            norm_pool(pool, ln2)
            conv_pool(pool)
            norm_pool(pool, rms_mlp2)
            norm_pool(pool, rms_mix3)
            short_pool(pool)
            gla_pool(pool)
            norm_pool(pool, rms_mlp3)
            norm_pool(pool, rms_final)


def lay_t5():
    n = np.clip(255 - np.arange(384), 0, None)
    large = 16 + (np.log(np.maximum(n, 1) / 16) / np.log(128 / 16) * 16).astype(np.int32)
    bucket = np.where(n < 16, n, np.minimum(large, 31))
    return (np.arange(32)[:, None] == bucket[None, :]).astype(np.float32)


def lay_swa_mask():
    dist = np.arange(P)[:, None] + P - np.arange(2 * P)[None, :]
    seen = (dist >= 0) & (dist < P)
    first = seen & (np.arange(2 * P) >= P)
    return np.where(np.stack([first, seen], 1), 0.0, -1e30).astype(np.float32)


def lay_gla_consts():
    j, i = np.arange(P)[:, None], np.arange(P)[None, :]
    out = np.zeros((P, 8, P), np.int32)
    for l in range(7):
        m = 64 >> l
        out[:, l] = (j // (2 * m) == i // (2 * m)) & (j // m % 2 == 0) & (i // m % 2 == 1)
    out[:, 7] = j == i
    return out


def kernel(**inputs):
    import concourse.bacc as bacc
    from concourse.bass_utils import run_bass_kernel_spmd

    def feats(v):
        return np.asarray(v).reshape(-1, P).T

    def units(w):
        w = np.asarray(w)
        w = np.pad(w, ((0, 0), (0, padded(w.shape[1]) - w.shape[1])))
        return w.reshape(DC, P, -1, P).transpose(2, 1, 0, 3).reshape(-1, P, UNIT)

    def mlp_units(up, down):
        up = units(up).reshape(NG, 4, P, UNIT)
        down = np.asarray(down).reshape(NG, FG // P, P, 4, 256).transpose(0, 3, 2, 1, 4).reshape(NG, 4, P, UNIT)
        return np.concatenate([up, down], 1).reshape(-1, P, UNIT)

    def taps(w):
        w = np.asarray(w)
        return w.reshape(w.shape[0], -1, P).transpose(2, 1, 0).reshape(P, -1)

    def third(w):
        parts = dict(zip("qkvgrbcx", np.split(np.asarray(w), np.cumsum([256, 256, 512, 512, 16, 512, 512]), 1)))
        return np.concatenate([parts[name] for name in ORDER3], 1)

    def rows(v):
        return np.broadcast_to(np.asarray(v).reshape(1, -1), (P, np.asarray(v).size))

    i = inputs
    twice = lambda v: np.tile(np.asarray(v).reshape(-1), 2).reshape(P, 1)
    full = lambda c: np.full((P, 1), c, np.float32)
    by_name = {
        "ln_in_g": feats(i["ln_in_g"]), "ln_in_b": feats(i["ln_in_b"]), "ln1_g": feats(i["ln1_g"]),
        "ln1_b": feats(i["ln1_b"]), "ln2_g": feats(i["ln2_g"]), "ln2_b": feats(i["ln2_b"]), "b1": feats(i["b1"]),
        "b2": feats(i["b2"]), "gdn_g": feats(i["gdn_norm_g"]), "na_g": twice(i["na_norm_g"]),
        "conv_w": taps(i["conv_w"][0]), "a_log": rows(i["a_log"]), "dt_bias": rows(i["dt_bias"]),
        "mix_g_2": feats(i["norm_mix_g_2"]), "q_g": twice(i["q_norm_g_2"]), "k_g": twice(i["k_norm_g_2"]),
        "conv_w_2": taps(i["conv_w_2"][0]), "conv_b_2": feats(i["conv_b_2"]), "cln_g": feats(i["conv_ln_g_2"]),
        "cln_b": feats(i["conv_ln_b_2"]), "attn_g": feats(i["attn_out_g_2"]), "cout_g": feats(i["conv_out_g_2"]),
        "mlp_g_2": feats(i["norm_mlp_g_2"]), "sinks": rows(i["sinks_2"]), "mix_g_3": feats(i["norm_mix_w_3"]),
        "b_gate": feats(i["b_gate_3"]), "gla_g": feats(i["gla_norm_w_3"]), "conv_w_3": taps(i["conv_w_3"][0]),
        "mlp_g_3": feats(i["norm_mlp_w_3"]), "final_g": feats(i["norm_final_w_3"]),
        "eps5": full(1e-5), "eps6": full(1e-6), "zero": full(0.0), "one": full(1.0),
    }
    arrays = {
        "x": np.asarray(i["x"])[0].T.reshape(DC, P, T).transpose(1, 0, 2),
        "meta": np.asarray(i["meta_tokens_3"]).T.reshape(DC, P, META).transpose(1, 0, 2),
        "params": np.concatenate([by_name[name] for name in PARAMS], 1),
        "consts": lay_consts(), "gdn_consts": lay_gdn_consts(), "na_mask": lay_na_mask(),
        "w_in1": units(i["w_in"][0]), "w_out1": units(i["w_out"][0]), "w_mlp1": mlp_units(i["w1"][0], i["w2"][0]),
        "w_in2": units(i["w_in_2"][0]), "w_out2": units(i["w_out_2"][0]),
        "w_mlp2": mlp_units(i["w_mlp_up_2"][0], i["w_mlp_down_2"][0]),
        "w_in3": units(third(i["w_in_3"][0])), "w_out3": units(i["w_out_3"][0]),
        "w_mlp3": mlp_units(i["w_up_3"][0], i["w_down_3"][0]),
        "rpb": np.pad(np.asarray(i["rpb"])[0], ((0, 0), (0, 0), (48, 48))).reshape(NH1, -1),
        "rel_bias": i["rel_bias_2"], "t5": lay_t5(), "swa_mask": lay_swa_mask(), "w_gate": np.asarray(i["w_gate_up_3"])[0], "gla_consts": lay_gla_consts(),
    }
    nc = bacc.Bacc("TRN2", target_bir_lowering=False, num_devices=1)
    feed, drams = {}, {}
    for name, a in arrays.items():
        a = np.ascontiguousarray(a)
        feed["in_" + name] = a
        drams[name] = nc.dram_tensor("in_" + name, a.shape, mybir.dt.from_np(a.dtype), kind="ExternalInput").ap()
    for name, shape in {"h1": [padded(COLS1), T], "conv1": [3 * GH * P, T], "h2": [padded(COLS2), T], "h3": [padded(COLS3), TM], 
                        "rpb_rows": [NH1, GRID, (2 * KR - 1) * (2 * KC - 1 + 96)],
                        "t5_rows": [8, P, 384]}.items():
        drams[name] = nc.dram_tensor(name, shape, F32, kind="Internal").ap()
    drams["out"] = nc.dram_tensor("out", [DC, P, T], F32, kind="ExternalOutput").ap()
    build_program(nc, drams)
    r = run_bass_kernel_spmd(nc, [feed], core_ids=[0])
    return r.results[0]["out"].reshape(1, D, T).transpose(0, 2, 1)
```
